# Optimizing a Trainium2 kernel written in Bass

```python
import jax, jax.numpy as jnp
from jax import lax
import numpy as np

D_MODEL = 1024
BATCH = 1
SEQ = 256
DEPTH = 2

CHUNK = 128
A_HEADS = 4
A_WIDTH = D_MODEL // 2
A_HEAD_DIM = A_WIDTH // A_HEADS
B_WIDTH = D_MODEL // 2
B_GROUPS = 4
CONV_B_WIDTH = 31
CONV_B_PAD = CONV_B_WIDTH // 2
EVEN_IN = 2 * A_WIDTH + 2 * B_WIDTH
EVEN_MIX = A_WIDTH + B_WIDTH
C_WIDTH = D_MODEL
CONV_C_WIDTH = 3
CONV_C_PAD = CONV_C_WIDTH // 2
D_FF = 2816
N_EXPERTS = 8
TOP_K = 2
RMS_EPS = 1e-6
LN_EPS = 1e-5

kernel_name = "hybrid_gmlp_conformer_shortconv_moe_encoder"

def rmsnorm(x, g):
    xf = x.astype(jnp.float32)
    y = xf * lax.rsqrt(jnp.mean(xf * xf, axis=-1, keepdims=True) + RMS_EPS)
    return (y * g.astype(jnp.float32)).astype(x.dtype)

def layernorm(x, g, b):
    xf = x.astype(jnp.float32)
    mu = jnp.mean(xf, axis=-1, keepdims=True)
    xc = xf - mu
    y = xc * lax.rsqrt(jnp.mean(xc * xc, axis=-1, keepdims=True) + LN_EPS)
    return (y * g.astype(jnp.float32) + b.astype(jnp.float32)).astype(x.dtype)

def depthwise_conv(x, w, pad):
    c = x.shape[-1]
    return lax.conv_general_dilated(
        x, w[:, None, :].astype(x.dtype), window_strides=(1,), padding=[(pad, pad)],
        dimension_numbers=("NWC", "WIO", "NWC"), feature_group_count=c)

def swiglu(x, w1, w3, w2):
    return (jax.nn.silu(x @ w1) * (x @ w3)) @ w2

def mixer_ab(h, w_in, ws, bs, ln_a_g, ln_a_b, conv_w, conv_b, ln_b_g, ln_b_b, w_out):
    bsz, s, _ = h.shape
    z = h @ w_in
    a_z, b_a, b_g = z[..., :2 * A_WIDTH], z[..., 2 * A_WIDTH:2 * A_WIDTH + B_WIDTH], z[..., 2 * A_WIDTH + B_WIDTH:]
    a_z = jax.nn.gelu(a_z)
    a_u, a_v = a_z[..., :A_WIDTH], a_z[..., A_WIDTH:]
    a_v = layernorm(a_v, ln_a_g, ln_a_b)
    v = a_v.reshape(bsz, s // CHUNK, CHUNK, A_HEADS, A_HEAD_DIM)
    v = jnp.einsum("hts,bcshd->bcthd", ws, v) + bs.T[None, None, :, :, None]
    a_out = a_u * v.reshape(bsz, s, A_WIDTH)
    glu = b_a * jax.nn.sigmoid(b_g)
    c = depthwise_conv(glu, conv_w, CONV_B_PAD) + conv_b
    b_out = jax.nn.silu(layernorm(c, ln_b_g, ln_b_b))
    return jnp.concatenate([a_out, b_out], axis=-1) @ w_out

def mixer_c(h, w_in, conv_w, w_out):
    z = h @ w_in
    gate_b, gate_c, v = z[..., :C_WIDTH], z[..., C_WIDTH:2 * C_WIDTH], z[..., 2 * C_WIDTH:]
    y = gate_b * depthwise_conv(gate_c * v, conv_w, CONV_C_PAD)
    return y @ w_out

def moe_swiglu(h, router, w1, w3, w2):
    bsz, s, d = h.shape
    xf = h.reshape(bsz * s, d)
    logits = (xf @ router).astype(jnp.float32)
    top_v, top_i = lax.top_k(logits, TOP_K)
    gate = jax.nn.softmax(top_v, axis=-1)
    combine = jnp.einsum("nk,nke->ne", gate,
                         jax.nn.one_hot(top_i, N_EXPERTS, dtype=jnp.float32)).astype(h.dtype)
    out = jnp.zeros_like(xf)
    for e in range(N_EXPERTS):
        out = out + combine[:, e:e + 1] * swiglu(xf, w1[e], w3[e], w2[e])
    return out.reshape(bsz, s, d)

def setup_inputs(seed: int = 0) -> dict:
    key = jax.random.key(seed)
    ks = iter(jax.random.split(key, 32))
    n_even = (DEPTH + 1) // 2
    n_odd = DEPTH // 2
    f32 = jnp.float32

    def nrm(shape, scale):
        return jax.random.normal(next(ks), shape, f32) * scale

    def gain(shape):
        return 1.0 + 0.02 * jax.random.normal(next(ks), shape, f32)

    D = D_MODEL
    return {
        "x": jax.random.normal(next(ks), (BATCH, SEQ, D), f32),
        "norm_mix_g": gain((DEPTH, D)),
        "norm_ffn_g": gain((DEPTH, D)),
        "ev_w_in": nrm((n_even, D, EVEN_IN), D ** -0.5),
        "ev_ws": nrm((n_even, A_HEADS, CHUNK, CHUNK), CHUNK ** -0.5),
        "ev_bs": gain((n_even, A_HEADS, CHUNK)),
        "ev_ln_a_g": gain((n_even, A_WIDTH)),
        "ev_ln_a_b": nrm((n_even, A_WIDTH), 0.02),
        "ev_conv_w": nrm((n_even, CONV_B_WIDTH, B_WIDTH), CONV_B_WIDTH ** -0.5),
        "ev_conv_b": nrm((n_even, B_WIDTH), 0.02),
        "ev_ln_b_g": gain((n_even, B_WIDTH)),
        "ev_ln_b_b": nrm((n_even, B_WIDTH), 0.02),
        "ev_w_out": nrm((n_even, EVEN_MIX, D), EVEN_MIX ** -0.5),
        "od_w_in": nrm((n_odd, D, 3 * C_WIDTH), D ** -0.5),
        "od_conv_w": nrm((n_odd, CONV_C_WIDTH, C_WIDTH), CONV_C_WIDTH ** -0.5),
        "od_w_out": nrm((n_odd, C_WIDTH, D), C_WIDTH ** -0.5),
        "ffn_w1": nrm((n_even, D, D_FF), D ** -0.5),
        "ffn_w3": nrm((n_even, D, D_FF), D ** -0.5),
        "ffn_w2": nrm((n_even, D_FF, D), D_FF ** -0.5),
        "moe_router": nrm((n_odd, D, N_EXPERTS), D ** -0.5),
        "moe_w1": nrm((n_odd, N_EXPERTS, D, D_FF), D ** -0.5),
        "moe_w3": nrm((n_odd, N_EXPERTS, D, D_FF), D ** -0.5),
        "moe_w2": nrm((n_odd, N_EXPERTS, D_FF, D), D_FF ** -0.5),
        "final_g": gain((D,)),
    }

def reference(x, norm_mix_g, norm_ffn_g, ev_w_in, ev_ws, ev_bs, ev_ln_a_g, ev_ln_a_b,
              ev_conv_w, ev_conv_b, ev_ln_b_g, ev_ln_b_b, ev_w_out,
              od_w_in, od_conv_w, od_w_out, ffn_w1, ffn_w3, ffn_w2,
              moe_router, moe_w1, moe_w3, moe_w2, final_g):
    for layer in range(DEPTH):
        i = layer // 2
        hn = rmsnorm(x, norm_mix_g[layer])
        if layer % 2 == 0:
            x = x + mixer_ab(hn, ev_w_in[i], ev_ws[i], ev_bs[i], ev_ln_a_g[i], ev_ln_a_b[i],
                             ev_conv_w[i], ev_conv_b[i], ev_ln_b_g[i], ev_ln_b_b[i], ev_w_out[i])
            hn = rmsnorm(x, norm_ffn_g[layer])
            x = x + swiglu(hn, ffn_w1[i], ffn_w3[i], ffn_w2[i])
        else:
            x = x + mixer_c(hn, od_w_in[i], od_conv_w[i], od_w_out[i])
            hn = rmsnorm(x, norm_ffn_g[layer])
            x = x + moe_swiglu(hn, moe_router[i], moe_w1[i], moe_w3[i], moe_w2[i])
    return rmsnorm(x, final_g)


_drawn_inputs = setup_inputs


def setup_inputs(seed=0):
    import zlib

    import numpy as np

    out = dict(_drawn_inputs(seed))
    spreads = {}
    factors = {'ev_bs': 2.834,
     'ev_ln_a_g': 2.769,
     'ev_ln_a_b': 2.87,
     'final_g': 8.443,
     'norm_ffn_g': 3.074,
     'ev_ln_b_g': 5.252,
     'ev_ln_b_b': 8.0}
    for name, (base, spread) in spreads.items():
        noise = np.random.default_rng([zlib.crc32(name.encode()), seed]).standard_normal(out[name].shape)
        drawn = base * np.exp(spread * noise) if base else spread * noise
        out[name] = __import__('jax').numpy.asarray(drawn.astype(out[name].dtype))
    for name, factor in factors.items():
        out[name] = (out[name] * factor).astype(out[name].dtype)
    return out
```

```python
from contextlib import ExitStack

import concourse.bass as bass
from concourse import mybir

ALU = mybir.AluOpType
ACT = mybir.ActivationFunctionType
AX = mybir.AxisListType
F32 = mybir.dt.float32
F32R = mybir.dt.float32r
BF16 = mybir.dt.bfloat16
I32 = mybir.dt.int32

P = 128
D = 1024
SEQ = 256
BLK = SEQ // P
KD = D // P
AW = 512
HEADS = AW // P
TAPS = 31
PAD = TAPS // 2
FF = 2816
NE = 8
RMS_EPS = 1e-6
LN_EPS = 1e-5

SLAB = 2048
RAW = 11
SPLIT = 3
CH = 512
CHUNKS = [CH] * (FF // CH) + [FF % CH]
NCH = len(CHUNKS)
MAX_OVER = (2 * SEQ) // (P + 1)
MAX_JOBS = NE + MAX_OVER


def swiglu_slabs():
    out = []
    for c in range(NCH + 1):
        if c < NCH:
            parts = [0, 1] if CHUNKS[c] == CH else [None]
            out += [(k, c, h) for h in parts for k in ("w1", "w3")]
        if c > 0:
            parts = [0, 1] if CHUNKS[c - 1] == CH else [0]
            out += [("w2", c - 1, h) for h in parts]
    return out


SW = swiglu_slabs()
PER = len(SW)
LAST_H = [max(i for i, s in enumerate(SW) if s[0] != "w2" and s[1] == c) for c in range(NCH)]
FIRST_Y = [min(i for i, s in enumerate(SW) if s[0] == "w2" and s[1] == c) for c in range(NCH)]
LAST_Y = [max(i for i, s in enumerate(SW) if s[0] == "w2" and s[1] == c) for c in range(NCH)]

S_IN = 0
S_OUT = S_IN + D * 4 * AW // (P * SLAB)
S_FFN = S_OUT + 2 * AW * D // (P * SLAB)
S_CIN = S_FFN + PER
S_COUT = S_CIN + D * 3 * D // (P * SLAB)
S_MOE = S_COUT + D * D // (P * SLAB)
assert PER % RAW == 0 and PER % SPLIT == 0


T_AT = [LAST_H[c] + (3 if c else 1) for c in range(NCH - 1)] + [FIRST_Y[NCH - 2]]
SC_AT = [3, 5, 6, 7]
PT_AT = 8
G_AT = [13, 19]
GT_AT = 29
RT_DIFF, RT_SEL = 1, 2
N_ROW_DMAS = 9
ROOTS = 5 * BLK + 2 * BLK


def trunk(nc, x, norm_mix_g, norm_ffn_g, ev_w_in, ev_ws, ev_bs, ev_ln_a_g, ev_ln_a_b, ev_conv_w,
          ev_conv_b, ev_ln_b_g, ev_ln_b_b, ev_w_out, od_w_in, od_conv_w, od_w_out, ffn_w1, ffn_w3,
          ffn_w2, moe_router, moe_w1, moe_w3, moe_w2, final_g, out):
    ctx = ExitStack()
    with ctx:
        def sb(name, shape, dt=F32):
            return ctx.enter_context(nc.sbuf_tensor(name, shape, dt))

        def sem(name):
            return ctx.enter_context(nc.semaphore(name))

        raw = sb("raw", [P, RAW, SLAB])
        hi = sb("hi", [P, SPLIT, SLAB], F32R)
        lo = sb("lo", [P, SPLIT, SLAB], F32R)
        xres = sb("xres", [P, BLK, D])
        actT_h = sb("actT_h", [P, KD * SEQ], F32R)
        actT_l = sb("actT_l", [P, KD * SEQ], F32R)
        tokA = sb("tokA", [P, BLK, D])
        tokB = sb("tokB", [P, 2 * D])
        with nc.sbuf_tensor("scratch", [P, 6144], F32) as scratch:
            pass
        mlp_h = sb("mlp_h", [P, 3072], F32R)
        mlp_l = sb("mlp_l", [P, 3072], F32R)
        ident = sb("ident", [P, P])
        iota_s = sb("iota_s", [P, P])
        onehot = sb("onehot", [P, BLK, P], F32R)
        onehotT = sb("onehotT", [P, SEQ], F32R)
        tri = sb("tri", [P, P], BF16)
        ones = sb("ones", [P, P], BF16)
        prm = sb("prm", [P, 196])
        rw = sb("rw", [P, KD, NE])
        rw_hl = sb("rw_hl", [P, KD, 2 * NE], F32R)
        ss = sb("ss", [P, 5, BLK])
        mean2 = sb("mean2", [P, ROOTS])
        root = sb("root", [P, ROOTS])
        power = sb("power", [P, 1])
        bst = sb("bst", [P, 4, 6])
        mv = sb("mv", [P, 4, 2])
        rt = sb("rt", [P, 12, BLK, NE])
        rs = sb("rs", [P, 10, BLK])
        sel_bf = sb("sel_bf", [P, BLK, NE], BF16)
        iota_e = sb("iota_e", [P, BLK, NE])
        iota_id = sb("iota_id", [P, NE])
        posj = sb("posj", [P, BLK, MAX_JOBS + 1])
        gatej = sb("gatej", [P, BLK, MAX_JOBS + 1])
        gate_hl = sb("gate_hl", [P, BLK, MAX_JOBS + 1, 2], F32R)
        ov = sb("ov", [P, 6, NE])
        ovs = sb("ovs", [P, 8])
        job_i = sb("job_i", [P, 1 + MAX_OVER], I32)
        gslot = sb("gslot", [P, 1])

        PB = [ctx.enter_context(nc.psum_tensor(f"PB{i}", [P, 512], F32)) for i in range(8)]

        raw_loaded = [sem(f"raw_loaded{i}") for i in range(RAW)]
        hi_done = sem("hi_done")
        lo_done = sem("lo_done")
        slab_used = sem("slab_used")
        x_loaded = sem("x_loaded")
        rows_loaded = sem("rows_loaded")
        bcast_loaded = sem("bcast_loaded")
        router_loaded = sem("router_loaded")
        consts_step = sem("consts_step")
        setup_T = sem("setup_T")
        prm_done = sem("prm_done")
        x_updated = sem("x_updated")
        sq_done = sem("sq_done")
        xn_done = sem("xn_done")
        xn_T = sem("xn_T")
        hn_hi = sem("hn_hi")
        hn_lo = sem("hn_lo")
        dve_step = sem("dve_step")
        mean2_done = sem("mean2_done")
        root_done = sem("root_done")
        sig_done = sem("sig_done")
        glu_done = sem("glu_done")
        glu_T = sem("glu_T")
        gluT_done = sem("gluT_done")
        conv_step = sem("conv_step")
        v_done = sem("v_done")
        vn_done = sem("vn_done")
        gated = sem("gated")
        u_done = sem("u_done")
        aout_done = sem("aout_done")
        aout_T = sem("aout_T")
        c_T = sem("c_T")
        cn_done = sem("cn_done")
        cn_T = sem("cn_T")
        cs_done = sem("cs_done")
        gc_done = sem("gc_done")
        t_done = sem("t_done")
        t_T = sem("t_T")
        tT_done = sem("tT_done")
        gb_done = sem("gb_done")
        gb_T = sem("gb_T")
        y_done = sem("y_done")
        silu_done = sem("silu_done")
        hid_done = sem("hid_done")
        hid_T = sem("hid_T")
        hidT_hi = sem("hidT_hi")
        hidT_lo = sem("hidT_lo")
        logits_done = sem("logits_done")
        exp_done = sem("exp_done")
        rt_step = sem("rt_step")
        counts_done = sem("counts_done")
        rw_hi = sem("rw_hi")
        rw_lo = sem("rw_lo")
        tok_hi = sem("tok_hi")
        tok_lo = sem("tok_lo")
        routed = sem("routed")
        place_done = sem("place_done")
        picked = sem("picked")
        picked_sb = sem("picked_sb")
        pick_T = sem("pick_T")
        pickT_hi = sem("pickT_hi")
        pickT_lo = sem("pickT_lo")
        place_T = sem("place_T")
        placeT_done = sem("placeT_done")
        gslot_done = sem("gslot_done")
        ysc_hi = sem("ysc_hi")
        ysc_lo = sem("ysc_lo")
        scat = sem("scat")
        out_ready = sem("out_ready")
        out_sem = sem("out_sem")

        def slab_source(w1, w3, w2, kind, c, part):
            if kind == "w2":
                r0 = c * CH + part * 2 * P
                return w2[r0:r0 + 2 * P, :].rearrange("(k p) n -> p k n", p=P)
            w = w1 if kind == "w1" else w3
            n0 = c * CH
            if part is None:
                return w[:, n0:n0 + CHUNKS[c]].rearrange("(k p) n -> p k n", p=P)
            return w[part * 4 * P:(part + 1) * 4 * P, n0:n0 + CH].rearrange("(k p) n -> p k n", p=P)

        def in_source(w, col, part):
            return w[part * 4 * P:(part + 1) * 4 * P, col:col + 512].rearrange("(k p) n -> p k n", p=P)

        def out_source(w, i):
            return w[i * 2 * P:(i + 1) * 2 * P, :].rearrange("(k p) n -> p k n", p=P)

        sources = []
        for col in (2 * AW, 3 * AW, AW, 0):
            sources += [in_source(ev_w_in[0], col, h) for h in range(2)]
        sources += [out_source(ev_w_out[0], i) for i in range(4)]
        sources += [slab_source(ffn_w1[0], ffn_w3[0], ffn_w2[0], *s) for s in SW]
        for col in (D, 2 * D, D + 512, 2 * D + 512, 0, 512):
            sources += [in_source(od_w_in[0], col, h) for h in range(2)]
        sources += [out_source(od_w_out[0], i) for i in range(4)]
        assert len(sources) == S_MOE

        def raw_as(slot, like):
            k = like.shape[1]
            return raw[:, slot, :].rearrange("p (k n) -> p k n", k=k)

        C_CONV, C_BS = 0, TAPS * HEADS
        C_MIX = C_BS + HEADS
        C_FFN = C_MIX + 2 * KD
        C_CB = C_FFN + 2 * KD
        C_LG = C_CB + HEADS
        C_LB = C_LG + HEADS
        C_OD = C_LB + HEADS
        N_ROWS2 = C_OD + 3 * KD - P
        GAIN = [C_MIX, C_FFN, C_MIX + KD, C_FFN + KD]

        lna = tokB[:, 0:2 * AW].rearrange("p (a n) -> p a n", a=2)
        ws_rows = tokB[:, 1024:1536].rearrange("p (h s) -> p h s", h=HEADS)
        prm_rows = tokB[:, 1536:1792].rearrange("p (a n) -> p a n", a=2)
        glu = scratch[:, 0:1024].rearrange("p (b n) -> p b n", b=BLK)
        GP = SEQ + 2 * PAD
        gluT = scratch[:, 1024:1024 + HEADS * GP].rearrange("p (c t) -> p c t", c=HEADS)
        o = 1024 + HEADS * GP
        conv = scratch[:, o:o + 1024].rearrange("p (c t) -> p c t", c=HEADS)
        va = scratch[:, o + 1024:o + 2048].rearrange("p (b n) -> p b n", b=BLK)
        ua = scratch[:, o + 2048:o + 3072].rearrange("p (b n) -> p b n", b=BLK)
        wsT = scratch[:, o + 3072:o + 3584].rearrange("p (h t) -> p h t", h=HEADS)
        cn = tokA[:, 0, :].rearrange("p (b n) -> p b n", b=BLK)
        cs = glu.rearrange("p b n -> p (b n)").rearrange("p (c t) -> p c t", c=HEADS)
        gcv = scratch[:, 0:1024].rearrange("p (b n) -> p b n", b=BLK)
        tt = scratch[:, 1024:2048].rearrange("p (b n) -> p b n", b=BLK)
        TP = SEQ + 2
        tT = [scratch[:, 2048 + h * 4 * TP:2048 + (h + 1) * 4 * TP].rearrange("p (c t) -> p c t", c=4)
              for h in range(2)]
        gbs = scratch[:, 4112:5136].rearrange("p (b n) -> p b n", b=BLK)
        yT = tokA[:, :, :].rearrange("p b n -> p (b n)").rearrange("p (k t) -> p k t", k=KD)
        hid = tokA

        def hidT(t, c, w):
            o = (c % 2) * 4 * w
            return t[:, o:o + 4 * w]

        tokn_h = mlp_h[:, 1024:3072].rearrange("p (b n) -> p b n", b=BLK)
        tokn_l = mlp_l[:, 1024:3072].rearrange("p (b n) -> p b n", b=BLK)
        pick = tokB[:, 0:D]
        pickT_h, pickT_l = actT_h[:, 0:D], actT_l[:, 0:D]
        ysc_h, ysc_l = actT_h[:, D:2 * D], actT_l[:, D:2 * D]

        X_MIX, X_FFN, X_C = 4, 8, 12

        block = ctx.enter_context(nc.Block())

        @block.sync
        def _(sp):
            sp.dma_start(xres[:, :, :], x[0].rearrange("(b p) d -> p b d", p=P)).then_inc(x_loaded, 16)
            for i, src in enumerate(sources):
                if i >= RAW:
                    sp.wait_ge(lo_done, i - RAW + 1)
                sp.dma_start(raw_as(i % RAW, src), src).then_inc(raw_loaded[i % RAW], 16)

            def expert_slabs(job, e):
                w1, w3, w2 = (w[0, bass.ds(e, 1)].rearrange("a r n -> (a r) n")
                              for w in (moe_w1, moe_w3, moe_w2))
                for m, s in enumerate(SW):
                    i = S_MOE + m
                    src = slab_source(w1, w3, w2, *s)
                    sp.wait_ge(lo_done, job * PER + (i - RAW + 1))
                    sp.dma_start(raw_as(i % RAW, src), src).then_inc(raw_loaded[i % RAW], 16)

            with sp.Fori(0, NE) as j:
                expert_slabs(j, j)
            sp.wait_ge(routed, 1)
            n_over = sp.value_load(job_i[0:1, 0:1], min_val=0, max_val=MAX_OVER)
            with sp.If(n_over > 0):
                with sp.Fori(0, n_over) as i:
                    e = sp.value_load(job_i[0:1, bass.ds(1 + i, 1)], min_val=0, max_val=NE - 1)
                    expert_slabs(i + NE, e)

            sp.wait_ge(out_ready, BLK)
            sp.dma_start(out[0].rearrange("(b p) d -> p b d", p=P), tokA[:, :, :]).then_inc(out_sem, 16)
            sp.wait_ge(out_sem, 16)

        @block.gpsimd
        def _(pool):
            n = [0]

            def step(ins):
                n[0] += 1
                ins.then_inc(consts_step, 1)

            step(nc.gpsimd.memset(ident[:, :], 0.0))
            pool.wait_ge(consts_step, 1)
            step(nc.gpsimd.affine_select(out=ident[:, :], in_=ident[:, :], compare_op=ALU.not_equal,
                                         fill=1.0, base=0, pattern=[[-1, P]], channel_multiplier=1))
            step(nc.gpsimd.memset(gluT[:, :, :], 0.0))
            step(nc.gpsimd.iota(iota_s[:, :], [[1, P]], base=0, channel_multiplier=0,
                                allow_small_or_imprecise_dtypes=True))
            step(nc.gpsimd.iota(iota_e[:, :, :], [[0, BLK], [-1, NE]], base=NE, channel_multiplier=0,
                                allow_small_or_imprecise_dtypes=True))
            step(nc.gpsimd.iota(iota_id[:, :], [[1, NE]], base=0, channel_multiplier=0,
                                allow_small_or_imprecise_dtypes=True))
            step(nc.gpsimd.memset(ones[:, :], 1.0))
            pool.wait_ge(consts_step, 7)
            step(nc.gpsimd.affine_select(out=tri[:, :], in_=ones[:, :], compare_op=ALU.is_gt,
                                         fill=0.0, base=0, pattern=[[1, P]], channel_multiplier=-1))
            step(nc.gpsimd.memset(posj[:, :, :], -1.0))
            step(nc.gpsimd.memset(gatej[:, :, :], 0.0))
            step(nc.gpsimd.memset(gslot[:, :], 0.0))
            step(nc.gpsimd.memset(onehotT[:, :].bitcast(F32), 0.0))

            step(nc.gpsimd.memset(power[:, :], -0.5))
            pool.wait_ge(consts_step, 13)
            for r in range(ROOTS):
                pool.wait_ge(mean2_done, r + 1)
                nc.gpsimd.tensor_tensor(root[:, r:r + 1], mean2[:, r:r + 1], power[:, :], ALU.pow).then_inc(root_done, 1)

        CONSTS = 12

        @block.tensor
        def _(pe):
            def product(i, outs, stat, n, k_of, cols, first, last, idx=None):
                h = hi[:, i % SPLIT, :].rearrange("p (k n) -> p k n", n=n)
                l = lo[:, i % SPLIT, :].rearrange("p (k n) -> p k n", n=n)
                pe.wait_ge(lo_done, i + 1 if idx is None else idx + 1)
                mm = None
                for kk, k in enumerate(k_of):
                    for b in range(len(outs)):
                        for q, ps in enumerate(outs[b]):
                            s = slice(q * cols, (q + 1) * cols)
                            st, en = first and kk == 0, last and kk == len(k_of) - 1
                            nc.tensor.matmul(ps, stat(0, k, b), h[:, kk, s], start=st, stop=False)
                            nc.tensor.matmul(ps, stat(0, k, b), l[:, kk, s], start=False, stop=False)
                            mm = nc.tensor.matmul(ps, stat(1, k, b), h[:, kk, s], start=False, stop=en)
                mm.then_inc(slab_used, 1)

            def act_tile(part, k, b):
                t = (actT_h, actT_l)[part]
                return t[:, k * SEQ + b * P:k * SEQ + (b + 1) * P]

            def pick_tile(part, k, b):
                return (pickT_h, pickT_l)[part][:, k * P:(k + 1) * P]

            def norm_T(n):
                for b in range(BLK):
                    pe.wait_ge(xn_done, BLK * n + b + 1)
                    for k in range(KD):
                        o = (k % 2) * SEQ + b * P
                        t = nc.tensor.transpose(PB[k // 2][:, o:o + P], tokA[:, b, k * P:(k + 1) * P], ident[:, :])
                    t.then_inc(xn_T, 1)

            def in_group(i, banks):
                for h in range(2):
                    product(i + h, [[PB[b][:, :]] for b in banks], act_tile, 512,
                            range(4 * h, 4 * h + 4), 512, h == 0, h == 1)

            pe.wait_ge(consts_step, 2)
            pe.wait_ge(rows_loaded, 16 * N_ROW_DMAS)
            nc.tensor.transpose(PB[0][:, 0:P], prm_rows[:, 0, :], ident[:, :])
            nc.tensor.transpose(PB[0][:, P:P + N_ROWS2], prm_rows[0:N_ROWS2, 1, :], ident[0:N_ROWS2, 0:N_ROWS2])
            for h in range(HEADS):
                t = nc.tensor.transpose(PB[4][:, h * P:(h + 1) * P], ws_rows[:, h, :], ident[:, :])
            t.then_inc(setup_T, 1)
            pe.wait_ge(prm_done, 1)
            norm_T(0)

            pe.wait_ge(hn_lo, KD)
            pe.wait_ge(prm_done, 2)
            in_group(S_IN, (4, 5))
            in_group(S_IN + 2, (6, 7))
            product(S_IN + 4, [[PB[2][:, :]], [PB[3][:, :]]], act_tile, 512, range(4), 512, True, False)
            pe.wait_ge(glu_done, BLK)
            for b in range(BLK):
                for c in range(HEADS):
                    o = (c % 2) * SEQ + b * P
                    t = nc.tensor.transpose(PB[c // 2][:, o:o + P], glu[:, b, c * P:(c + 1) * P], ident[:, :])
            t.then_inc(glu_T, 1)
            product(S_IN + 5, [[PB[2][:, :]], [PB[3][:, :]]], act_tile, 512, range(4, 8), 512, False, True)
            in_group(S_IN + 6, (4, 5))
            pe.wait_ge(vn_done, BLK)
            for b in range(BLK):
                for h in range(HEADS):
                    t = nc.tensor.matmul(PB[6 + b][:, h * P:(h + 1) * P], wsT[:, h, :], va[:, b, h * P:(h + 1) * P],
                                         start=True, stop=True)
                t.then_inc(gated, 1)
            pe.wait_ge(gluT_done, 1)
            pe.wait_ge(aout_done, BLK)
            for b in range(BLK):
                for c in range(HEADS):
                    o = (c % 2) * SEQ + b * P
                    t = nc.tensor.transpose(PB[c // 2][:, o:o + P], ua[:, b, c * P:(c + 1) * P], ident[:, :])
            t.then_inc(aout_T, 1)

            out_banks = [[PB[4 + 2 * b][:, :], PB[5 + 2 * b][:, :]] for b in range(BLK)]
            pe.wait_ge(hn_lo, KD + 4)
            for i in range(2):
                product(S_OUT + i, out_banks, act_tile, D, range(2 * i, 2 * i + 2), 512, i == 0, False)
            pe.wait_ge(conv_step, HEADS * TAPS)
            for b in range(BLK):
                for c in range(HEADS):
                    t = nc.tensor.transpose(PB[b][:, c * P:(c + 1) * P], conv[:, c, b * P:(b + 1) * P], ident[:, :])
                t.then_inc(c_T, 1)
            pe.wait_ge(cn_done, BLK)
            for b in range(BLK):
                for c in range(HEADS):
                    o = (c % 2) * SEQ + b * P
                    t = nc.tensor.transpose(PB[2 + c // 2][:, o:o + P], cn[:, b, c * P:(c + 1) * P], ident[:, :])
            t.then_inc(cn_T, 1)
            pe.wait_ge(hn_lo, KD + 8)
            for i in range(2, 4):
                product(S_OUT + i, out_banks, act_tile, D, range(2 * i, 2 * i + 2), 512, False, i == 3)

            def hid_transposes(c, b, bank, w, count):
                pe.wait_ge(hid_done, count)
                for kk in range(CHUNKS[c] // P):
                    t = nc.tensor.transpose(bank[:, kk * P:(kk + 1) * P], hid[:, b, (c % 2) * 512 + kk * P:
                                                                            (c % 2) * 512 + (kk + 1) * P], ident[:, :])
                t.then_inc(hid_T, 1)

            norm_T(1)
            pe.wait_ge(hn_lo, 2 * KD + 8)
            for m, (kind, c, part) in enumerate(SW):
                i = S_FFN + m
                if kind == "w2":
                    if m == FIRST_Y[c]:
                        pe.wait_ge(hidT_lo, BLK * (c + 1))

                    def stat(p, k, b, c=c):
                        t = hidT((mlp_h, mlp_l)[p], c, SEQ)
                        return t[:, (b * 4 + k) * P:(b * 4 + k + 1) * P]
                    product(i, out_banks, stat, D, range(2 * part, 2 * part + 2), 512,
                            m == FIRST_Y[0], m == PER - 1)
                else:
                    if c > 0 and part in (0, None) and kind == "w1":
                        pe.wait_ge(hidT_lo, BLK * c)
                    n = CHUNKS[c]
                    w = 0 if kind == "w1" else 2
                    ks = range(KD) if part is None else range(4 * part, 4 * part + 4)
                    product(i, [[PB[w + b][:, 0:n]] for b in range(BLK)], act_tile, n, ks, n,
                            part in (0, None), part in (1, None))
                if (c == 0 and m == LAST_H[0]) or (kind == "w2" and m == FIRST_Y[c] and c + 1 < NCH):
                    nxt = 0 if m == LAST_H[0] else c + 1
                    for b in range(BLK):
                        hid_transposes(nxt, b, PB[b], SEQ, BLK * nxt + b + 1)

            def tile_T(src, banks, signal):
                for b in range(BLK):
                    for c in range(4):
                        o = (c % 2) * SEQ + b * P
                        t = nc.tensor.transpose(PB[banks[c // 2]][:, o:o + P], src[:, b, c * P:(c + 1) * P], ident[:, :])
                t.then_inc(signal, 1)

            norm_T(2)
            pe.wait_ge(hn_lo, 3 * KD + 8)
            in_group(S_CIN, (0, 1))
            in_group(S_CIN + 2, (2, 3))
            in_group(S_CIN + 4, (4, 5))
            pe.wait_ge(t_done, BLK)
            tile_T(tt, (0, 1), t_T)
            in_group(S_CIN + 6, (6, 7))
            in_group(S_CIN + 8, (2, 3))
            pe.wait_ge(t_done, 2 * BLK)
            tile_T(tt, (4, 5), t_T)
            product(S_CIN + 10, [[PB[6][:, :]], [PB[7][:, :]]], act_tile, 512, range(4), 512, True, False)
            pe.wait_ge(tT_done, 1)
            pe.wait_ge(gb_done, BLK)
            tile_T(gbs, (0, 1), gb_T)
            product(S_CIN + 11, [[PB[6][:, :]], [PB[7][:, :]]], act_tile, 512, range(4, 8), 512, False, True)
            pe.wait_ge(gb_done, 2 * BLK)
            tile_T(gbs, (2, 3), gb_T)
            pe.wait_ge(tT_done, 2)
            for i in range(4):
                if i % 2 == 0:
                    pe.wait_ge(hn_lo, 3 * KD + 8 + 4 * (i // 2 + 1))
                product(S_COUT + i, out_banks, act_tile, D, range(2 * i, 2 * i + 2), 512, i == 0, i == 3)

            norm_T(3)
            pe.wait_ge(rw_lo, 1)
            pe.wait_ge(hn_lo, 4 * KD + 16)
            for b in range(BLK):
                for k in range(KD):
                    nc.tensor.matmul(PB[4 + b][:, 0:2 * NE], act_tile(0, k, b), rw_hl[:, k, :], start=(k == 0), stop=False)
                    t = nc.tensor.matmul(PB[4 + b][:, 0:2 * NE], act_tile(1, k, b), rw_hl[:, k, :], start=False,
                                         stop=(k == KD - 1))
            t.then_inc(logits_done, 1)
            pe.wait_ge(rt_step, RT_SEL)
            nc.tensor.matmul(PB[6][:, 0:NE], tri[:, :], sel_bf[:, 0, :], start=True, stop=True)
            nc.tensor.matmul(PB[6][:, NE:2 * NE], ones[:, :], sel_bf[:, 0, :], start=True, stop=False)
            nc.tensor.matmul(PB[6][:, NE:2 * NE], tri[:, :], sel_bf[:, 1, :], start=False, stop=True)
            nc.tensor.matmul(PB[6][:, 2 * NE:3 * NE], ones[:, :], sel_bf[:, 0, :], start=True, stop=False)
            nc.tensor.matmul(PB[6][:, 2 * NE:3 * NE], ones[:, :], sel_bf[:, 1, :], start=False,
                             stop=True).then_inc(counts_done, 1)

            MISC = PB[5]

            def gather(half):
                s = slice(half * 512, (half + 1) * 512)
                for c in range(BLK):
                    nc.tensor.matmul(MISC[:, :], onehot[:, c, :], tokn_h[:, c, s], start=(c == 0), stop=False)
                    t = nc.tensor.matmul(MISC[:, :], onehot[:, c, :], tokn_l[:, c, s], start=False, stop=(c == BLK - 1))
                t.then_inc(picked, 1)

            def gather_T(banks):
                for k in range(KD):
                    t = nc.tensor.transpose(banks[k // 4][:, (k % 4) * P:(k % 4 + 1) * P], pick[:, k * P:(k + 1) * P],
                                            ident[:, :])
                t.then_inc(pick_T, 1)

            def scatter(piece):
                b, s = piece // 2, slice((piece % 2) * 512, (piece % 2 + 1) * 512)
                st = onehotT[:, b * P:(b + 1) * P]
                nc.tensor.matmul(MISC[:, :], st, ysc_h[:, s], start=True, stop=False)
                nc.tensor.matmul(MISC[:, :], st, ysc_l[:, s], start=False, stop=True).then_inc(scat, 1)

            pe.wait_ge(place_done, 1)
            pe.wait_ge(tok_lo, 1)
            for half in range(2):
                if half:
                    pe.wait_ge(picked_sb, 1)
                gather(half)
            pe.wait_ge(picked_sb, 2)
            gather_T([PB[0], PB[1]])
            pe.wait_ge(routed, 1)
            n_over = pe.value_load(job_i[0:1, 0:1], min_val=0, max_val=MAX_OVER)
            with pe.Fori(0, n_over + NE) as j:
                pe.wait_ge(pickT_lo, j + 1)
                for m, (kind, c, part) in enumerate(SW):
                    i = S_MOE + m
                    if kind == "w2":
                        if m == FIRST_Y[c]:
                            pe.wait_ge(hidT_lo, j * NCH + (BLK * NCH + c + 1))

                        def stat(p, k, b, c=c):
                            return hidT((mlp_h, mlp_l)[p], c, P)[:, k * P:(k + 1) * P]
                        product(i, [[PB[6][:, :], PB[7][:, :]]], stat, D, range(2 * part, 2 * part + 2), 512,
                                m == FIRST_Y[0], m == PER - 1, idx=j * PER + i)
                    else:
                        n = CHUNKS[c]
                        bank = PB[2 * (c % 2) + (0 if kind == "w1" else 1)]
                        ks = range(KD) if part is None else range(4 * part, 4 * part + 4)
                        product(i, [[bank[:, 0:n]]], pick_tile, n, ks, n, part in (0, None), part in (1, None),
                                idx=j * PER + i)
                    for c in range(NCH):
                        if m == T_AT[c]:
                            pe.wait_ge(hid_done, j * NCH + (BLK * NCH + c + 1))
                            for kk in range(CHUNKS[c] // P):
                                t = nc.tensor.transpose(PB[4][:, kk * P:(kk + 1) * P],
                                                        hid[:, 0, (c % 2) * 512 + kk * P:(c % 2) * 512 + (kk + 1) * P],
                                                        ident[:, :])
                            t.then_inc(hid_T, 1)
                    if m in SC_AT:
                        piece = SC_AT.index(m)
                        if piece == 0:
                            pe.wait_ge(ysc_lo, j + 1)
                        else:
                            pe.wait_ge(x_updated, j * 4 + (X_C + piece))
                        scatter(piece)
                    if m == PT_AT:
                        pe.wait_ge(x_updated, j * 4 + (X_C + 4))
                        for b in range(BLK):
                            nc.tensor.transpose(MISC[:, b * P:(b + 1) * P], onehot[:, b, :].bitcast(F32), ident[:, :])
                        for b in range(BLK):
                            t = nc.tensor.matmul(MISC[:, SEQ:SEQ + 2], onehot[:, b, :],
                                                 gate_hl[:, b, bass.ds(j, 1), :].rearrange("p a t -> p (a t)"),
                                                 start=(b == 0), stop=(b == BLK - 1))
                        t.then_inc(place_T, 1)
                    if m in G_AT:
                        half = G_AT.index(m)
                        if half == 0:
                            pe.wait_ge(placeT_done, j + 1)
                            pe.wait_ge(gslot_done, j + 1)
                            pe.wait_ge(place_done, j + 2)
                        else:
                            pe.wait_ge(picked_sb, j * 2 + 3)
                        gather(half)
                    if m == GT_AT:
                        pe.wait_ge(picked_sb, j * 2 + 4)
                        gather_T([PB[0], PB[1]])
            jobs = n_over + NE
            pe.wait_ge(ysc_lo, jobs + 1)
            for piece in range(4):
                if piece:
                    pe.wait_ge(x_updated, jobs * 4 + (X_C + piece))
                scatter(piece)

        @block.scalar
        def _(act):
            act.dma_start(prm_rows[0:TAPS * HEADS, 0, :],
                          ev_conv_w[0].rearrange("t (c n) -> (t c) n", n=P)).then_inc(rows_loaded, 16)
            act.dma_start(prm_rows[TAPS * HEADS:P, 0, :], ev_bs[0]).then_inc(rows_loaded, 16)
            r = 0
            for src in (norm_mix_g.rearrange("l (k n) -> (l k) n", n=P),
                        norm_ffn_g.rearrange("l (k n) -> (l k) n", n=P),
                        ev_conv_b.rearrange("l (k n) -> (l k) n", n=P),
                        ev_ln_b_g.rearrange("l (k n) -> (l k) n", n=P),
                        ev_ln_b_b.rearrange("l (k n) -> (l k) n", n=P),
                        od_conv_w[0].rearrange("t (k n) -> (t k) n", n=P)):
                act.dma_start(prm_rows[r:r + src.shape[0], 1, :], src).then_inc(rows_loaded, 16)
                r += src.shape[0]
            act.dma_start(ws_rows, ev_ws[0].rearrange("h t s -> t h s")).then_inc(rows_loaded, 16)
            act.dma_start(lna[:, 0, :], ev_ln_a_g.partition_broadcast(P)).then_inc(bcast_loaded, 16)
            act.dma_start(lna[:, 1, :], ev_ln_a_b.partition_broadcast(P)).then_inc(bcast_loaded, 16)
            act.dma_start(rw[:, :, :], moe_router[0].rearrange("(k p) e -> p k e", p=P)).then_inc(router_loaded, 16)

            done = [0]

            def split(upto):
                while done[0] <= upto:
                    i = done[0]
                    act.wait_ge(raw_loaded[i % RAW], 16 * (i // RAW + 1))
                    if i >= SPLIT:
                        act.wait_ge(slab_used, i - SPLIT + 1)
                    nc.scalar.copy(hi[:, i % SPLIT, :], raw[:, i % RAW, :]).then_inc(hi_done, 1)
                    done[0] += 1

            def squares(n):
                for b in range(BLK):
                    if n == 0:
                        act.wait_ge(x_loaded, 16)
                    else:
                        act.wait_ge(x_updated, 4 * (n - 1) + 2 * b + 2)
                    if n or b:
                        act.wait_ge(sq_done, BLK * n + b)
                    nc.scalar.activation(tokB[:, D:2 * D] if n else scratch[:, 3072:4096], xres[:, b, :], ACT.Square,
                                         accum_out=ss[:, n, b:b + 1]).then_inc(sq_done, 1)

            def norm_hi(n):
                act.wait_ge(xn_T, BLK * (n + 1))
                for k in range(KD):
                    o = (k % 2) * SEQ
                    nc.scalar.activation(actT_h[:, k * SEQ:(k + 1) * SEQ], PB[k // 2][:, o:o + SEQ], ACT.Copy,
                                         scale=prm[:, GAIN[n] + k:GAIN[n] + k + 1]).then_inc(hn_hi, 1)

            squares(0)
            act.wait_ge(setup_T, 1)
            nc.scalar.copy(prm[:, :], PB[0][:, 0:P + N_ROWS2]).then_inc(prm_done, 1)
            norm_hi(0)
            nc.scalar.copy(wsT, PB[4][:, :].rearrange("p (h t) -> p h t", h=HEADS)).then_inc(prm_done, 1)
            act.wait_ge(router_loaded, 16)
            nc.scalar.copy(rw_hl[:, :, 0:NE], rw[:, :, :]).then_inc(rw_hi, 1)
            split(S_IN + 5)
            act.wait_ge(slab_used, S_IN + 4)
            for b in range(BLK):
                nc.scalar.activation(glu[:, b, :], PB[6 + b][:, :], ACT.Sigmoid).then_inc(sig_done, 1)
            split(S_IN + 6)
            act.wait_ge(consts_step, 3)
            act.wait_ge(glu_T, 1)
            for c in range(0, HEADS, 2):
                t = nc.scalar.copy(gluT[:, c:c + 2, PAD:PAD + SEQ],
                                   PB[c // 2][:, :].rearrange("p (c t) -> p c t", c=2))
            t.then_inc(gluT_done, 1)
            split(S_IN + 7)
            act.wait_ge(slab_used, S_IN + 6)
            for b in range(BLK):
                nc.scalar.activation(va[:, b, :], PB[2 + b][:, :], ACT.Gelu_apprx_tanh).then_inc(v_done, 1)
            split(S_OUT + 1)
            act.wait_ge(slab_used, S_IN + 8)
            for b in range(BLK):
                nc.scalar.activation(ua[:, b, :], PB[4 + b][:, :], ACT.Gelu_apprx_tanh).then_inc(u_done, 1)
            act.wait_ge(aout_T, 1)
            for c in range(0, HEADS, 2):
                nc.scalar.copy(actT_h[:, c * SEQ:(c + 2) * SEQ], PB[c // 2][:, :]).then_inc(hn_hi, 2)
            split(S_OUT + 3)
            act.wait_ge(cn_T, 1)
            for c in range(HEADS):
                o = (c % 2) * SEQ
                nc.scalar.activation(cs[:, c, :], PB[2 + c // 2][:, o:o + SEQ], ACT.Silu,
                                     bias=prm[:, C_LB + c:C_LB + c + 1],
                                     scale=prm[:, C_LG + c:C_LG + c + 1]).then_inc(cs_done, 1)
            for c in range(HEADS):
                act.wait_ge(cs_done, c + 1)
                nc.scalar.copy(actT_h[:, (4 + c) * SEQ:(5 + c) * SEQ], cs[:, c, :]).then_inc(hn_hi, 1)
            split(S_FFN + 1)

            squares(1)
            norm_hi(1)
            for c in range(NCH):
                n, q = CHUNKS[c], S_FFN + LAST_H[c]
                split(min(q + 2, S_CIN - 1))
                act.wait_ge(slab_used, q + 1)
                for b in range(BLK):
                    if c > 1:
                        act.wait_ge(hid_T, BLK * (c - 2) + b + 1)
                    nc.scalar.activation(hid[:, b, (c % 2) * 512:(c % 2) * 512 + n], PB[b][:, 0:n],
                                         ACT.Silu).then_inc(silu_done, 1)
                if c:
                    split(q + 3)
                for b in range(BLK):
                    act.wait_ge(hid_T, BLK * c + b + 1)
                    o = b * 512
                    nc.scalar.copy(hidT(mlp_h, c, SEQ)[:, o:o + n], PB[b][:, 0:n]).then_inc(hidT_hi, 1)

            split(S_CIN + 1)
            squares(2)
            norm_hi(2)
            for h in range(2):
                i = S_CIN + 4 * h
                split(i + 3)
                act.wait_ge(slab_used, i + 2)
                if h:
                    act.wait_ge(t_done, BLK)
                for b in range(BLK):
                    nc.scalar.copy(gcv[:, b, :], PB[4 * h + b][:, :]).then_inc(gc_done, 1)
                split(i + 7)
                if h == 0:
                    act.wait_ge(consts_step, CONSTS)
                act.wait_ge(t_T, h + 1)
                for c in range(0, 4, 2):
                    t = nc.scalar.copy(tT[h][:, c:c + 2, 1:1 + SEQ],
                                       PB[4 * h + c // 2][:, :].rearrange("p (c t) -> p c t", c=2))
                t.then_inc(tT_done, 1)
            for h in range(2):
                q = S_CIN + 9 + 2 * h
                split(min(q + 2, S_COUT + 1))
                act.wait_ge(slab_used, q + 1)
                if h:
                    act.wait_ge(gb_T, 1)
                for b in range(BLK):
                    nc.scalar.copy(gbs[:, b, :], PB[(2, 6)[h] + b][:, :]).then_inc(gb_done, 1)
            for k in range(KD):
                act.wait_ge(y_done, k + 1)
                nc.scalar.copy(actT_h[:, k * SEQ:(k + 1) * SEQ], yT[:, k, :]).then_inc(hn_hi, 1)
            split(S_MOE - 1)

            squares(3)
            act.wait_ge(sq_done, 4 * BLK)
            act.dma_start(tokB[:, D:2 * D], final_g.partition_broadcast(P)).then_inc(bcast_loaded, 16)
            norm_hi(3)
            for b in range(BLK):
                nc.scalar.copy(tokn_h[:, b, :], tokA[:, b, :]).then_inc(tok_hi, 1)
            act.wait_ge(rt_step, RT_DIFF)
            nc.scalar.activation(rs[:, 3, :], rs[:, 2, :], ACT.Exp).then_inc(exp_done, 1)

            def picked_copy(count, half):
                act.wait_ge(picked, count)
                nc.scalar.copy(pick[:, half * 512:(half + 1) * 512], PB[5][:, :]).then_inc(picked_sb, 1)

            def pickT_copy(count):
                act.wait_ge(pick_T, count)
                for k in range(KD):
                    nc.scalar.activation(pickT_h[:, k * P:(k + 1) * P], PB[k // 4][:, (k % 4) * P:(k % 4 + 1) * P],
                                         ACT.Copy, scale=prm[:, GAIN[3] + k:GAIN[3] + k + 1]).then_inc(pickT_hi, 1)

            def gated_hi(done_slabs):
                act.wait_ge(slab_used, done_slabs)
                for half in range(2):
                    nc.scalar.activation(ysc_h[:, half * 512:(half + 1) * 512], PB[6 + half][:, :], ACT.Copy,
                                         scale=gslot[:, 0:1]).then_inc(ysc_hi, 1)

            for half in range(2):
                picked_copy(half + 1, half)
            pickT_copy(1)
            act.wait_ge(consts_step, CONSTS)
            act.wait_ge(routed, 1)
            n_over = act.value_load(job_i[0:1, 0:1], min_val=0, max_val=MAX_OVER)
            with act.Fori(0, n_over + NE) as j:
                for m in range(PER):
                    i = S_MOE + m
                    act.wait_ge(raw_loaded[i % RAW], j * (16 * PER // RAW) + 16 * (i // RAW + 1))
                    act.wait_ge(slab_used, j * PER + (i - SPLIT + 1))
                    nc.scalar.copy(hi[:, i % SPLIT, :], raw[:, i % RAW, :]).then_inc(hi_done, 1)
                    if m == 1:
                        gated_hi(j * PER + S_MOE)
                    for c in range(NCH):
                        n = CHUNKS[c]
                        if m == min(LAST_H[c] + 2, PER - 1):
                            act.wait_ge(slab_used, j * PER + (S_MOE + LAST_H[c] + 1))
                            nc.scalar.activation(hid[:, 0, (c % 2) * 512:(c % 2) * 512 + n],
                                                 PB[2 * (c % 2)][:, 0:n], ACT.Silu).then_inc(silu_done, 1)
                        if m == min(T_AT[c] + 2, PER - 1):
                            act.wait_ge(hid_T, j * NCH + (BLK * NCH + c + 1))
                            nc.scalar.copy(hidT(mlp_h, c, P)[:, 0:n], PB[4][:, 0:n]).then_inc(hidT_hi, 1)
                    if m == PT_AT + 2:
                        act.wait_ge(place_T, j + 1)
                        nc.scalar.copy(onehotT[:, :], PB[5][:, 0:SEQ]).then_inc(placeT_done, 1)
                    for half in range(2):
                        if m == G_AT[half] + 2:
                            picked_copy(j * 2 + (3 + half), half)
                    if m == GT_AT + 2:
                        pickT_copy(j + 2)
            gated_hi((n_over + NE) * PER + S_MOE)

            for b in range(BLK):
                act.wait_ge(x_updated, (n_over + NE) * 4 + (X_C + 2 * b + 2))
                nc.scalar.activation(tokA[:, b, :], xres[:, b, :], ACT.Square,
                                     accum_out=ss[:, 4, b:b + 1]).then_inc(sq_done, 1)

        @block.vector
        def _(dve):
            chain, done = [0], [0]

            def link(ins):
                chain[0] += 1
                ins.then_inc(dve_step, 1)
                dve.wait_ge(dve_step, chain[0])

            def split(upto):
                while done[0] <= upto:
                    i = done[0]
                    dve.wait_ge(hi_done, i + 1)
                    nc.vector.tensor_sub(lo[:, i % SPLIT, :], raw[:, i % RAW, :],
                                         hi[:, i % SPLIT, :].bitcast(F32)).then_inc(lo_done, 1)
                    done[0] += 1

            roots = [0]

            def inv_root(src, scale, eps):
                r = roots[0]
                roots[0] += 1
                nc.vector.tensor_scalar(mean2[:, r:r + 1], src, scale, eps, ALU.mult, ALU.add).then_inc(mean2_done, 1)
                dve.wait_ge(root_done, r + 1)
                return root[:, r:r + 1]

            def normalise(n):
                for b in range(BLK):
                    dve.wait_ge(sq_done, BLK * n + b + 1)
                    r = inv_root(ss[:, n, b:b + 1], 1.0 / D, RMS_EPS)
                    nc.vector.tensor_scalar(tokA[:, b, :], xres[:, b, :], r, None,
                                            ALU.mult).then_inc(xn_done, 1)

            def norm_lo(n):
                base = n * KD + (8 if n > 0 else 0) + (8 if n > 2 else 0)
                for k in range(KD):
                    o = (k % 2) * SEQ
                    dve.wait_ge(hn_hi, base + 2 * (k // 2) + 2)
                    nc.vector.scalar_tensor_tensor(out=actT_l[:, k * SEQ:(k + 1) * SEQ], in0=PB[k // 2][:, o:o + SEQ],
                                                   scalar=prm[:, GAIN[n] + k:GAIN[n] + k + 1],
                                                   in1=actT_h[:, k * SEQ:(k + 1) * SEQ].bitcast(F32),
                                                   op0=ALU.mult, op1=ALU.subtract).then_inc(hn_lo, 1)

            def residual(done_slabs):
                dve.wait_ge(slab_used, done_slabs)
                for b in range(BLK):
                    for h in range(2):
                        xs = xres[:, b, h * 512:(h + 1) * 512]
                        nc.vector.tensor_tensor(xs, xs, PB[4 + 2 * b + h][:, :], ALU.add).then_inc(x_updated, 1)

            def layer_stats(src, s):
                link(nc.vector.bn_stats(bst[:, s, :], src))
                link(nc.vector.bn_aggr(mv[:, s, :], bst[:, s, :]))
                return inv_root(mv[:, s, 1:2], 1.0, LN_EPS)

            normalise(0)
            dve.wait_ge(prm_done, 1)
            norm_lo(0)
            dve.wait_ge(rw_hi, 1)
            nc.vector.tensor_sub(rw_hl[:, :, NE:2 * NE], rw[:, :, :], rw_hl[:, :, 0:NE].bitcast(F32)).then_inc(rw_lo, 1)
            split(S_IN + 5)
            for b in range(BLK):
                dve.wait_ge(sig_done, b + 1)
                nc.vector.tensor_tensor(glu[:, b, :], glu[:, b, :], PB[4 + b][:, :], ALU.mult).then_inc(glu_done, 1)
            split(S_IN + 6)

            def taps(a, z):
                for tap in range(a, z):
                    for c in range(HEADS):
                        w = prm[:, C_CONV + tap * HEADS + c:C_CONV + tap * HEADS + c + 1]
                        src = gluT[:, c, tap:tap + SEQ]
                        if tap == 0:
                            nc.vector.tensor_scalar(conv[:, c, :], src, w, prm[:, C_CB + c:C_CB + c + 1], ALU.mult,
                                                    ALU.add).then_inc(conv_step, 1)
                        else:
                            dve.wait_ge(conv_step, (tap - 1) * HEADS + c + 1)
                            nc.vector.scalar_tensor_tensor(out=conv[:, c, :], in0=src, scalar=w, in1=conv[:, c, :],
                                                           op0=ALU.mult, op1=ALU.add).then_inc(conv_step, 1)

            dve.wait_ge(gluT_done, 1)
            taps(0, 3)
            split(S_IN + 7)
            dve.wait_ge(bcast_loaded, 32)
            for b in range(BLK):
                dve.wait_ge(v_done, b + 1)
                r = layer_stats(va[:, b, :], b)
                link(nc.vector.tensor_scalar(va[:, b, :], va[:, b, :], mv[:, b, 0:1], r,
                                             ALU.subtract, ALU.mult))
                link(nc.vector.tensor_tensor(va[:, b, :], va[:, b, :], lna[:, 0, :], ALU.mult))
                nc.vector.tensor_tensor(va[:, b, :], va[:, b, :], lna[:, 1, :], ALU.add).then_inc(vn_done, 1)
            split(S_OUT)
            taps(3, 6)
            split(S_OUT + 1)
            for b in range(BLK):
                dve.wait_ge(u_done, b + 1)
                dve.wait_ge(gated, b + 1)
                for h in range(HEADS):
                    s = slice(h * P, (h + 1) * P)
                    t = nc.vector.scalar_tensor_tensor(out=ua[:, b, s], in0=PB[6 + b][:, s],
                                                       scalar=prm[:, C_BS + h:C_BS + h + 1], in1=ua[:, b, s],
                                                       op0=ALU.add, op1=ALU.mult)
                t.then_inc(aout_done, 1)
            for c in range(0, HEADS, 2):
                dve.wait_ge(hn_hi, KD + c + 2)
                nc.vector.tensor_tensor(actT_l[:, c * SEQ:(c + 2) * SEQ], PB[c // 2][:, :],
                                        actT_h[:, c * SEQ:(c + 2) * SEQ].bitcast(F32), ALU.subtract).then_inc(hn_lo, 2)
            taps(6, 10)
            split(S_OUT + 2)
            taps(10, 16)
            split(S_OUT + 3)
            taps(16, TAPS)
            for b in range(BLK):
                dve.wait_ge(c_T, b + 1)
                r = layer_stats(PB[b][:, :], 2 + b)
                nc.vector.tensor_scalar(cn[:, b, :], PB[b][:, :], mv[:, 2 + b, 0:1], r,
                                        ALU.subtract, ALU.mult).then_inc(cn_done, 1)
            for c in range(HEADS):
                dve.wait_ge(hn_hi, KD + 4 + c + 1)
                nc.vector.tensor_tensor(actT_l[:, (4 + c) * SEQ:(5 + c) * SEQ], cs[:, c, :],
                                        actT_h[:, (4 + c) * SEQ:(5 + c) * SEQ].bitcast(F32),
                                        ALU.subtract).then_inc(hn_lo, 1)
            split(S_FFN + 1)
            residual(S_FFN)

            normalise(1)
            norm_lo(1)
            for c in range(NCH):
                n, q = CHUNKS[c], S_FFN + LAST_H[c]
                split(min(q + 2, S_CIN - 1))
                for b in range(BLK):
                    dve.wait_ge(silu_done, BLK * c + b + 1)
                    hs = hid[:, b, (c % 2) * 512:(c % 2) * 512 + n]
                    nc.vector.tensor_tensor(hs, hs, PB[2 + b][:, 0:n], ALU.mult).then_inc(hid_done, 1)
                if c:
                    split(q + 3)
                for b in range(BLK):
                    dve.wait_ge(hidT_hi, BLK * c + b + 1)
                    o = b * 512
                    nc.vector.tensor_tensor(hidT(mlp_l, c, SEQ)[:, o:o + n], PB[b][:, 0:n],
                                            hidT(mlp_h, c, SEQ)[:, o:o + n].bitcast(F32),
                                            ALU.subtract).then_inc(hidT_lo, 1)
            split(S_CIN + 1)
            residual(S_CIN)

            normalise(2)
            norm_lo(2)
            for h in range(2):
                nc.vector.memset(tT[h][:, :, 0:1], 0.0).then_inc(dve_step, 1)
                nc.vector.memset(tT[h][:, :, TP - 1:TP], 0.0).then_inc(dve_step, 1)
            chain[0] += 4
            dve.wait_ge(dve_step, chain[0])

            def conv3(h):
                dve.wait_ge(tT_done, h + 1)
                for tap in range(3):
                    for c in range(4):
                        k = 4 * h + c
                        w = prm[:, C_OD + tap * KD + k:C_OD + tap * KD + k + 1]
                        src = tT[h][:, c, tap:tap + SEQ]
                        if tap == 0:
                            t = nc.vector.tensor_scalar(yT[:, k, :], src, w, None, ALU.mult)
                        else:
                            dve.wait_ge(dve_step, chain[0] - 3)
                            t = nc.vector.scalar_tensor_tensor(out=yT[:, k, :], in0=src, scalar=w, in1=yT[:, k, :],
                                                               op0=ALU.mult, op1=ALU.add)
                        t.then_inc(dve_step, 1)
                        chain[0] += 1

            def gate_b(h, banks):
                dve.wait_ge(gb_T, h + 1)
                dve.wait_ge(dve_step, chain[0])
                for c in range(4):
                    k = 4 * h + c
                    o = (c % 2) * SEQ
                    nc.vector.tensor_tensor(yT[:, k, :], yT[:, k, :], PB[banks[c // 2]][:, o:o + SEQ],
                                            ALU.mult).then_inc(y_done, 1)

            for h in range(2):
                i = S_CIN + 4 * h
                split(i + 5)
                dve.wait_ge(slab_used, i + 4)
                if h:
                    dve.wait_ge(t_T, 1)
                for b in range(BLK):
                    dve.wait_ge(gc_done, BLK * h + b + 1)
                    nc.vector.tensor_tensor(tt[:, b, :], gcv[:, b, :], PB[(2, 6)[h] + b][:, :],
                                            ALU.mult).then_inc(t_done, 1)
                split(i + 7)
                conv3(h) if h == 0 else None
            conv3(1)
            split(S_COUT + 1)
            for h in range(2):
                gate_b(h, ((0, 1), (2, 3))[h])
                for k in range(4 * h, 4 * h + 4):
                    dve.wait_ge(hn_hi, 3 * KD + 8 + k + 1)
                    nc.vector.tensor_tensor(actT_l[:, k * SEQ:(k + 1) * SEQ], yT[:, k, :],
                                            actT_h[:, k * SEQ:(k + 1) * SEQ].bitcast(F32),
                                            ALU.subtract).then_inc(hn_lo, 1)
            split(S_MOE - 1)
            residual(S_MOE)

            normalise(3)
            norm_lo(3)
            dve.wait_ge(logits_done, 1)
            for b in range(BLK):
                lg = rt[:, 0, b, :]
                link(nc.vector.tensor_copy(lg, PB[4 + b][:, 0:NE]))
                link(nc.vector.tensor_tensor(lg, lg, PB[4 + b][:, NE:2 * NE], ALU.add))

            def wide(v):
                return v.unsqueeze(2).to_broadcast([P, BLK, NE])

            def first_max(src, val, eq, key, kmax, hot):
                link(nc.vector.tensor_reduce(val, src, AX.X, ALU.max))
                link(nc.vector.tensor_tensor(eq, src, wide(val), ALU.is_equal))
                link(nc.vector.tensor_tensor(key, eq, iota_e[:, :, :], ALU.mult))
                link(nc.vector.tensor_reduce(kmax, key, AX.X, ALU.max))
                link(nc.vector.tensor_tensor(hot, key, wide(kmax), ALU.is_equal))

            dve.wait_ge(consts_step, CONSTS)
            hot1, hot2 = rt[:, 3, :, :], rt[:, 7, :, :]
            first_max(rt[:, 0, :, :], rs[:, 0, :], rt[:, 1, :, :], rt[:, 2, :, :], rs[:, 4, :], hot1)
            link(nc.vector.scalar_tensor_tensor(out=rt[:, 4, :, :], in0=hot1, scalar=-3.0e38, in1=rt[:, 0, :, :],
                                                op0=ALU.mult, op1=ALU.add))
            first_max(rt[:, 4, :, :], rs[:, 1, :], rt[:, 5, :, :], rt[:, 6, :, :], rs[:, 5, :], hot2)
            nc.vector.tensor_tensor(rs[:, 2, :], rs[:, 1, :], rs[:, 0, :], ALU.subtract).then_inc(rt_step, 1)
            nc.vector.tensor_tensor(sel_bf[:, :, :], hot1, hot2, ALU.add).then_inc(rt_step, 1)
            link(nc.vector.tensor_tensor(rt[:, 8, :, :], hot1, hot2, ALU.add))
            dve.wait_ge(exp_done, 1)
            link(nc.vector.tensor_scalar(rs[:, 6, :], rs[:, 3, :], 1.0, None, ALU.add))
            link(nc.vector.reciprocal(rs[:, 6, :], rs[:, 6, :]))
            link(nc.vector.tensor_tensor(rs[:, 7, :], rs[:, 3, :], rs[:, 6, :], ALU.mult))
            link(nc.vector.tensor_tensor(rt[:, 9, :, :], hot1, wide(rs[:, 6, :]), ALU.mult))
            link(nc.vector.tensor_tensor(rt[:, 10, :, :], hot2, wide(rs[:, 7, :]), ALU.mult))
            link(nc.vector.tensor_tensor(gatej[:, :, 0:NE], rt[:, 9, :, :], rt[:, 10, :, :], ALU.add))
            dve.wait_ge(counts_done, 1)
            pos = PB[6][:, 0:2 * NE].rearrange("p (b e) -> p b e", b=BLK)
            link(nc.vector.scalar_tensor_tensor(out=rt[:, 11, :, :], in0=pos, scalar=1.0, in1=rt[:, 8, :, :],
                                                op0=ALU.add, op1=ALU.mult))
            link(nc.vector.tensor_scalar(posj[:, :, 0:NE], rt[:, 11, :, :], -1.0, None, ALU.add))

            def one_hot(job):
                for b in range(BLK):
                    t = nc.vector.tensor_scalar(onehot[:, b, :], iota_s[:, :], posj[:, b, bass.ds(job, 1)], None,
                                                ALU.is_equal)
                t.then_inc(place_done, 1)

            one_hot(0)
            for b in range(BLK):
                dve.wait_ge(tok_hi, b + 1)
                t = nc.vector.tensor_sub(tokn_l[:, b, :], tokA[:, b, :], tokn_h[:, b, :].bitcast(F32))
            t.then_inc(tok_lo, 1)
            over = ov[:, 0, :]
            link(nc.vector.tensor_scalar(over, PB[6][:, 2 * NE:3 * NE], float(P), None, ALU.is_gt))
            link(nc.vector.tensor_reduce(ovs[:, 0:1], over, AX.X, ALU.add))
            link(nc.vector.tensor_copy(job_i[:, 0:1], ovs[:, 0:1]))
            for i in range(MAX_OVER):
                key, hot, ids = ov[:, 1, :], ov[:, 2, :], ov[:, 3, :]
                link(nc.vector.tensor_tensor(key, over, iota_e[:, 0, :], ALU.mult))
                link(nc.vector.tensor_reduce(ovs[:, 1:2], key, AX.X, ALU.max))
                link(nc.vector.scalar_tensor_tensor(out=hot, in0=key, scalar=ovs[:, 1:2], in1=over,
                                                    op0=ALU.is_equal, op1=ALU.mult))
                link(nc.vector.tensor_tensor(over, over, hot, ALU.subtract))
                link(nc.vector.tensor_tensor(ids, hot, iota_id[:, :], ALU.mult))
                link(nc.vector.tensor_reduce(ovs[:, 2:3], ids, AX.X, ALU.add))
                link(nc.vector.tensor_copy(job_i[:, 1 + i:2 + i], ovs[:, 2:3]))
                for b in range(BLK):
                    q = rt[:, 1 + b, 0, :]
                    link(nc.vector.scalar_tensor_tensor(out=q, in0=posj[:, b, 0:NE], scalar=float(1 - P), in1=hot,
                                                        op0=ALU.add, op1=ALU.mult))
                    link(nc.vector.tensor_reduce(rs[:, 8, b:b + 1], q, AX.X, ALU.add))
                    link(nc.vector.tensor_scalar(posj[:, b, NE + i:NE + i + 1], rs[:, 8, b:b + 1], -1.0, None, ALU.add))
                    link(nc.vector.tensor_tensor(q, gatej[:, b, 0:NE], hot, ALU.mult))
                    link(nc.vector.tensor_reduce(gatej[:, b, NE + i:NE + i + 1], q, AX.X, ALU.add))
            link(nc.vector.tensor_copy(gate_hl[:, :, :, 0], gatej[:, :, :]))
            link(nc.vector.tensor_tensor(gate_hl[:, :, :, 1], gatej[:, :, :], gate_hl[:, :, :, 0].bitcast(F32),
                                         ALU.subtract))
            nc.vector.memset(gslot[:, :], 0.0).then_inc(routed, 1)

            def pickT_split(first, hi_count):
                for k in range(KD):
                    dve.wait_ge(pickT_hi, hi_count + 4 * (k // 4 + 1))
                    s = slice(k * P, (k + 1) * P)
                    t = nc.vector.scalar_tensor_tensor(out=pickT_l[:, s], in0=PB[k // 4][:, (k % 4) * P:(k % 4 + 1) * P],
                                                       scalar=prm[:, GAIN[3] + k:GAIN[3] + k + 1],
                                                       in1=pickT_h[:, s].bitcast(F32), op0=ALU.mult, op1=ALU.subtract)
                t.then_inc(pickT_lo, 1)

            def gated_lo(hi_count):
                for half in range(2):
                    dve.wait_ge(ysc_hi, hi_count + (half + 1))
                    s = slice(half * 512, (half + 1) * 512)
                    t = nc.vector.scalar_tensor_tensor(out=ysc_l[:, s], in0=PB[6 + half][:, :], scalar=gslot[:, 0:1],
                                                       in1=ysc_h[:, s].bitcast(F32), op0=ALU.mult, op1=ALU.subtract)
                t.then_inc(ysc_lo, 1)

            def scatter_add(job4, piece):
                dve.wait_ge(scat, job4 + (piece + 1))
                dve.wait_ge(x_updated, job4 + (X_C - 3 + piece))
                xs = xres[:, piece // 2, (piece % 2) * 512:(piece % 2 + 1) * 512]
                nc.vector.tensor_tensor(xs, xs, PB[5][:, :], ALU.add).then_inc(x_updated, 1)

            pickT_split(1, 0)
            dve.wait_ge(routed, 1)
            n_over = dve.value_load(job_i[0:1, 0:1], min_val=0, max_val=MAX_OVER)
            with dve.Fori(0, n_over + NE) as j:
                for m in range(PER):
                    i = S_MOE + m
                    dve.wait_ge(hi_done, j * PER + (i + 1))
                    nc.vector.tensor_sub(lo[:, i % SPLIT, :], raw[:, i % RAW, :],
                                         hi[:, i % SPLIT, :].bitcast(F32)).then_inc(lo_done, 1)
                    if m == 1:
                        gated_lo(j * 2)
                    for c in range(NCH):
                        n = CHUNKS[c]
                        if m == min(LAST_H[c] + 2, PER - 1):
                            dve.wait_ge(silu_done, j * NCH + (BLK * NCH + c + 1))
                            hs = hid[:, 0, (c % 2) * 512:(c % 2) * 512 + n]
                            nc.vector.tensor_tensor(hs, hs, PB[2 * (c % 2) + 1][:, 0:n], ALU.mult).then_inc(hid_done, 1)
                        if m == min(T_AT[c] + 2, PER - 1):
                            dve.wait_ge(hidT_hi, j * NCH + (BLK * NCH + c + 1))
                            nc.vector.tensor_tensor(hidT(mlp_l, c, P)[:, 0:n], PB[4][:, 0:n],
                                                    hidT(mlp_h, c, P)[:, 0:n].bitcast(F32),
                                                    ALU.subtract).then_inc(hidT_lo, 1)
                    for piece in range(4):
                        if m == SC_AT[piece] + 2:
                            scatter_add(j * 4, piece)
                    if m == PT_AT + 2:
                        dve.wait_ge(placeT_done, j + 1)
                        nc.vector.tensor_reduce(gslot[:, 0:1], PB[5][:, SEQ:SEQ + 2], AX.X,
                                                ALU.add).then_inc(gslot_done, 1)
                        one_hot(j + 1)
                    if m == GT_AT + 2:
                        pickT_split(0, j * KD + KD)
            jobs = n_over + NE
            gated_lo(jobs * 2)
            for piece in range(4):
                scatter_add(jobs * 4, piece)

            dve.wait_ge(bcast_loaded, 48)
            for b in range(BLK):
                dve.wait_ge(sq_done, 4 * BLK + b + 1)
                r = inv_root(ss[:, 4, b:b + 1], 1.0 / D, RMS_EPS)
                nc.vector.scalar_tensor_tensor(out=tokA[:, b, :], in0=xres[:, b, :], scalar=r,
                                               in1=tokB[:, D:2 * D], op0=ALU.mult, op1=ALU.mult).then_inc(out_ready, 1)


_INS = ["x", "norm_mix_g", "norm_ffn_g", "ev_w_in", "ev_ws", "ev_bs", "ev_ln_a_g", "ev_ln_a_b", "ev_conv_w",
        "ev_conv_b", "ev_ln_b_g", "ev_ln_b_b", "ev_w_out", "od_w_in", "od_conv_w", "od_w_out", "ffn_w1", "ffn_w3",
        "ffn_w2", "moe_router", "moe_w1", "moe_w3", "moe_w2", "final_g"]


def kernel(**inputs):
    import numpy as np
    import concourse.bacc as bacc
    from concourse.bass_utils import run_bass_kernel_spmd

    nc = bacc.Bacc("TRN2", target_bir_lowering=False, num_devices=1)
    arrays, args = {}, []
    for name in _INS:
        a = np.ascontiguousarray(inputs[name])
        arrays[f"in_{name}"] = a
        args.append(nc.dram_tensor(f"in_{name}", a.shape, mybir.dt.from_np(a.dtype), kind="ExternalInput").ap())
    out = nc.dram_tensor("out_0", (1, SEQ, D), F32, kind="ExternalOutput").ap()
    trunk(nc, *args, out)
    r = run_bass_kernel_spmd(nc, [arrays], core_ids=[0])
    return r.results[0]["out_0"]
```

```python
from contextlib import ExitStack

import concourse.bass as bass
from concourse import mybir

ALU = mybir.AluOpType
ACT = mybir.ActivationFunctionType
AX = mybir.AxisListType
F32 = mybir.dt.float32
F32R = mybir.dt.float32r
BF16 = mybir.dt.bfloat16
I32 = mybir.dt.int32

P = 128
D = 1024
SEQ = 256
BLK = SEQ // P
KD = D // P
AW = 512
HEADS = AW // P
TAPS = 31
PAD = TAPS // 2
FF = 2816
NE = 8
RMS_EPS = 1e-6
LN_EPS = 1e-5

SLAB = 2048
RAW = 11
SPLIT = 3
CH = 512
CHUNKS = [CH] * (FF // CH) + [FF % CH]
NCH = len(CHUNKS)
MAX_OVER = (2 * SEQ) // (P + 1)
MAX_JOBS = NE + MAX_OVER


def swiglu_slabs(order):
    out = []
    for step, c in order:
        whole = CHUNKS[c] == CH
        if step == "H":
            out += [(k, c, h) for h in ([0, 1] if whole else [None]) for k in ("w1", "w3")]
        else:
            out += [("w2", c, h) for h in ([0, 1] if whole else [0])]
    return out


def places(slabs):
    last_h = [max(i for i, s in enumerate(slabs) if s[0] != "w2" and s[1] == c) for c in range(NCH)]
    first_y = [min(i for i, s in enumerate(slabs) if s[0] == "w2" and s[1] == c) for c in range(NCH)]
    return last_h, first_y


DENSE = swiglu_slabs([x for c in range(NCH + 1) for x in [("H", c)] * (c < NCH) + [("Y", c - 1)] * (c > 0)])
EXPERT = swiglu_slabs([("H", 0), ("H", 1), ("Y", 0), ("H", 2), ("Y", 1), ("H", 3), ("Y", 2), ("H", 4), ("H", 5),
                       ("Y", 3), ("Y", 4), ("Y", 5)])
PER = len(DENSE)
LAST_H, FIRST_Y = places(DENSE)
E_LAST_H, E_FIRST_Y = places(EXPERT)

S_IN = 0
S_OUT = S_IN + D * 4 * AW // (P * SLAB)
S_FFN = S_OUT + 2 * AW * D // (P * SLAB)
S_CIN = S_FFN + PER
S_COUT = S_CIN + D * 3 * D // (P * SLAB)
S_MOE = S_COUT + D * D // (P * SLAB)
assert PER % RAW == 0 and PER % SPLIT == 0


T_AT = [4, 10, 16, 22, 27, 29]
T_BANK = [4, 6, 5, 7]
SC_AT = [3, 5, 6, 7]
LNA_AT = 22
PT_AT = 8
G_AT = [13, 19]
GT_AT = 28
RT_DIFF, RT_SEL = 1, 2
N_ROW_DMAS = 8
ROOTS = 5 * BLK + 2 * BLK


def trunk(nc, x, norm_mix_g, norm_ffn_g, ev_w_in, ev_ws, ev_bs, ev_ln_a_g, ev_ln_a_b, ev_conv_w,
          ev_conv_b, ev_ln_b_g, ev_ln_b_b, ev_w_out, od_w_in, od_conv_w, od_w_out, ffn_w1, ffn_w3,
          ffn_w2, moe_router, moe_w1, moe_w3, moe_w2, final_g, out):
    ctx = ExitStack()
    with ctx:
        def sb(name, shape, dt=F32):
            return ctx.enter_context(nc.sbuf_tensor(name, shape, dt))

        def sem(name):
            return ctx.enter_context(nc.semaphore(name))

        raw = sb("raw", [P, RAW, SLAB])
        hi = sb("hi", [P, SPLIT, SLAB], F32R)
        lo = sb("lo", [P, SPLIT, SLAB], F32R)
        xres = sb("xres", [P, BLK, D])
        actT_h = sb("actT_h", [P, KD * SEQ], F32R)
        actT_l = sb("actT_l", [P, KD * SEQ], F32R)
        tokA = sb("tokA", [P, BLK, D])
        tokB = sb("tokB", [P, 2 * D])
        MLP = 3072
        with nc.sbuf_tensor("scratch", [P, 2 * MLP], F32) as scratch:
            pass
        mlp_h = sb("mlp_h", [P, MLP], F32R)
        mlp_l = sb("mlp_l", [P, MLP], F32R)
        ident = sb("ident", [P, P])
        iota_s = sb("iota_s", [P, P])
        onehot = sb("onehot", [P, BLK, P], F32R)
        onehotT = sb("onehotT", [P, SEQ], F32R)
        tri = sb("tri", [P, P], BF16)
        ones = sb("ones", [P, P], BF16)
        prm = sb("prm", [P, 196])
        rw = sb("rw", [P, KD, NE])
        rw_hl = sb("rw_hl", [P, KD, 2 * NE], F32R)
        ss = sb("ss", [P, 5, BLK])
        mean2 = sb("mean2", [P, ROOTS])
        root = sb("root", [P, ROOTS])
        power = sb("power", [P, 1])
        bst = sb("bst", [P, 4, 6])
        mv = sb("mv", [P, 4, 2])
        rt = sb("rt", [P, 12, BLK, NE])
        rs = sb("rs", [P, 10, BLK])
        sel_bf = sb("sel_bf", [P, BLK, NE], BF16)
        iota_e = sb("iota_e", [P, BLK, NE])
        iota_id = sb("iota_id", [P, NE])
        posj = sb("posj", [P, BLK, MAX_JOBS + 1])
        gatej = sb("gatej", [P, BLK, MAX_JOBS + 1])
        gate_hl = sb("gate_hl", [P, BLK, MAX_JOBS + 1, 2], F32R)
        ov = sb("ov", [P, 6, NE])
        ovs = sb("ovs", [P, 8])
        job_i = sb("job_i", [P, 1 + MAX_OVER], I32)
        gslot = sb("gslot", [P, 1])

        PB = [ctx.enter_context(nc.psum_tensor(f"PB{i}", [P, 512], F32)) for i in range(8)]

        raw_loaded = [sem(f"raw_loaded{i}") for i in range(RAW)]
        hi_done = sem("hi_done")
        lo_done = sem("lo_done")
        slab_used = sem("slab_used")
        x_loaded = sem("x_loaded")
        rows_loaded = sem("rows_loaded")
        ws_loaded = sem("ws_loaded")
        bcast_loaded = sem("bcast_loaded")
        router_loaded = sem("router_loaded")
        consts_step = sem("consts_step")
        setup_T = sem("setup_T")
        prm_done = sem("prm_done")
        x_updated = sem("x_updated")
        sq_done = sem("sq_done")
        x_T = sem("x_T")
        half_out = sem("half_out")
        hn_hi = sem("hn_hi")
        hn_lo = sem("hn_lo")
        dve_step = sem("dve_step")
        mean2_done = sem("mean2_done")
        root_done = sem("root_done")
        sig_done = sem("sig_done")
        glu_done = sem("glu_done")
        glu_T = sem("glu_T")
        gluT_done = sem("gluT_done")
        conv_dve = sem("conv_dve")
        tap_product = sem("tap_product")
        conv_pool = sem("conv_pool")
        v_done = sem("v_done")
        vn_done = sem("vn_done")
        gated = sem("gated")
        u_done = sem("u_done")
        aout_done = sem("aout_done")
        aout_T = sem("aout_T")
        c_T = sem("c_T")
        cn_done = sem("cn_done")
        cn_T = sem("cn_T")
        cs_done = sem("cs_done")
        gc_done = sem("gc_done")
        t_done = sem("t_done")
        t_T = sem("t_T")
        tT_done = sem("tT_done")
        gb_done = sem("gb_done")
        gb_T = sem("gb_T")
        y_done = sem("y_done")
        silu_done = sem("silu_done")
        hid_done = sem("hid_done")
        hid_T = sem("hid_T")
        hidT_hi = sem("hidT_hi")
        hidT_lo = sem("hidT_lo")
        logits_done = sem("logits_done")
        exp_done = sem("exp_done")
        rt_step = sem("rt_step")
        pool_step = sem("pool_step")
        chosen = sem("chosen")
        gates_split = sem("gates_split")
        counts_done = sem("counts_done")
        rw_hi = sem("rw_hi")
        rw_lo = sem("rw_lo")
        tok_hi = sem("tok_hi")
        tok_lo = sem("tok_lo")
        routed = sem("routed")
        place_done = sem("place_done")
        picked = sem("picked")
        picked_sb = sem("picked_sb")
        pick_T = sem("pick_T")
        pickT_hi = sem("pickT_hi")
        pickT_lo = sem("pickT_lo")
        place_T = sem("place_T")
        placeT_done = sem("placeT_done")
        gslot_done = sem("gslot_done")
        ysc_hi = sem("ysc_hi")
        ysc_lo = sem("ysc_lo")
        scat = sem("scat")
        out_ready = sem("out_ready")
        out_sem = sem("out_sem")

        def slab_source(w1, w3, w2, kind, c, part):
            if kind == "w2":
                r0 = c * CH + part * 2 * P
                return w2[r0:r0 + 2 * P, :].rearrange("(k p) n -> p k n", p=P)
            w = w1 if kind == "w1" else w3
            n0 = c * CH
            if part is None:
                return w[:, n0:n0 + CHUNKS[c]].rearrange("(k p) n -> p k n", p=P)
            return w[part * 4 * P:(part + 1) * 4 * P, n0:n0 + CH].rearrange("(k p) n -> p k n", p=P)

        def in_source(w, col, part):
            return w[part * 4 * P:(part + 1) * 4 * P, col:col + 512].rearrange("(k p) n -> p k n", p=P)

        def out_source(w, i):
            return w[i * 2 * P:(i + 1) * 2 * P, :].rearrange("(k p) n -> p k n", p=P)

        def half_source(w, col):
            return w[:, col:col + 256].rearrange("(k p) n -> p k n", p=P)

        sources = [half_source(ev_w_in[0], col + 256 * h) for h in range(2) for col in (2 * AW, 3 * AW)]
        sources += [in_source(ev_w_in[0], col, h) for col in (AW, 0) for h in range(2)]
        sources += [out_source(ev_w_out[0], i) for i in range(4)]
        sources += [slab_source(ffn_w1[0], ffn_w3[0], ffn_w2[0], *s) for s in DENSE]
        for col in (D, D + 512):
            sources += [in_source(od_w_in[0], col + v, h) for h in range(2) for v in (0, D)]
        sources += [in_source(od_w_in[0], col, h) for col in (0, 512) for h in range(2)]
        sources += [out_source(od_w_out[0], i) for i in range(4)]
        assert len(sources) == S_MOE

        def raw_as(slot, like):
            k = like.shape[1]
            return raw[:, slot, :].rearrange("p (k n) -> p k n", k=k)

        C_CONV, C_BS = 0, TAPS * HEADS
        C_MIX = C_BS + HEADS
        C_FFN = C_MIX + 2 * KD
        C_CB = C_FFN + 2 * KD
        C_LG = C_CB + HEADS
        C_LB = C_LG + HEADS
        C_OD = C_LB + HEADS
        N_ROWS2 = C_OD + 3 * KD - P
        GAIN = [C_MIX, C_FFN, C_MIX + KD, C_FFN + KD]

        lna = tokB[:, 0:2 * AW].rearrange("p (a n) -> p a n", a=2)
        ws_rows = tokB[:, 1024:1536].rearrange("p (h s) -> p h s", h=HEADS)
        prm_rows = tokB[:, 1536:1792].rearrange("p (a n) -> p a n", a=2)
        glu = scratch[:, 0:1024].rearrange("p (b n) -> p b n", b=BLK)
        GP = SEQ + 2 * PAD
        gluT = scratch[:, 1024:1024 + HEADS * GP].rearrange("p (c t) -> p c t", c=HEADS)
        o = 1024 + HEADS * GP
        conv = scratch[:, o:o + 1024].rearrange("p (c t) -> p c t", c=HEADS)
        va = scratch[:, o + 1024:o + 2048].rearrange("p (b n) -> p b n", b=BLK)
        ua = scratch[:, o + 2048:o + 3072].rearrange("p (b n) -> p b n", b=BLK)
        wsT = scratch[:, o + 3072:o + 3584].rearrange("p (h t) -> p h t", h=HEADS)
        dve_sum = tokA[:, 1, 0:SEQ]
        tap_ring = [tokA[:, 0, i * SEQ:(i + 1) * SEQ] for i in range(4)]
        tap_ring += [tokA[:, 1, i * SEQ:(i + 1) * SEQ] for i in range(1, 4)]
        cn = tokA[:, 0, :].rearrange("p (b n) -> p b n", b=BLK)
        cs = glu.rearrange("p b n -> p (b n)").rearrange("p (c t) -> p c t", c=HEADS)
        gcv = scratch[:, 0:1024].rearrange("p (b n) -> p b n", b=BLK)
        tt = scratch[:, 1024:2048].rearrange("p (b n) -> p b n", b=BLK)
        TP = SEQ + 2
        tT = [scratch[:, 2048 + h * 4 * TP:2048 + (h + 1) * 4 * TP].rearrange("p (c t) -> p c t", c=4)
              for h in range(2)]
        gbs = scratch[:, 4112:5136].rearrange("p (b n) -> p b n", b=BLK)
        yT = tokA[:, :, :].rearrange("p b n -> p (b n)").rearrange("p (k t) -> p k t", k=KD)
        hid = tokA

        def hidT(t, c, w):
            o = 8 * w if c == NCH - 1 and w == SEQ else (c % 2) * 4 * w
            return t[:, o:o + 4 * w]

        tokn_h = mlp_h[:, 1024:3072].rearrange("p (b n) -> p b n", b=BLK)
        tokn_l = mlp_l[:, 1024:3072].rearrange("p (b n) -> p b n", b=BLK)
        pick = tokB[:, 0:D]
        pickT_h, pickT_l = actT_h[:, 0:D], actT_l[:, 0:D]
        ysc_h, ysc_l = actT_h[:, D:2 * D], actT_l[:, D:2 * D]

        X_C = 12

        R_NORM = [0, 3 * BLK, 4 * BLK, 5 * BLK, 6 * BLK]
        R_LNA, R_LNB = BLK, 2 * BLK

        def rms(n, b):
            return root[:, R_NORM[n] + b:R_NORM[n] + b + 1]

        block = ctx.enter_context(nc.Block())

        @block.sync
        def _(sp):
            for b in range(BLK):
                sp.dma_start(xres[:, b, :], x[0, b * P:(b + 1) * P, :]).then_inc(x_loaded, 16)
            r = 0
            for src in (norm_mix_g.rearrange("l (k n) -> (l k) n", n=P),
                        norm_ffn_g.rearrange("l (k n) -> (l k) n", n=P),
                        ev_conv_b.rearrange("l (k n) -> (l k) n", n=P),
                        ev_ln_b_g.rearrange("l (k n) -> (l k) n", n=P),
                        ev_ln_b_b.rearrange("l (k n) -> (l k) n", n=P),
                        od_conv_w[0].rearrange("t (k n) -> (t k) n", n=P)):
                sp.dma_start(prm_rows[r:r + src.shape[0], 1, :], src).then_inc(rows_loaded, 16)
                r += src.shape[0]
            sp.dma_start(prm_rows[0:TAPS * HEADS, 0, :],
                         ev_conv_w[0].rearrange("t (c n) -> (t c) n", n=P)).then_inc(rows_loaded, 16)
            sp.dma_start(prm_rows[TAPS * HEADS:P, 0, :], ev_bs[0]).then_inc(rows_loaded, 16)
            for i, src in enumerate(sources):
                if i == 4:
                    sp.dma_start(ws_rows, ev_ws[0].rearrange("h t s -> t h s")).then_inc(ws_loaded, 16)
                    sp.dma_start(lna[:, 0, :], ev_ln_a_g.partition_broadcast(P)).then_inc(bcast_loaded, 16)
                    sp.dma_start(lna[:, 1, :], ev_ln_a_b.partition_broadcast(P)).then_inc(bcast_loaded, 16)
                    sp.dma_start(rw[:, :, :], moe_router[0].rearrange("(k p) e -> p k e", p=P)).then_inc(router_loaded, 16)
                if i >= RAW:
                    sp.wait_ge(lo_done, i - RAW + 1)
                sp.dma_start(raw_as(i % RAW, src), src).then_inc(raw_loaded[i % RAW], 16)

            def expert_slabs(job, e):
                w1, w3, w2 = (w[0, bass.ds(e, 1)].rearrange("a r n -> (a r) n")
                              for w in (moe_w1, moe_w3, moe_w2))
                for m, s in enumerate(EXPERT):
                    i = S_MOE + m
                    src = slab_source(w1, w3, w2, *s)
                    sp.wait_ge(lo_done, job * PER + (i - RAW + 1))
                    sp.dma_start(raw_as(i % RAW, src), src).then_inc(raw_loaded[i % RAW], 16)

            with sp.Fori(0, NE) as j:
                expert_slabs(j, j)
            sp.wait_ge(routed, 1)
            n_over = sp.value_load(job_i[0:1, 0:1], min_val=0, max_val=MAX_OVER)
            with sp.If(n_over > 0):
                with sp.Fori(0, n_over) as i:
                    e = sp.value_load(job_i[0:1, bass.ds(1 + i, 1)], min_val=0, max_val=NE - 1)
                    expert_slabs(i + NE, e)

            sp.wait_ge(out_ready, BLK)
            sp.dma_start(out[0].rearrange("(b p) d -> p b d", p=P), tokA[:, :, :]).then_inc(out_sem, 16)
            sp.wait_ge(out_sem, 16)

        DVE_GROUPS, POOL_GROUPS = (0, 2), (1, 3)
        DVE_STEPS = len(DVE_GROUPS) * (TAPS + 1)
        PRODUCTS = [(c, tap) for c in POOL_GROUPS for tap in range(TAPS)]

        def adds(p):
            return sum(tap > 0 for c, tap in PRODUCTS[:p + 1])

        def tap_of(c, tap):
            return prm[:, C_CONV + tap * HEADS + c:C_CONV + tap * HEADS + c + 1], gluT[:, c, tap:tap + SEQ]

        @block.gpsimd
        def _(pool):
            n = [0]

            def step(ins):
                n[0] += 1
                ins.then_inc(consts_step, 1)

            step(nc.gpsimd.memset(ident[:, :], 0.0))
            pool.wait_ge(consts_step, 1)
            step(nc.gpsimd.affine_select(out=ident[:, :], in_=ident[:, :], compare_op=ALU.not_equal,
                                         fill=1.0, base=0, pattern=[[-1, P]], channel_multiplier=1))
            step(nc.gpsimd.memset(gluT[:, :, :], 0.0))
            step(nc.gpsimd.iota(iota_s[:, :], [[1, P]], base=0, channel_multiplier=0,
                                allow_small_or_imprecise_dtypes=True))
            step(nc.gpsimd.iota(iota_e[:, :, :], [[0, BLK], [-1, NE]], base=NE, channel_multiplier=0,
                                allow_small_or_imprecise_dtypes=True))
            step(nc.gpsimd.iota(iota_id[:, :], [[1, NE]], base=0, channel_multiplier=0,
                                allow_small_or_imprecise_dtypes=True))
            step(nc.gpsimd.memset(ones[:, :], 1.0))
            pool.wait_ge(consts_step, 7)
            step(nc.gpsimd.affine_select(out=tri[:, :], in_=ones[:, :], compare_op=ALU.is_gt,
                                         fill=0.0, base=0, pattern=[[1, P]], channel_multiplier=-1))
            step(nc.gpsimd.memset(posj[:, :, :], -1.0))
            step(nc.gpsimd.memset(gatej[:, :, :], 0.0))
            step(nc.gpsimd.memset(gslot[:, :], 0.0))
            step(nc.gpsimd.memset(onehotT[:, :].bitcast(F32), 0.0))

            step(nc.gpsimd.memset(power[:, :], -0.5))
            pool.wait_ge(consts_step, 13)

            def powers(a, z):
                for r in range(a, z):
                    pool.wait_ge(mean2_done, r + 1)
                    nc.gpsimd.tensor_tensor(root[:, r:r + 1], mean2[:, r:r + 1], power[:, :],
                                            ALU.pow).then_inc(root_done, 1)

            powers(0, BLK)
            for p, (c, tap) in enumerate(PRODUCTS):
                if tap:
                    pool.wait_ge(tap_product, p + 1)
                    if tap > 1:
                        pool.wait_ge(conv_pool, adds(p - 1))
                    acc = conv[:, c, :]
                    nc.gpsimd.tensor_tensor(acc, acc, tap_ring[p % len(tap_ring)], ALU.add).then_inc(conv_pool, 1)
                if p == LNA_AT:
                    powers(BLK, 2 * BLK)
            powers(2 * BLK, ROOTS - BLK)

            m = [0]

            def link(ins):
                m[0] += 1
                ins.then_inc(pool_step, 1)
                pool.wait_ge(pool_step, m[0])

            def fold(dst, src):
                w = NE // 2
                while w >= 1:
                    link(nc.gpsimd.tensor_tensor(dst if w == 1 else src[:, 0:w], src[:, 0:w], src[:, w:2 * w], ALU.add))
                    w //= 2

            pool.wait_ge(chosen, 1)
            over = ov[:, 0, :]
            link(nc.gpsimd.tensor_scalar(over, ov[:, 4, :], float(P), None, ALU.is_gt))
            link(nc.gpsimd.tensor_copy(ov[:, 1, :], over))
            fold(ovs[:, 0:1], ov[:, 1, :])
            link(nc.gpsimd.tensor_copy(job_i[:, 0:1], ovs[:, 0:1]))
            before = ov[:, 5, :]
            link(nc.gpsimd.memset(before[:, 0:1], 0.0))
            for e in range(1, NE):
                link(nc.gpsimd.tensor_tensor(before[:, e:e + 1], before[:, e - 1:e], over[:, e - 1:e], ALU.add))
            for i in range(MAX_OVER):
                hot, ids = ov[:, 2, :], ov[:, 3, :]
                link(nc.gpsimd.tensor_scalar(hot, before, float(i), None, ALU.is_equal))
                link(nc.gpsimd.tensor_tensor(hot, hot, over, ALU.mult))
                link(nc.gpsimd.tensor_tensor(ids, hot, iota_id[:, :], ALU.mult))
                fold(ovs[:, 2:3], ids)
                link(nc.gpsimd.tensor_copy(job_i[:, 1 + i:2 + i], ovs[:, 2:3]))
                for b in range(BLK):
                    q = ov[:, 1, :]
                    link(nc.gpsimd.tensor_scalar(q, posj[:, b, 0:NE], float(1 - P), None, ALU.add))
                    link(nc.gpsimd.tensor_tensor(q, q, hot, ALU.mult))
                    fold(ovs[:, 3:4], q)
                    link(nc.gpsimd.tensor_scalar(posj[:, b, NE + i:NE + i + 1], ovs[:, 3:4], -1.0, None, ALU.add))
                    link(nc.gpsimd.tensor_tensor(q, gatej[:, b, 0:NE], hot, ALU.mult))
                    fold(gatej[:, b, NE + i:NE + i + 1], q)
            link(nc.gpsimd.tensor_copy(gate_hl[:, :, NE:, 0], gatej[:, :, NE:]))
            nc.gpsimd.tensor_tensor(gate_hl[:, :, NE:, 1], gatej[:, :, NE:], gate_hl[:, :, NE:, 0].bitcast(F32),
                                    ALU.subtract).then_inc(routed, 1)
            powers(ROOTS - BLK, ROOTS)

        CONSTS = 12

        @block.tensor
        def _(pe):
            def product(i, outs, stat, n, k_of, cols, first, last, idx=None, ready=None, halves=False):
                h = hi[:, i % SPLIT, :].rearrange("p (k n) -> p k n", n=n)
                l = lo[:, i % SPLIT, :].rearrange("p (k n) -> p k n", n=n)
                pe.wait_ge(lo_done, i + 1 if idx is None else idx + 1)
                steps = [(kk, k, b, q) for kk, k in enumerate(k_of) for b in range(len(outs))
                         for q in range(len(outs[b]))]
                if halves:
                    steps.sort(key=lambda s: s[3])
                mm = None
                for n_step, (kk, k, b, q) in enumerate(steps):
                    ps, s = outs[b][q], slice(q * cols, (q + 1) * cols)
                    if ready is not None and b == 0 and q == 0 and k % 2 == 0:
                        pe.wait_ge(hn_lo, ready + k + 2)
                    st, en = first and kk == 0, last and kk == len(k_of) - 1
                    nc.tensor.matmul(ps, stat(0, k, b), h[:, kk, s], start=st, stop=False)
                    nc.tensor.matmul(ps, stat(0, k, b), l[:, kk, s], start=False, stop=False)
                    mm = nc.tensor.matmul(ps, stat(1, k, b), h[:, kk, s], start=False, stop=en)
                    if halves and n_step == len(steps) // 2 - 1:
                        mm.then_inc(half_out, 1)
                mm.then_inc(slab_used, 1)

            def act_tile(part, k, b):
                t = (actT_h, actT_l)[part]
                return t[:, k * SEQ + b * P:k * SEQ + (b + 1) * P]

            def pick_tile(part, k, b):
                return (pickT_h, pickT_l)[part][:, k * P:(k + 1) * P]

            def stream_T(n, half):
                if n:
                    pe.wait_ge(x_updated, 4 * (n - 1) + 2 * half + 2)
                elif half == 0:
                    pe.wait_ge(x_loaded, 16 * BLK)
                for k in range(4 * half, 4 * half + 4):
                    for b in range(BLK):
                        o = (k % 2) * SEQ + b * P
                        t = nc.tensor.transpose(PB[T_BANK[k // 2]][:, o:o + P], xres[:, b, k * P:(k + 1) * P], ident[:, :])
                t.then_inc(x_T, 1)

            def in_half(i, h, banks, ready=None):
                product(i, [[PB[b][:, :]] for b in banks], act_tile, 512, range(4 * h, 4 * h + 4), 512, h == 0, h == 1,
                        ready=ready)

            def in_group(i, banks):
                for h in range(2):
                    in_half(i + h, h, banks)

            pe.wait_ge(consts_step, 2)
            for half in range(2):
                stream_T(0, half)
            pe.wait_ge(rows_loaded, 16 * N_ROW_DMAS)
            nc.tensor.transpose(PB[0][:, 0:P], prm_rows[:, 0, :], ident[:, :])
            nc.tensor.transpose(PB[0][:, P:P + N_ROWS2], prm_rows[0:N_ROWS2, 1, :],
                                ident[0:N_ROWS2, 0:N_ROWS2]).then_inc(setup_T, 1)

            def b_half(i, banks, ready=None):
                product(i, [[PB[b][:, 0:256]] for b in banks], act_tile, 256, range(KD), 256, True, True, ready=ready)

            def glu_half_T(h, bank):
                pe.wait_ge(glu_done, h + 1)
                for c in range(2):
                    for b in range(BLK):
                        o = c * SEQ + b * P
                        t = nc.tensor.transpose(PB[bank][:, o:o + P], glu[:, b, (2 * h + c) * P:(2 * h + c + 1) * P],
                                                ident[:, :])
                t.then_inc(glu_T, 1)

            pe.wait_ge(prm_done, 1)
            b_half(S_IN, (0, 1), ready=0)
            b_half(S_IN + 1, (2, 3))
            b_half(S_IN + 2, (4, 5))
            glu_half_T(0, 0)
            b_half(S_IN + 3, (6, 7))
            in_half(S_IN + 4, 0, (2, 3))
            glu_half_T(1, 4)
            pe.wait_ge(gluT_done, 1)
            pe.wait_ge(ws_loaded, 16)
            for h in range(HEADS):
                t = nc.tensor.transpose(PB[0][:, h * P:(h + 1) * P], ws_rows[:, h, :], ident[:, :])
            t.then_inc(setup_T, 1)
            in_half(S_IN + 5, 1, (2, 3))
            in_group(S_IN + 6, (6, 7))
            pe.wait_ge(prm_done, 2)
            pe.wait_ge(gluT_done, 2)
            for b in range(BLK):
                pe.wait_ge(vn_done, b + 1)
                for h in range(HEADS):
                    t = nc.tensor.matmul(PB[(1, 5)[b]][:, h * P:(h + 1) * P], wsT[:, h, :], va[:, b, h * P:(h + 1) * P],
                                         start=True, stop=True)
                t.then_inc(gated, 1)
            pe.wait_ge(aout_done, BLK)
            for c in range(HEADS):
                for b in range(BLK):
                    o = (c % 2) * SEQ + b * P
                    t = nc.tensor.transpose(PB[(0, 4)[c // 2]][:, o:o + P], ua[:, b, c * P:(c + 1) * P], ident[:, :])
                if c % 2:
                    t.then_inc(aout_T, 1)

            out_banks = [[PB[4 + 2 * b][:, :], PB[5 + 2 * b][:, :]] for b in range(BLK)]
            pe.wait_ge(hn_lo, KD + 4)
            for i in range(2):
                product(S_OUT + i, out_banks, act_tile, D, range(2 * i, 2 * i + 2), 512, i == 0, False)
            pe.wait_ge(conv_dve, DVE_STEPS)
            pe.wait_ge(conv_pool, adds(len(PRODUCTS) - 1))
            for b in range(BLK):
                for c in range(HEADS):
                    t = nc.tensor.transpose(PB[b][:, c * P:(c + 1) * P], conv[:, c, b * P:(b + 1) * P], ident[:, :])
                t.then_inc(c_T, 1)
            pe.wait_ge(cn_done, BLK)
            for b in range(BLK):
                for c in range(HEADS):
                    o = (c % 2) * SEQ + b * P
                    t = nc.tensor.transpose(PB[2 + c // 2][:, o:o + P], cn[:, b, c * P:(c + 1) * P], ident[:, :])
            t.then_inc(cn_T, 1)
            pe.wait_ge(hn_lo, KD + 8)
            for i in range(2, 4):
                product(S_OUT + i, out_banks, act_tile, D, range(2 * i, 2 * i + 2), 512, False, i == 3, halves=i == 3)

            def hid_transposes(c, b, bank, w, count):
                pe.wait_ge(hid_done, count)
                for kk in range(CHUNKS[c] // P):
                    t = nc.tensor.transpose(bank[:, kk * P:(kk + 1) * P], hid[:, b, (c % 2) * 512 + kk * P:
                                                                            (c % 2) * 512 + (kk + 1) * P], ident[:, :])
                t.then_inc(hid_T, 1)

            stream_T(1, 0)
            for m, (kind, c, part) in enumerate(DENSE):
                if m == 1:
                    stream_T(1, 1)
                i = S_FFN + m
                if kind == "w2":
                    if m == FIRST_Y[c]:
                        pe.wait_ge(hidT_lo, BLK * (c + 1))

                    def stat(p, k, b, c=c):
                        t = hidT((mlp_h, mlp_l)[p], c, SEQ)
                        return t[:, (b * 4 + k) * P:(b * 4 + k + 1) * P]
                    product(i, out_banks, stat, D, range(2 * part, 2 * part + 2), 512,
                            m == FIRST_Y[0], m == PER - 1, halves=m == PER - 1)
                else:
                    if c > 0 and part in (0, None) and kind == "w1":
                        pe.wait_ge(hidT_lo, BLK * c)
                    n = CHUNKS[c]
                    w = 0 if kind == "w1" else 2
                    ks = range(KD) if part is None else range(4 * part, 4 * part + 4)
                    product(i, [[PB[w + b][:, 0:n]] for b in range(BLK)], act_tile, n, ks, n,
                            part in (0, None), part in (1, None), ready=KD + 8 if c == 0 else None)
                if (c == 0 and m == LAST_H[0]) or (kind == "w2" and m == FIRST_Y[c] and c + 1 < NCH):
                    nxt = 0 if m == LAST_H[0] else c + 1
                    for b in range(BLK):
                        hid_transposes(nxt, b, PB[b], SEQ, BLK * nxt + b + 1)

            def tile_T(src, banks, signal):
                for b in range(BLK):
                    for c in range(4):
                        o = (c % 2) * SEQ + b * P
                        t = nc.tensor.transpose(PB[banks[c // 2]][:, o:o + P], src[:, b, c * P:(c + 1) * P], ident[:, :])
                t.then_inc(signal, 1)

            stream_T(2, 0)
            for i in range(4):
                in_half(S_CIN + i, i // 2, ((0, 1), (2, 3))[i % 2], ready=2 * KD + 8)
                if i == 0:
                    stream_T(2, 1)
            for i in range(4, 8):
                in_half(S_CIN + i, i // 2 - 2, ((4, 5), (6, 7))[i % 2])
                if i == 5:
                    pe.wait_ge(t_done, BLK)
                    tile_T(tt, (0, 1), t_T)
            in_group(S_CIN + 8, (2, 3))
            pe.wait_ge(t_done, 2 * BLK)
            tile_T(tt, (4, 5), t_T)
            product(S_CIN + 10, [[PB[6][:, :]], [PB[7][:, :]]], act_tile, 512, range(4), 512, True, False)
            pe.wait_ge(tT_done, 1)
            pe.wait_ge(gb_done, BLK)
            tile_T(gbs, (0, 1), gb_T)
            product(S_CIN + 11, [[PB[6][:, :]], [PB[7][:, :]]], act_tile, 512, range(4, 8), 512, False, True)
            pe.wait_ge(gb_done, 2 * BLK)
            tile_T(gbs, (2, 3), gb_T)
            pe.wait_ge(tT_done, 2)
            for i in range(4):
                if i % 2 == 0:
                    pe.wait_ge(hn_lo, 3 * KD + 8 + 4 * (i // 2 + 1))
                product(S_COUT + i, out_banks, act_tile, D, range(2 * i, 2 * i + 2), 512, i == 0, i == 3, halves=i == 3)

            pe.wait_ge(rw_lo, 1)
            for half in range(2):
                stream_T(3, half)
                pe.wait_ge(hn_lo, 3 * KD + 16 + 4 * half + 4)
                for k in range(4 * half, 4 * half + 4):
                    for b in range(BLK):
                        nc.tensor.matmul(PB[b][:, 0:2 * NE], act_tile(0, k, b), rw_hl[:, k, :], start=(k == 0), stop=False)
                        t = nc.tensor.matmul(PB[b][:, 0:2 * NE], act_tile(1, k, b), rw_hl[:, k, :], start=False,
                                             stop=(k == KD - 1))
            t.then_inc(logits_done, 1)
            pe.wait_ge(rt_step, RT_SEL)
            nc.tensor.matmul(PB[2][:, 0:NE], tri[:, :], sel_bf[:, 0, :], start=True, stop=True)
            nc.tensor.matmul(PB[2][:, NE:2 * NE], ones[:, :], sel_bf[:, 0, :], start=True, stop=False)
            nc.tensor.matmul(PB[2][:, NE:2 * NE], tri[:, :], sel_bf[:, 1, :], start=False, stop=True)
            nc.tensor.matmul(PB[2][:, 2 * NE:3 * NE], ones[:, :], sel_bf[:, 0, :], start=True, stop=False)
            nc.tensor.matmul(PB[2][:, 2 * NE:3 * NE], ones[:, :], sel_bf[:, 1, :], start=False,
                             stop=True).then_inc(counts_done, 1)

            MISC = PB[5]

            def gather(half):
                s = slice(half * 512, (half + 1) * 512)
                for c in range(BLK):
                    nc.tensor.matmul(MISC[:, :], onehot[:, c, :], tokn_h[:, c, s], start=(c == 0), stop=False)
                    t = nc.tensor.matmul(MISC[:, :], onehot[:, c, :], tokn_l[:, c, s], start=False, stop=(c == BLK - 1))
                t.then_inc(picked, 1)

            def gather_T(banks):
                for k in range(KD):
                    t = nc.tensor.transpose(banks[k // 4][:, (k % 4) * P:(k % 4 + 1) * P], pick[:, k * P:(k + 1) * P],
                                            ident[:, :])
                t.then_inc(pick_T, 1)

            def scatter(piece):
                b, s = piece % 2, slice((piece // 2) * 512, (piece // 2 + 1) * 512)
                st = onehotT[:, b * P:(b + 1) * P]
                nc.tensor.matmul(MISC[:, :], st, ysc_h[:, s], start=True, stop=False)
                nc.tensor.matmul(MISC[:, :], st, ysc_l[:, s], start=False, stop=True).then_inc(scat, 1)

            pe.wait_ge(place_done, 1)
            pe.wait_ge(tok_lo, 1)
            for half in range(2):
                if half:
                    pe.wait_ge(picked_sb, 1)
                gather(half)
            pe.wait_ge(picked_sb, 2)
            gather_T([PB[0], PB[1]])

            def run_job(j):
                pe.wait_ge(pickT_lo, j + 1)
                for m, (kind, c, part) in enumerate(EXPERT):
                    i = S_MOE + m
                    if kind == "w2":
                        if m == E_FIRST_Y[c]:
                            pe.wait_ge(hidT_lo, j * NCH + (BLK * NCH + c + 1))

                        def stat(p, k, b, c=c):
                            return hidT((mlp_h, mlp_l)[p], c, P)[:, k * P:(k + 1) * P]
                        product(i, [[PB[6][:, :], PB[7][:, :]]], stat, D, range(2 * part, 2 * part + 2), 512,
                                m == E_FIRST_Y[0], m == PER - 1, idx=j * PER + i)
                    else:
                        n = CHUNKS[c]
                        bank = PB[2 * (c % 2) + (0 if kind == "w1" else 1)]
                        ks = range(KD) if part is None else range(4 * part, 4 * part + 4)
                        product(i, [[bank[:, 0:n]]], pick_tile, n, ks, n, part in (0, None), part in (1, None),
                                idx=j * PER + i)
                    for c in range(NCH):
                        if m == T_AT[c]:
                            pe.wait_ge(hid_done, j * NCH + (BLK * NCH + c + 1))
                            if c:
                                pe.wait_ge(hidT_lo, j * NCH + (BLK * NCH + c))
                            for kk in range(CHUNKS[c] // P):
                                t = nc.tensor.transpose(PB[4][:, kk * P:(kk + 1) * P],
                                                        hid[:, 0, (c % 2) * 512 + kk * P:(c % 2) * 512 + (kk + 1) * P],
                                                        ident[:, :])
                            t.then_inc(hid_T, 1)
                    if m in SC_AT:
                        piece = SC_AT.index(m)
                        if piece == 0:
                            pe.wait_ge(ysc_lo, j + 1)
                        else:
                            pe.wait_ge(x_updated, j * 4 + (X_C + piece))
                        scatter(piece)
                    if m == PT_AT:
                        pe.wait_ge(x_updated, j * 4 + (X_C + 4))
                        for b in range(BLK):
                            nc.tensor.transpose(MISC[:, b * P:(b + 1) * P], onehot[:, b, :].bitcast(F32), ident[:, :])
                        for b in range(BLK):
                            t = nc.tensor.matmul(MISC[:, SEQ:SEQ + 2], onehot[:, b, :],
                                                 gate_hl[:, b, bass.ds(j, 1), :].rearrange("p a t -> p (a t)"),
                                                 start=(b == 0), stop=(b == BLK - 1))
                        t.then_inc(place_T, 1)
                    if m in G_AT:
                        half = G_AT.index(m)
                        if half == 0:
                            pe.wait_ge(placeT_done, j + 1)
                            pe.wait_ge(gslot_done, j + 1)
                            pe.wait_ge(place_done, j + 2)
                        else:
                            pe.wait_ge(picked_sb, j * 2 + 3)
                        gather(half)
                    if m == GT_AT:
                        pe.wait_ge(picked_sb, j * 2 + 4)
                        gather_T([PB[0], PB[1]])

            pe.wait_ge(gates_split, 1)
            with pe.Fori(0, NE) as j:
                run_job(j)
            pe.wait_ge(routed, 1)
            n_over = pe.value_load(job_i[0:1, 0:1], min_val=0, max_val=MAX_OVER)
            with pe.If(n_over > 0):
                with pe.Fori(0, n_over) as i:
                    run_job(i + NE)
            jobs = n_over + NE
            pe.wait_ge(ysc_lo, jobs + 1)
            for piece in range(4):
                if piece:
                    pe.wait_ge(x_updated, jobs * 4 + (X_C + piece))
                scatter(piece)

        @block.scalar
        def _(act):
            done = [0]

            def split(upto):
                while done[0] <= upto:
                    i = done[0]
                    act.wait_ge(raw_loaded[i % RAW], 16 * (i // RAW + 1))
                    if i >= SPLIT:
                        act.wait_ge(slab_used, i - SPLIT + 1)
                    nc.scalar.copy(hi[:, i % SPLIT, :], raw[:, i % RAW, :]).then_inc(hi_done, 1)
                    done[0] += 1

            def squares(n):
                for b in range(BLK):
                    if n == 0:
                        act.wait_ge(x_loaded, 16 * BLK)
                    else:
                        act.wait_ge(x_updated, 4 * (n - 1) + 3 + b)
                    if b or n:
                        act.wait_ge(sq_done, BLK * n + b)
                    nc.scalar.activation(tokB[:, D:2 * D] if n else scratch[:, 3072:4096], xres[:, b, :], ACT.Square,
                                         accum_out=ss[:, n, b:b + 1]).then_inc(sq_done, 1)

            def stream_hi(n):
                for half in range(2):
                    act.wait_ge(x_T, 2 * n + half + 1)
                    for k in range(4 * half, 4 * half + 4):
                        o = (k % 2) * SEQ
                        nc.scalar.activation(actT_h[:, k * SEQ:(k + 1) * SEQ], PB[T_BANK[k // 2]][:, o:o + SEQ],
                                             ACT.Copy, scale=prm[:, GAIN[n] + k:GAIN[n] + k + 1]).then_inc(hn_hi, 1)

            squares(0)
            act.wait_ge(setup_T, 1)
            nc.scalar.copy(prm[:, :], PB[0][:, 0:P + N_ROWS2]).then_inc(prm_done, 1)
            act.wait_ge(prm_done, 1)
            stream_hi(0)

            def b_gate(h):
                act.wait_ge(slab_used, S_IN + 2 * h + 2)
                for b in range(BLK):
                    act.wait_ge(root_done, R_NORM[0] + b + 1)
                    nc.scalar.activation(glu[:, b, h * 256:(h + 1) * 256], PB[(2, 6)[h] + b][:, 0:256], ACT.Sigmoid,
                                         scale=rms(0, b)).then_inc(sig_done, 1)

            sent = [0]

            def products(upto):
                while sent[0] < upto:
                    p = sent[0]
                    c, tap = PRODUCTS[p]
                    w, src = tap_of(c, tap)
                    if tap == 0:
                        act.wait_ge(gluT_done, c // 2 + 1)
                        nc.scalar.activation(conv[:, c, :], src, ACT.Identity, bias=prm[:, C_CB + c:C_CB + c + 1],
                                             scale=w).then_inc(tap_product, 1)
                    else:
                        if p >= len(tap_ring):
                            act.wait_ge(conv_pool, adds(p - len(tap_ring)))
                        nc.scalar.activation(tap_ring[p % len(tap_ring)], src, ACT.Copy, scale=w).then_inc(tap_product, 1)
                    sent[0] += 1

            def gluT_copy(h):
                act.wait_ge(glu_T, h + 1)
                nc.scalar.copy(gluT[:, 2 * h:2 * h + 2, PAD:PAD + SEQ],
                               PB[(0, 4)[h]][:, :].rearrange("p (c t) -> p c t", c=2)).then_inc(gluT_done, 1)

            split(S_IN + 3)
            b_gate(0)
            split(S_IN + 4)
            act.wait_ge(consts_step, 3)
            gluT_copy(0)
            products(7)
            split(S_IN + 5)
            b_gate(1)
            products(11)
            act.wait_ge(router_loaded, 16)
            nc.scalar.copy(rw_hl[:, :, 0:NE], rw[:, :, :]).then_inc(rw_hi, 1)
            split(S_IN + 6)
            products(14)
            gluT_copy(1)
            act.wait_ge(setup_T, 2)
            nc.scalar.copy(wsT, PB[0][:, :].rearrange("p (h t) -> p h t", h=HEADS)).then_inc(prm_done, 1)
            products(17)
            split(S_IN + 7)
            products(20)
            act.wait_ge(slab_used, S_IN + 6)
            for b in range(BLK):
                nc.scalar.activation(va[:, b, :], PB[2 + b][:, :], ACT.Gelu_apprx_tanh,
                                     scale=rms(0, b)).then_inc(v_done, 1)
            split(S_OUT)
            products(26)
            split(S_OUT + 1)
            products(32)
            act.wait_ge(slab_used, S_IN + 8)
            for b in range(BLK):
                nc.scalar.activation(ua[:, b, :], PB[6 + b][:, :], ACT.Gelu_apprx_tanh,
                                     scale=rms(0, b)).then_inc(u_done, 1)
            split(S_OUT + 2)
            products(35)
            for c in range(0, HEADS, 2):
                act.wait_ge(aout_T, c // 2 + 1)
                nc.scalar.copy(actT_h[:, c * SEQ:(c + 2) * SEQ], PB[(0, 4)[c // 2]][:, :]).then_inc(hn_hi, 2)
            products(44)
            split(S_OUT + 3)
            products(51)
            split(S_FFN)
            products(len(PRODUCTS))
            act.wait_ge(cn_T, 1)
            for c in range(HEADS):
                o = (c % 2) * SEQ
                nc.scalar.activation(cs[:, c, :], PB[2 + c // 2][:, o:o + SEQ], ACT.Silu,
                                     bias=prm[:, C_LB + c:C_LB + c + 1],
                                     scale=prm[:, C_LG + c:C_LG + c + 1]).then_inc(cs_done, 1)
            for c in range(HEADS):
                act.wait_ge(cs_done, c + 1)
                nc.scalar.copy(actT_h[:, (4 + c) * SEQ:(5 + c) * SEQ], cs[:, c, :]).then_inc(hn_hi, 1)
            split(S_FFN + 1)

            stream_hi(1)
            squares(1)
            for c in range(NCH):
                n, q = CHUNKS[c], S_FFN + LAST_H[c]
                split(min(q + 2, S_CIN - 1))
                act.wait_ge(slab_used, q + 1)
                for b in range(BLK):
                    if c == 0:
                        act.wait_ge(root_done, R_NORM[1] + b + 1)
                    if c > 1:
                        act.wait_ge(hid_T, BLK * (c - 2) + b + 1)
                    nc.scalar.activation(hid[:, b, (c % 2) * 512:(c % 2) * 512 + n], PB[b][:, 0:n],
                                         ACT.Silu, scale=rms(1, b)).then_inc(silu_done, 1)
                if c:
                    split(q + 3)
                for b in range(BLK):
                    act.wait_ge(hid_T, BLK * c + b + 1)
                    o = b * 512
                    nc.scalar.copy(hidT(mlp_h, c, SEQ)[:, o:o + n], PB[b][:, 0:n]).then_inc(hidT_hi, 1)

            split(S_CIN + 1)
            stream_hi(2)
            squares(2)

            def c_gate(h):
                act.wait_ge(slab_used, S_CIN + 4 * h + 3)
                if h:
                    act.wait_ge(t_done, BLK)
                for b in range(BLK):
                    act.wait_ge(root_done, R_NORM[2] + b + 1)
                    nc.scalar.activation(gcv[:, b, :], PB[4 * h + b][:, :], ACT.Copy, scale=rms(2, b)).then_inc(gc_done, 1)

            def tT_copy(h):
                act.wait_ge(t_T, h + 1)
                for c in range(0, 4, 2):
                    t = nc.scalar.copy(tT[h][:, c:c + 2, 1:1 + SEQ],
                                       PB[4 * h + c // 2][:, :].rearrange("p (c t) -> p c t", c=2))
                t.then_inc(tT_done, 1)

            def b_copy(h):
                act.wait_ge(slab_used, S_CIN + 10 + 2 * h)
                if h:
                    act.wait_ge(gb_T, 1)
                for b in range(BLK):
                    nc.scalar.activation(gbs[:, b, :], PB[(2, 6)[h] + b][:, :], ACT.Copy, scale=rms(2, b)).then_inc(gb_done, 1)

            def y_hi(h):
                for k in range(4 * h, 4 * h + 4):
                    act.wait_ge(y_done, k + 1)
                    nc.scalar.copy(actT_h[:, k * SEQ:(k + 1) * SEQ], yT[:, k, :]).then_inc(hn_hi, 1)

            split(S_CIN + 4)
            c_gate(0)
            split(S_CIN + 7)
            tT_copy(0)
            split(S_CIN + 8)
            c_gate(1)
            split(S_CIN + 11)
            b_copy(0)
            tT_copy(1)
            split(S_COUT + 1)
            y_hi(0)
            b_copy(1)
            y_hi(1)
            split(S_MOE - 1)

            stream_hi(3)
            squares(3)
            act.wait_ge(sq_done, 4 * BLK)
            act.dma_start(tokB[:, D:2 * D], final_g.partition_broadcast(P)).then_inc(bcast_loaded, 16)
            for b in range(BLK):
                act.wait_ge(root_done, R_NORM[3] + b + 1)
                nc.scalar.activation(tokn_h[:, b, :], xres[:, b, :], ACT.Copy, scale=rms(3, b)).then_inc(tok_hi, 1)
            act.wait_ge(rt_step, RT_DIFF)
            nc.scalar.activation(rs[:, 3, :], rs[:, 2, :], ACT.Exp).then_inc(exp_done, 1)

            def picked_copy(count, half):
                act.wait_ge(picked, count)
                nc.scalar.copy(pick[:, half * 512:(half + 1) * 512], PB[5][:, :]).then_inc(picked_sb, 1)

            def pickT_copy(count):
                act.wait_ge(pick_T, count)
                for k in range(KD):
                    nc.scalar.activation(pickT_h[:, k * P:(k + 1) * P], PB[k // 4][:, (k % 4) * P:(k % 4 + 1) * P],
                                         ACT.Copy, scale=prm[:, GAIN[3] + k:GAIN[3] + k + 1]).then_inc(pickT_hi, 1)

            def gated_hi(done_slabs):
                act.wait_ge(slab_used, done_slabs)
                for half in range(2):
                    nc.scalar.activation(ysc_h[:, half * 512:(half + 1) * 512], PB[6 + half][:, :], ACT.Copy,
                                         scale=gslot[:, 0:1]).then_inc(ysc_hi, 1)

            for half in range(2):
                picked_copy(half + 1, half)
            pickT_copy(1)
            act.wait_ge(consts_step, CONSTS)

            def run_job(j):
                for m in range(PER):
                    i = S_MOE + m
                    act.wait_ge(raw_loaded[i % RAW], j * (16 * PER // RAW) + 16 * (i // RAW + 1))
                    act.wait_ge(slab_used, j * PER + (i - SPLIT + 1))
                    nc.scalar.copy(hi[:, i % SPLIT, :], raw[:, i % RAW, :]).then_inc(hi_done, 1)
                    if m == 1:
                        gated_hi(j * PER + S_MOE)
                    for c in range(NCH):
                        n = CHUNKS[c]
                        if m == min(E_LAST_H[c] + 2, PER - 1):
                            act.wait_ge(slab_used, j * PER + (S_MOE + E_LAST_H[c] + 1))
                            nc.scalar.activation(hid[:, 0, (c % 2) * 512:(c % 2) * 512 + n],
                                                 PB[2 * (c % 2)][:, 0:n], ACT.Silu).then_inc(silu_done, 1)
                        if m == min(T_AT[c] + 2, PER - 1):
                            act.wait_ge(hid_T, j * NCH + (BLK * NCH + c + 1))
                            nc.scalar.copy(hidT(mlp_h, c, P)[:, 0:n], PB[4][:, 0:n]).then_inc(hidT_hi, 1)
                    if m == PT_AT + 2:
                        act.wait_ge(place_T, j + 1)
                        nc.scalar.copy(onehotT[:, :], PB[5][:, 0:SEQ]).then_inc(placeT_done, 1)
                    for half in range(2):
                        if m == G_AT[half] + 2:
                            picked_copy(j * 2 + (3 + half), half)
                    if m == GT_AT + 2:
                        pickT_copy(j + 2)

            with act.Fori(0, NE) as j:
                run_job(j)
            act.wait_ge(routed, 1)
            n_over = act.value_load(job_i[0:1, 0:1], min_val=0, max_val=MAX_OVER)
            with act.If(n_over > 0):
                with act.Fori(0, n_over) as i:
                    run_job(i + NE)
            gated_hi((n_over + NE) * PER + S_MOE)

            for b in range(BLK):
                act.wait_ge(x_updated, (n_over + NE) * 4 + (X_C + 3 + b))
                nc.scalar.activation(tokA[:, b, :], xres[:, b, :], ACT.Square,
                                     accum_out=ss[:, 4, b:b + 1]).then_inc(sq_done, 1)

        @block.vector
        def _(dve):
            chain, done = [0], [0]

            def link(ins):
                chain[0] += 1
                ins.then_inc(dve_step, 1)
                dve.wait_ge(dve_step, chain[0])

            def split(upto):
                while done[0] <= upto:
                    i = done[0]
                    dve.wait_ge(hi_done, i + 1)
                    nc.vector.tensor_sub(lo[:, i % SPLIT, :], raw[:, i % RAW, :],
                                         hi[:, i % SPLIT, :].bitcast(F32)).then_inc(lo_done, 1)
                    done[0] += 1

            def mean_square(src, r, scale, eps):
                nc.vector.tensor_scalar(mean2[:, r:r + 1], src, scale, eps, ALU.mult, ALU.add).then_inc(mean2_done, 1)

            def mean_squares(n):
                for b in range(BLK):
                    dve.wait_ge(sq_done, BLK * n + b + 1)
                    mean_square(ss[:, n, b:b + 1], R_NORM[n] + b, 1.0 / D, RMS_EPS)

            def stream_lo(n):
                base = n * KD + (8 if n > 0 else 0) + (8 if n > 2 else 0)
                for k in range(KD):
                    o = (k % 2) * SEQ
                    dve.wait_ge(hn_hi, base + 2 * (k // 2) + 2)
                    nc.vector.scalar_tensor_tensor(out=actT_l[:, k * SEQ:(k + 1) * SEQ],
                                                   in0=PB[T_BANK[k // 2]][:, o:o + SEQ],
                                                   scalar=prm[:, GAIN[n] + k:GAIN[n] + k + 1],
                                                   in1=actT_h[:, k * SEQ:(k + 1) * SEQ].bitcast(F32),
                                                   op0=ALU.mult, op1=ALU.subtract).then_inc(hn_lo, 1)

            def residual(n, done_slabs):
                for h in range(2):
                    if h == 0:
                        dve.wait_ge(half_out, n)
                    else:
                        dve.wait_ge(slab_used, done_slabs)
                    for b in range(BLK):
                        xs = xres[:, b, h * 512:(h + 1) * 512]
                        nc.vector.tensor_tensor(xs, xs, PB[4 + 2 * b + h][:, :], ALU.add).then_inc(x_updated, 1)

            def layer_stats(src, s, r):
                link(nc.vector.bn_stats(bst[:, s, :], src))
                link(nc.vector.bn_aggr(mv[:, s, :], bst[:, s, :]))
                mean_square(mv[:, s, 1:2], r, 1.0, LN_EPS)

            mean_squares(0)
            dve.wait_ge(prm_done, 1)
            stream_lo(0)

            def glu_half(h):
                for b in range(BLK):
                    dve.wait_ge(sig_done, BLK * h + b + 1)
                    g = glu[:, b, h * 256:(h + 1) * 256]
                    t = nc.vector.scalar_tensor_tensor(out=g, in0=PB[(0, 4)[h] + b][:, 0:256], scalar=rms(0, b), in1=g,
                                                       op0=ALU.mult, op1=ALU.mult)
                t.then_inc(glu_done, 1)

            def taps(e, a, z):
                c = DVE_GROUPS[e]
                base = e * (TAPS + 1)
                first_sum = conv[:, c, :]
                for tap in range(a, z):
                    w, src = tap_of(c, tap)
                    if tap == 0:
                        t = nc.vector.tensor_scalar(first_sum, src, w, prm[:, C_CB + c:C_CB + c + 1], ALU.mult, ALU.add)
                    elif tap == 1:
                        if e:
                            dve.wait_ge(conv_dve, base)
                        t = nc.vector.tensor_scalar(dve_sum, src, w, None, ALU.mult)
                    else:
                        dve.wait_ge(conv_dve, base + tap - 1)
                        acc = dve_sum if tap % 2 else first_sum
                        t = nc.vector.scalar_tensor_tensor(out=acc, in0=src, scalar=w, in1=acc, op0=ALU.mult, op1=ALU.add)
                    t.then_inc(conv_dve, 1)
                if z == TAPS:
                    dve.wait_ge(conv_dve, base + TAPS)
                    nc.vector.tensor_tensor(first_sum, first_sum, dve_sum, ALU.add).then_inc(conv_dve, 1)

            split(S_IN + 3)
            glu_half(0)
            split(S_IN + 4)
            dve.wait_ge(gluT_done, 1)
            taps(0, 0, 6)
            split(S_IN + 5)
            glu_half(1)
            dve.wait_ge(rw_hi, 1)
            nc.vector.tensor_sub(rw_hl[:, :, NE:2 * NE], rw[:, :, :], rw_hl[:, :, 0:NE].bitcast(F32)).then_inc(rw_lo, 1)
            taps(0, 6, 11)
            split(S_IN + 6)
            taps(0, 11, 17)
            split(S_IN + 7)
            dve.wait_ge(bcast_loaded, 32)
            for b in range(BLK):
                dve.wait_ge(v_done, b + 1)
                layer_stats(va[:, b, :], b, R_LNA + b)
            split(S_OUT)
            for b in range(BLK):
                dve.wait_ge(root_done, R_LNA + b + 1)
                link(nc.vector.tensor_scalar(va[:, b, :], va[:, b, :], mv[:, b, 0:1], root[:, R_LNA + b:R_LNA + b + 1],
                                             ALU.subtract, ALU.mult))
                link(nc.vector.tensor_tensor(va[:, b, :], va[:, b, :], lna[:, 0, :], ALU.mult))
                nc.vector.tensor_tensor(va[:, b, :], va[:, b, :], lna[:, 1, :], ALU.add).then_inc(vn_done, 1)
            taps(0, 17, 19)
            split(S_OUT + 1)
            for b in range(BLK):
                dve.wait_ge(u_done, b + 1)
                dve.wait_ge(gated, b + 1)
                for h in range(HEADS):
                    s = slice(h * P, (h + 1) * P)
                    t = nc.vector.scalar_tensor_tensor(out=ua[:, b, s], in0=PB[(1, 5)[b]][:, s],
                                                       scalar=prm[:, C_BS + h:C_BS + h + 1], in1=ua[:, b, s],
                                                       op0=ALU.add, op1=ALU.mult)
                t.then_inc(aout_done, 1)
            taps(0, 19, 22)
            for c in range(0, HEADS, 2):
                dve.wait_ge(hn_hi, KD + c + 2)
                nc.vector.tensor_tensor(actT_l[:, c * SEQ:(c + 2) * SEQ], PB[(0, 4)[c // 2]][:, :],
                                        actT_h[:, c * SEQ:(c + 2) * SEQ].bitcast(F32), ALU.subtract).then_inc(hn_lo, 2)
            split(S_OUT + 2)
            dve.wait_ge(gluT_done, 2)
            taps(0, 22, TAPS)
            split(S_OUT + 3)
            taps(1, 0, 12)
            split(S_FFN)
            taps(1, 12, TAPS)
            for b in range(BLK):
                dve.wait_ge(c_T, b + 1)
                layer_stats(PB[b][:, :], 2 + b, R_LNB + b)
            for b in range(BLK):
                dve.wait_ge(root_done, R_LNB + b + 1)
                nc.vector.tensor_scalar(cn[:, b, :], PB[b][:, :], mv[:, 2 + b, 0:1], root[:, R_LNB + b:R_LNB + b + 1],
                                        ALU.subtract, ALU.mult).then_inc(cn_done, 1)
            for c in range(HEADS):
                dve.wait_ge(hn_hi, KD + 4 + c + 1)
                nc.vector.tensor_tensor(actT_l[:, (4 + c) * SEQ:(5 + c) * SEQ], cs[:, c, :],
                                        actT_h[:, (4 + c) * SEQ:(5 + c) * SEQ].bitcast(F32),
                                        ALU.subtract).then_inc(hn_lo, 1)
            split(S_FFN + 1)
            residual(1, S_FFN)

            stream_lo(1)
            mean_squares(1)
            for c in range(NCH):
                n, q = CHUNKS[c], S_FFN + LAST_H[c]
                split(min(q + 2, S_CIN - 1))
                for b in range(BLK):
                    dve.wait_ge(silu_done, BLK * c + b + 1)
                    hs = hid[:, b, (c % 2) * 512:(c % 2) * 512 + n]
                    nc.vector.scalar_tensor_tensor(out=hs, in0=PB[2 + b][:, 0:n], scalar=rms(1, b), in1=hs,
                                                   op0=ALU.mult, op1=ALU.mult).then_inc(hid_done, 1)
                if c:
                    split(q + 3)
                for b in range(BLK):
                    dve.wait_ge(hidT_hi, BLK * c + b + 1)
                    o = b * 512
                    nc.vector.tensor_tensor(hidT(mlp_l, c, SEQ)[:, o:o + n], PB[b][:, 0:n],
                                            hidT(mlp_h, c, SEQ)[:, o:o + n].bitcast(F32),
                                            ALU.subtract).then_inc(hidT_lo, 1)
            split(S_CIN + 1)
            residual(2, S_CIN)

            stream_lo(2)
            mean_squares(2)
            for h in range(2):
                nc.vector.memset(tT[h][:, :, 0:1], 0.0).then_inc(dve_step, 1)
                nc.vector.memset(tT[h][:, :, TP - 1:TP], 0.0).then_inc(dve_step, 1)
            chain[0] += 4

            def gated_v(h):
                dve.wait_ge(slab_used, S_CIN + 4 * h + 4)
                if h:
                    dve.wait_ge(t_T, 1)
                for b in range(BLK):
                    dve.wait_ge(gc_done, BLK * h + b + 1)
                    nc.vector.scalar_tensor_tensor(out=tt[:, b, :], in0=PB[(2, 6)[h] + b][:, :], scalar=rms(2, b),
                                                   in1=gcv[:, b, :], op0=ALU.mult, op1=ALU.mult).then_inc(t_done, 1)

            def conv3(h, tap):
                if tap == 0:
                    dve.wait_ge(tT_done, h + 1)
                    dve.wait_ge(dve_step, chain[0])
                for c in range(4):
                    k = 4 * h + c
                    w = prm[:, C_OD + tap * KD + k:C_OD + tap * KD + k + 1]
                    src = tT[h][:, c, tap:tap + SEQ]
                    if tap == 0:
                        t = nc.vector.tensor_scalar(yT[:, k, :], src, w, None, ALU.mult)
                    else:
                        dve.wait_ge(dve_step, chain[0] - 3)
                        t = nc.vector.scalar_tensor_tensor(out=yT[:, k, :], in0=src, scalar=w, in1=yT[:, k, :],
                                                           op0=ALU.mult, op1=ALU.add)
                    t.then_inc(dve_step, 1)
                    chain[0] += 1

            def gate_b(h, taken):
                dve.wait_ge(gb_T, h + 1)
                dve.wait_ge(dve_step, taken)
                for k in range(4 * h, 4 * h + 4):
                    o = (k % 2) * SEQ
                    nc.vector.tensor_tensor(yT[:, k, :], yT[:, k, :], PB[2 * h + k % 4 // 2][:, o:o + SEQ],
                                            ALU.mult).then_inc(y_done, 1)

            def y_lo(h):
                for k in range(4 * h, 4 * h + 4):
                    dve.wait_ge(hn_hi, 3 * KD + 8 + k + 1)
                    nc.vector.tensor_tensor(actT_l[:, k * SEQ:(k + 1) * SEQ], yT[:, k, :],
                                            actT_h[:, k * SEQ:(k + 1) * SEQ].bitcast(F32),
                                            ALU.subtract).then_inc(hn_lo, 1)

            split(S_CIN + 5)
            gated_v(0)
            split(S_CIN + 7)
            conv3(0, 0)
            split(S_CIN + 8)
            conv3(0, 1)
            split(S_CIN + 9)
            gated_v(1)
            conv3(0, 2)
            first_half = chain[0]
            split(S_CIN + 11)
            conv3(1, 0)
            split(S_COUT)
            gate_b(0, first_half)
            conv3(1, 1)
            y_lo(0)
            split(S_COUT + 1)
            conv3(1, 2)
            gate_b(1, chain[0])
            y_lo(1)
            split(S_MOE - 1)
            residual(3, S_MOE)

            stream_lo(3)
            mean_squares(3)
            dve.wait_ge(logits_done, 1)
            for b in range(BLK):
                dve.wait_ge(root_done, R_NORM[3] + b + 1)
                lg = rt[:, 0, b, :]
                link(nc.vector.tensor_scalar(lg, PB[b][:, 0:NE], rms(3, b), None, ALU.mult))
                link(nc.vector.scalar_tensor_tensor(out=lg, in0=PB[b][:, NE:2 * NE], scalar=rms(3, b), in1=lg,
                                                    op0=ALU.mult, op1=ALU.add))

            def wide(v):
                return v.unsqueeze(2).to_broadcast([P, BLK, NE])

            def first_max(src, val, eq, key, kmax, hot):
                link(nc.vector.tensor_reduce(val, src, AX.X, ALU.max))
                link(nc.vector.tensor_tensor(eq, src, wide(val), ALU.is_equal))
                link(nc.vector.tensor_tensor(key, eq, iota_e[:, :, :], ALU.mult))
                link(nc.vector.tensor_reduce(kmax, key, AX.X, ALU.max))
                link(nc.vector.tensor_tensor(hot, key, wide(kmax), ALU.is_equal))

            dve.wait_ge(consts_step, CONSTS)
            hot1, hot2 = rt[:, 3, :, :], rt[:, 7, :, :]
            first_max(rt[:, 0, :, :], rs[:, 0, :], rt[:, 1, :, :], rt[:, 2, :, :], rs[:, 4, :], hot1)
            link(nc.vector.scalar_tensor_tensor(out=rt[:, 4, :, :], in0=hot1, scalar=-3.0e38, in1=rt[:, 0, :, :],
                                                op0=ALU.mult, op1=ALU.add))
            first_max(rt[:, 4, :, :], rs[:, 1, :], rt[:, 5, :, :], rt[:, 6, :, :], rs[:, 5, :], hot2)
            nc.vector.tensor_tensor(rs[:, 2, :], rs[:, 1, :], rs[:, 0, :], ALU.subtract).then_inc(rt_step, 1)
            nc.vector.tensor_tensor(sel_bf[:, :, :], hot1, hot2, ALU.add).then_inc(rt_step, 1)
            link(nc.vector.tensor_tensor(rt[:, 8, :, :], hot1, hot2, ALU.add))
            dve.wait_ge(counts_done, 1)
            pos = PB[2][:, 0:2 * NE].rearrange("p (b e) -> p b e", b=BLK)
            link(nc.vector.scalar_tensor_tensor(out=rt[:, 11, :, :], in0=pos, scalar=1.0, in1=rt[:, 8, :, :],
                                                op0=ALU.add, op1=ALU.mult))
            link(nc.vector.tensor_scalar(posj[:, :, 0:NE], rt[:, 11, :, :], -1.0, None, ALU.add))

            def one_hot(job):
                for b in range(BLK):
                    t = nc.vector.tensor_scalar(onehot[:, b, :], iota_s[:, :], posj[:, b, bass.ds(job, 1)], None,
                                                ALU.is_equal)
                t.then_inc(place_done, 1)

            one_hot(0)
            for b in range(BLK):
                dve.wait_ge(tok_hi, b + 1)
                t = nc.vector.scalar_tensor_tensor(out=tokn_l[:, b, :], in0=xres[:, b, :], scalar=rms(3, b),
                                                   in1=tokn_h[:, b, :].bitcast(F32), op0=ALU.mult, op1=ALU.subtract)
            t.then_inc(tok_lo, 1)
            dve.wait_ge(exp_done, 1)
            link(nc.vector.tensor_scalar(rs[:, 6, :], rs[:, 3, :], 1.0, None, ALU.add))
            link(nc.vector.reciprocal(rs[:, 6, :], rs[:, 6, :]))
            link(nc.vector.tensor_tensor(rs[:, 7, :], rs[:, 3, :], rs[:, 6, :], ALU.mult))
            link(nc.vector.tensor_tensor(rt[:, 9, :, :], hot1, wide(rs[:, 6, :]), ALU.mult))
            link(nc.vector.tensor_tensor(rt[:, 10, :, :], hot2, wide(rs[:, 7, :]), ALU.mult))
            link(nc.vector.tensor_tensor(gatej[:, :, 0:NE], rt[:, 9, :, :], rt[:, 10, :, :], ALU.add))
            nc.vector.tensor_copy(ov[:, 4, :], PB[2][:, 2 * NE:3 * NE]).then_inc(chosen, 1)
            link(nc.vector.tensor_copy(gate_hl[:, :, 0:NE, 0], gatej[:, :, 0:NE]))
            nc.vector.tensor_tensor(gate_hl[:, :, 0:NE, 1], gatej[:, :, 0:NE], gate_hl[:, :, 0:NE, 0].bitcast(F32),
                                    ALU.subtract).then_inc(gates_split, 1)

            def pickT_split(first, hi_count):
                for k in range(KD):
                    dve.wait_ge(pickT_hi, hi_count + 4 * (k // 4 + 1))
                    s = slice(k * P, (k + 1) * P)
                    t = nc.vector.scalar_tensor_tensor(out=pickT_l[:, s], in0=PB[k // 4][:, (k % 4) * P:(k % 4 + 1) * P],
                                                       scalar=prm[:, GAIN[3] + k:GAIN[3] + k + 1],
                                                       in1=pickT_h[:, s].bitcast(F32), op0=ALU.mult, op1=ALU.subtract)
                t.then_inc(pickT_lo, 1)

            def gated_lo(hi_count):
                for half in range(2):
                    dve.wait_ge(ysc_hi, hi_count + (half + 1))
                    s = slice(half * 512, (half + 1) * 512)
                    t = nc.vector.scalar_tensor_tensor(out=ysc_l[:, s], in0=PB[6 + half][:, :], scalar=gslot[:, 0:1],
                                                       in1=ysc_h[:, s].bitcast(F32), op0=ALU.mult, op1=ALU.subtract)
                t.then_inc(ysc_lo, 1)

            def scatter_add(job4, piece):
                dve.wait_ge(scat, job4 + (piece + 1))
                dve.wait_ge(x_updated, job4 + (X_C - 3 + piece))
                xs = xres[:, piece % 2, (piece // 2) * 512:(piece // 2 + 1) * 512]
                nc.vector.tensor_tensor(xs, xs, PB[5][:, :], ALU.add).then_inc(x_updated, 1)

            pickT_split(1, 0)

            def run_job(j):
                for m in range(PER):
                    i = S_MOE + m
                    dve.wait_ge(hi_done, j * PER + (i + 1))
                    nc.vector.tensor_sub(lo[:, i % SPLIT, :], raw[:, i % RAW, :],
                                         hi[:, i % SPLIT, :].bitcast(F32)).then_inc(lo_done, 1)
                    if m == 1:
                        gated_lo(j * 2)
                    for c in range(NCH):
                        n = CHUNKS[c]
                        if m == min(E_LAST_H[c] + 2, PER - 1):
                            dve.wait_ge(silu_done, j * NCH + (BLK * NCH + c + 1))
                            hs = hid[:, 0, (c % 2) * 512:(c % 2) * 512 + n]
                            nc.vector.tensor_tensor(hs, hs, PB[2 * (c % 2) + 1][:, 0:n], ALU.mult).then_inc(hid_done, 1)
                        if m == min(T_AT[c] + 2, PER - 1):
                            dve.wait_ge(hidT_hi, j * NCH + (BLK * NCH + c + 1))
                            nc.vector.tensor_tensor(hidT(mlp_l, c, P)[:, 0:n], PB[4][:, 0:n],
                                                    hidT(mlp_h, c, P)[:, 0:n].bitcast(F32),
                                                    ALU.subtract).then_inc(hidT_lo, 1)
                    for piece in range(4):
                        if m == SC_AT[piece] + 2:
                            scatter_add(j * 4, piece)
                    if m == PT_AT + 2:
                        dve.wait_ge(placeT_done, j + 1)
                        nc.vector.tensor_reduce(gslot[:, 0:1], PB[5][:, SEQ:SEQ + 2], AX.X,
                                                ALU.add).then_inc(gslot_done, 1)
                        dve.wait_ge(routed, 1)
                        one_hot(j + 1)
                    if m == GT_AT + 2:
                        pickT_split(0, j * KD + KD)

            with dve.Fori(0, NE) as j:
                run_job(j)
            n_over = dve.value_load(job_i[0:1, 0:1], min_val=0, max_val=MAX_OVER)
            with dve.If(n_over > 0):
                with dve.Fori(0, n_over) as i:
                    run_job(i + NE)
            jobs = n_over + NE
            gated_lo(jobs * 2)
            for piece in range(4):
                scatter_add(jobs * 4, piece)

            dve.wait_ge(bcast_loaded, 48)
            mean_squares(4)
            for b in range(BLK):
                dve.wait_ge(root_done, R_NORM[4] + b + 1)
                nc.vector.scalar_tensor_tensor(out=tokA[:, b, :], in0=xres[:, b, :], scalar=rms(4, b),
                                               in1=tokB[:, D:2 * D], op0=ALU.mult, op1=ALU.mult).then_inc(out_ready, 1)


_INS = ["x", "norm_mix_g", "norm_ffn_g", "ev_w_in", "ev_ws", "ev_bs", "ev_ln_a_g", "ev_ln_a_b", "ev_conv_w",
        "ev_conv_b", "ev_ln_b_g", "ev_ln_b_b", "ev_w_out", "od_w_in", "od_conv_w", "od_w_out", "ffn_w1", "ffn_w3",
        "ffn_w2", "moe_router", "moe_w1", "moe_w3", "moe_w2", "final_g"]


def kernel(**inputs):
    import numpy as np
    import concourse.bacc as bacc
    from concourse.bass_utils import run_bass_kernel_spmd

    nc = bacc.Bacc("TRN2", target_bir_lowering=False, num_devices=1)
    arrays, args = {}, []
    for name in _INS:
        a = np.ascontiguousarray(inputs[name])
        arrays[f"in_{name}"] = a
        args.append(nc.dram_tensor(f"in_{name}", a.shape, mybir.dt.from_np(a.dtype), kind="ExternalInput").ap())
    out = nc.dram_tensor("out_0", (1, SEQ, D), F32, kind="ExternalOutput").ap()
    trunk(nc, *args, out)
    r = run_bass_kernel_spmd(nc, [arrays], core_ids=[0])
    return r.results[0]["out_0"]
```

```python
from contextlib import ExitStack

import concourse.bass as bass
from concourse import mybir

ALU = mybir.AluOpType
ACT = mybir.ActivationFunctionType
AX = mybir.AxisListType
F32 = mybir.dt.float32
F32R = mybir.dt.float32r
BF16 = mybir.dt.bfloat16
I32 = mybir.dt.int32

P = 128
D = 1024
SEQ = 256
BLK = SEQ // P
KD = D // P
AW = 512
HEADS = AW // P
TAPS = 31
PAD = TAPS // 2
FF = 2816
NE = 8
RMS_EPS = 1e-6
LN_EPS = 1e-5

SLAB = 2048
RAW = 11
POOL_COLS = 512
SPLIT = 3
CH = 512
CHUNKS = [CH] * (FF // CH) + [FF % CH]
NCH = len(CHUNKS)
MAX_OVER = (2 * SEQ) // (P + 1)
MAX_JOBS = NE + MAX_OVER


def swiglu_slabs(order):
    out = []
    for step, c in order:
        whole = CHUNKS[c] == CH
        if step == "H":
            out += [(k, c, h) for h in ([0, 1] if whole else [None]) for k in ("w1", "w3")]
        else:
            out += [("w2", c, h) for h in ([0, 1] if whole else [0])]
    return out


def places(slabs):
    last_h = [max(i for i, s in enumerate(slabs) if s[0] != "w2" and s[1] == c) for c in range(NCH)]
    first_y = [min(i for i, s in enumerate(slabs) if s[0] == "w2" and s[1] == c) for c in range(NCH)]
    return last_h, first_y


DENSE = swiglu_slabs([x for c in range(NCH + 1) for x in [("H", c)] * (c < NCH) + [("Y", c - 1)] * (c > 0)])
EXPERT = swiglu_slabs([("H", 0), ("H", 1), ("Y", 0), ("H", 2), ("Y", 1), ("H", 3), ("Y", 2), ("H", 4), ("H", 5),
                       ("Y", 3), ("Y", 4), ("Y", 5)])
PER = len(DENSE)
LAST_H, FIRST_Y = places(DENSE)
E_LAST_H, E_FIRST_Y = places(EXPERT)

S_IN = 0
S_OUT = S_IN + D * 4 * AW // (P * SLAB)
S_FFN = S_OUT + 2 * AW * D // (P * SLAB)
S_CIN = S_FFN + PER
S_COUT = S_CIN + D * 3 * D // (P * SLAB)
S_MOE = S_COUT + D * D // (P * SLAB)
assert PER % RAW == 0 and PER % SPLIT == 0


T_AT = [4, 10, 16, 22, 27, 29]
T_BANK = [4, 6, 5, 7]
SC_AT = [3, 5, 6, 7]
LNA_AT = 22
PT_AT = 8
AHEAD = 3
G_AT = [13, 19]
GT_AT = 28
RT_DIFF, RT_SEL = 1, 2
N_ROW_DMAS = 8
ROOTS = 5 * BLK + 2 * BLK


def trunk(nc, x, norm_mix_g, norm_ffn_g, ev_w_in, ev_ws, ev_bs, ev_ln_a_g, ev_ln_a_b, ev_conv_w,
          ev_conv_b, ev_ln_b_g, ev_ln_b_b, ev_w_out, od_w_in, od_conv_w, od_w_out, ffn_w1, ffn_w3,
          ffn_w2, moe_router, moe_w1, moe_w3, moe_w2, final_g, out):
    ctx = ExitStack()
    with ctx:
        def sb(name, shape, dt=F32):
            return ctx.enter_context(nc.sbuf_tensor(name, shape, dt))

        def sem(name):
            return ctx.enter_context(nc.semaphore(name))

        raw = sb("raw", [P, RAW, SLAB])
        hi = sb("hi", [P, SPLIT, SLAB], F32R)
        lo = sb("lo", [P, SPLIT, SLAB], F32R)
        xres = sb("xres", [P, BLK, D])
        actT_h = sb("actT_h", [P, KD * SEQ], F32R)
        actT_l = sb("actT_l", [P, KD * SEQ], F32R)
        tokA = sb("tokA", [P, BLK, D])
        tokB = sb("tokB", [P, 2 * D])
        MLP = 3072
        with nc.sbuf_tensor("scratch", [P, 2 * MLP], F32) as scratch:
            pass
        mlp_h = sb("mlp_h", [P, MLP], F32R)
        mlp_l = sb("mlp_l", [P, MLP], F32R)
        ident = sb("ident", [P, P])
        iota_s = sb("iota_s", [P, P])
        onehot = sb("onehot", [P, BLK, P], F32R)
        onehotT = sb("onehotT", [P, SEQ], F32R)
        tri = sb("tri", [P, P], BF16)
        ones = sb("ones", [P, P], BF16)
        prm = sb("prm", [P, 196])
        rw = sb("rw", [P, KD, NE])
        rw_hl = sb("rw_hl", [P, KD, 2 * NE], F32R)
        ss = sb("ss", [P, 5, BLK, 2])
        mean2 = sb("mean2", [P, ROOTS])
        root = sb("root", [P, ROOTS])
        power = sb("power", [P, BLK])
        bst = sb("bst", [P, 4, 6])
        mv = sb("mv", [P, 4, 2])
        rt = sb("rt", [P, 12, BLK, NE])
        rs = sb("rs", [P, 10, BLK])
        sel_bf = sb("sel_bf", [P, BLK, NE], BF16)
        iota_e = sb("iota_e", [P, BLK, NE])
        iota_id = sb("iota_id", [P, NE])
        posj = sb("posj", [P, BLK, MAX_JOBS + 1])
        gatej = sb("gatej", [P, BLK, MAX_JOBS + 1])
        gate_hl = sb("gate_hl", [P, BLK, MAX_JOBS + 1, 2], F32R)
        pair_sum = sb("pair_sum", [2 * NE, NE])
        ov = sb("ov", [P, 6, NE])
        ovs = sb("ovs", [P, 8])
        job_i = sb("job_i", [P, 1 + MAX_OVER], I32)
        gslot = sb("gslot", [P, 1])

        PB = [ctx.enter_context(nc.psum_tensor(f"PB{i}", [P, 512], F32)) for i in range(8)]

        raw_loaded = [sem(f"raw_loaded{i}") for i in range(RAW)]
        hi_done = sem("hi_done")
        slab_split = [sem(f"slab_split{i}") for i in range(RAW)]
        slab_used = sem("slab_used")
        x_loaded = sem("x_loaded")
        rows_loaded = sem("rows_loaded")
        ws_loaded = sem("ws_loaded")
        bcast_loaded = sem("bcast_loaded")
        router_loaded = sem("router_loaded")
        consts_step = sem("consts_step")
        setup_T = sem("setup_T")
        prm_done = sem("prm_done")
        x_updated = sem("x_updated")
        sq_done = sem("sq_done")
        x_T = sem("x_T")
        half_out = sem("half_out")
        hn_hi = sem("hn_hi")
        hn_lo = sem("hn_lo")
        dve_step = sem("dve_step")
        mean2_done = sem("mean2_done")
        root_done = sem("root_done")
        sig_done = sem("sig_done")
        glu_done = sem("glu_done")
        glu_T = sem("glu_T")
        gluT_done = sem("gluT_done")
        conv_dve = sem("conv_dve")
        tap_product = sem("tap_product")
        conv_pool = sem("conv_pool")
        v_done = sem("v_done")
        vn_done = sem("vn_done")
        gated = sem("gated")
        u_done = sem("u_done")
        aout_done = sem("aout_done")
        aout_T = sem("aout_T")
        c_T = sem("c_T")
        cn_done = sem("cn_done")
        cn_T = sem("cn_T")
        cs_done = sem("cs_done")
        gc_done = sem("gc_done")
        t_done = sem("t_done")
        t_T = sem("t_T")
        tT_done = sem("tT_done")
        gb_done = sem("gb_done")
        gb_T = sem("gb_T")
        y_done = sem("y_done")
        silu_done = sem("silu_done")
        hid_done = sem("hid_done")
        hid_T = sem("hid_T")
        hidT_hi = sem("hidT_hi")
        hidT_lo = sem("hidT_lo")
        pair_done = sem("pair_done")
        logits_done = sem("logits_done")
        logits_sb = sem("logits_sb")
        exp_done = sem("exp_done")
        rt_step = sem("rt_step")
        pool_step = sem("pool_step")
        chosen = sem("chosen")
        gates_split = sem("gates_split")
        counts_done = sem("counts_done")
        rw_hi = sem("rw_hi")
        rw_lo = sem("rw_lo")
        tok_hi = sem("tok_hi")
        tok_lo = sem("tok_lo")
        routed = sem("routed")
        place_done = sem("place_done")
        picked = sem("picked")
        picked_sb = sem("picked_sb")
        pick_T = sem("pick_T")
        pickT_hi = sem("pickT_hi")
        pickT_lo = sem("pickT_lo")
        place_T = sem("place_T")
        placeT_done = sem("placeT_done")
        gslot_done = sem("gslot_done")
        ysc_hi = sem("ysc_hi")
        ysc_lo = sem("ysc_lo")
        scat = sem("scat")
        gained = sem("gained")
        out_ready = sem("out_ready")
        out_ready1 = sem("out_ready1")
        out_sem = sem("out_sem")

        def slab_source(w1, w3, w2, kind, c, part):
            if kind == "w2":
                r0 = c * CH + part * 2 * P
                return w2[r0:r0 + 2 * P, :].rearrange("(k p) n -> p k n", p=P)
            w = w1 if kind == "w1" else w3
            n0 = c * CH
            if part is None:
                return w[:, n0:n0 + CHUNKS[c]].rearrange("(k p) n -> p k n", p=P)
            return w[part * 4 * P:(part + 1) * 4 * P, n0:n0 + CH].rearrange("(k p) n -> p k n", p=P)

        def in_source(w, col, part):
            return w[part * 4 * P:(part + 1) * 4 * P, col:col + 512].rearrange("(k p) n -> p k n", p=P)

        def out_source(w, i):
            return w[i * 2 * P:(i + 1) * 2 * P, :].rearrange("(k p) n -> p k n", p=P)

        def half_source(w, col):
            return w[:, col:col + 256].rearrange("(k p) n -> p k n", p=P)

        sources = [half_source(ev_w_in[0], col + 256 * h) for h in range(2) for col in (2 * AW, 3 * AW)]
        sources += [in_source(ev_w_in[0], col, h) for col in (AW, 0) for h in range(2)]
        sources += [out_source(ev_w_out[0], i) for i in range(4)]
        sources += [slab_source(ffn_w1[0], ffn_w3[0], ffn_w2[0], *s) for s in DENSE]
        for col in (D, D + 512):
            sources += [in_source(od_w_in[0], col + v, h) for h in range(2) for v in (0, D)]
        sources += [in_source(od_w_in[0], col, h) for col in (0, 512) for h in range(2)]
        sources += [out_source(od_w_out[0], i) for i in range(4)]
        assert len(sources) == S_MOE

        def raw_as(slot, like):
            k = like.shape[1]
            return raw[:, slot, :].rearrange("p (k n) -> p k n", k=k)

        C_CONV, C_BS = 0, TAPS * HEADS
        C_MIX = C_BS + HEADS
        C_FFN = C_MIX + 2 * KD
        C_CB = C_FFN + 2 * KD
        C_LG = C_CB + HEADS
        C_LB = C_LG + HEADS
        C_OD = C_LB + HEADS
        N_ROWS2 = C_OD + 3 * KD - P
        GAIN = [C_MIX, C_FFN, C_MIX + KD, C_FFN + KD]

        lna = tokB[:, 0:2 * AW].rearrange("p (a n) -> p a n", a=2)
        ws_rows = tokB[:, 1024:1536].rearrange("p (h s) -> p h s", h=HEADS)
        prm_rows = tokB[:, 1536:1792].rearrange("p (a n) -> p a n", a=2)
        glu = scratch[:, 0:1024].rearrange("p (b n) -> p b n", b=BLK)
        GP = SEQ + 2 * PAD
        gluT = scratch[:, 1024:1024 + HEADS * GP].rearrange("p (c t) -> p c t", c=HEADS)
        o = 1024 + HEADS * GP
        conv = scratch[:, o:o + 1024].rearrange("p (c t) -> p c t", c=HEADS)
        va = scratch[:, o + 1024:o + 2048].rearrange("p (b n) -> p b n", b=BLK)
        ua = scratch[:, o + 2048:o + 3072].rearrange("p (b n) -> p b n", b=BLK)
        wsT = scratch[:, o + 3072:o + 3584].rearrange("p (h t) -> p h t", h=HEADS)
        dve_sum = tokA[:, 1, 0:SEQ]
        tap_ring = [tokA[:, 0, i * SEQ:(i + 1) * SEQ] for i in range(4)]
        tap_ring += [tokA[:, 1, i * SEQ:(i + 1) * SEQ] for i in range(1, 4)]
        cn = tokA[:, 0, :].rearrange("p (b n) -> p b n", b=BLK)
        cs = glu.rearrange("p b n -> p (b n)").rearrange("p (c t) -> p c t", c=HEADS)
        gcv = scratch[:, 0:1024].rearrange("p (b n) -> p b n", b=BLK)
        tt = scratch[:, 1024:2048].rearrange("p (b n) -> p b n", b=BLK)
        TP = SEQ + 2
        tT = [scratch[:, 2048 + h * 4 * TP:2048 + (h + 1) * 4 * TP].rearrange("p (c t) -> p c t", c=4)
              for h in range(2)]
        gbs = scratch[:, 4112:5136].rearrange("p (b n) -> p b n", b=BLK)
        yT = tokA[:, :, :].rearrange("p b n -> p (b n)").rearrange("p (k t) -> p k t", k=KD)
        hid = tokA

        def hidT(t, c, w):
            o = 8 * w if c == NCH - 1 and w == SEQ else (c % 2) * 4 * w
            return t[:, o:o + 4 * w]

        lgT = tokB[0:2 * NE, 0:SEQ]
        tokn_h = mlp_h[:, 1024:3072].rearrange("p (b n) -> p b n", b=BLK)
        tokn_l = mlp_l[:, 1024:3072].rearrange("p (b n) -> p b n", b=BLK)
        pick = tokB[:, 0:D]
        pickT_h, pickT_l = actT_h[:, 0:D], actT_l[:, 0:D]
        ysc_h, ysc_l = actT_h[:, D:2 * D], actT_l[:, D:2 * D]

        X_C = 12

        R_NORM = [0, 3 * BLK, 4 * BLK, 5 * BLK, 6 * BLK]
        R_LNA, R_LNB = BLK, 2 * BLK

        def rms(n, b):
            return root[:, R_NORM[n] + b:R_NORM[n] + b + 1]

        block = ctx.enter_context(nc.Block())

        @block.sync
        def _(sp):
            for b in range(BLK):
                sp.dma_start(xres[:, b, :], x[0, b * P:(b + 1) * P, :]).then_inc(x_loaded, 16)
            sp.dma_start(raw_as(0, sources[0]), sources[0]).then_inc(raw_loaded[0], 16)
            r = 0
            for src in (norm_mix_g.rearrange("l (k n) -> (l k) n", n=P),
                        norm_ffn_g.rearrange("l (k n) -> (l k) n", n=P),
                        ev_conv_b.rearrange("l (k n) -> (l k) n", n=P),
                        ev_ln_b_g.rearrange("l (k n) -> (l k) n", n=P),
                        ev_ln_b_b.rearrange("l (k n) -> (l k) n", n=P),
                        od_conv_w[0].rearrange("t (k n) -> (t k) n", n=P)):
                sp.dma_start(prm_rows[r:r + src.shape[0], 1, :], src).then_inc(rows_loaded, 16)
                r += src.shape[0]
            sp.dma_start(prm_rows[0:TAPS * HEADS, 0, :],
                         ev_conv_w[0].rearrange("t (c n) -> (t c) n", n=P)).then_inc(rows_loaded, 16)
            sp.dma_start(prm_rows[TAPS * HEADS:P, 0, :], ev_bs[0]).then_inc(rows_loaded, 16)
            for i, src in enumerate(sources):
                if i == 0:
                    continue
                if i == 4:
                    sp.dma_start(ws_rows, ev_ws[0].rearrange("h t s -> t h s")).then_inc(ws_loaded, 16)
                    sp.dma_start(lna[:, 0, :], ev_ln_a_g.partition_broadcast(P)).then_inc(bcast_loaded, 16)
                    sp.dma_start(lna[:, 1, :], ev_ln_a_b.partition_broadcast(P)).then_inc(bcast_loaded, 16)
                    sp.dma_start(rw[:, :, :], moe_router[0].rearrange("(k p) e -> p k e", p=P)).then_inc(router_loaded, 16)
                if i >= RAW:
                    sp.wait_ge(slab_split[i % RAW], 2 * (i // RAW))
                sp.dma_start(raw_as(i % RAW, src), src).then_inc(raw_loaded[i % RAW], 16)

            def expert_slabs(n, base, e):
                w1, w3, w2 = (w[0, bass.ds(e, 1)].rearrange("a r n -> (a r) n")
                              for w in (moe_w1, moe_w3, moe_w2))
                for m, s in enumerate(EXPERT):
                    i = S_MOE + m
                    src = slab_source(w1, w3, w2, *s)
                    sp.wait_ge(slab_split[i % RAW], n * (2 * PER // RAW) + 2 * ((base * PER + i) // RAW))
                    sp.dma_start(raw_as(i % RAW, src), src).then_inc(raw_loaded[i % RAW], 16)

            expert_slabs(0, 0, 0)
            with sp.Fori(0, NE - 1) as n:
                expert_slabs(n, 1, n + 1)
            sp.wait_ge(routed, 1)
            n_over = sp.value_load(job_i[0:1, 0:1], min_val=0, max_val=MAX_OVER)
            with sp.If(n_over > 0):
                with sp.Fori(0, n_over) as n:
                    e = sp.value_load(job_i[0:1, bass.ds(1 + n, 1)], min_val=0, max_val=NE - 1)
                    expert_slabs(n, NE, e)

            for b in range(BLK):
                sp.wait_ge((out_ready, out_ready1)[b], 1)
                sp.dma_start(out[0, b * P:(b + 1) * P, :], tokA[:, b, :]).then_inc(out_sem, 16)
            sp.wait_ge(out_sem, 16 * BLK)

        OWN = 4
        DVE_GROUPS, POOL_GROUPS = (0, 2), (1, 3)
        DVE_STEPS = len(DVE_GROUPS) * (TAPS + 1) + OWN + 1
        PRODUCTS = [(c, tap) for c in POOL_GROUPS for tap in range(TAPS - (OWN if c == 3 else 0))]

        def adds(p):
            return sum(tap > 0 for c, tap in PRODUCTS[:p + 1])

        def tap_of(c, tap):
            return prm[:, C_CONV + tap * HEADS + c:C_CONV + tap * HEADS + c + 1], gluT[:, c, tap:tap + SEQ]

        @block.gpsimd
        def _(pool):
            n = [0]

            def step(ins):
                n[0] += 1
                ins.then_inc(consts_step, 1)

            step(nc.gpsimd.memset(ident[:, :], 0.0))
            pool.wait_ge(consts_step, 1)
            step(nc.gpsimd.affine_select(out=ident[:, :], in_=ident[:, :], compare_op=ALU.not_equal,
                                         fill=1.0, base=0, pattern=[[-1, P]], channel_multiplier=1))
            step(nc.gpsimd.memset(gluT[:, :, :], 0.0))
            step(nc.gpsimd.iota(iota_s[:, :], [[1, P]], base=0, channel_multiplier=0,
                                allow_small_or_imprecise_dtypes=True))
            step(nc.gpsimd.iota(iota_e[:, :, :], [[0, BLK], [-1, NE]], base=NE, channel_multiplier=0,
                                allow_small_or_imprecise_dtypes=True))
            step(nc.gpsimd.iota(iota_id[:, :], [[1, NE]], base=0, channel_multiplier=0,
                                allow_small_or_imprecise_dtypes=True))
            step(nc.gpsimd.memset(ones[:, :], 1.0))
            pool.wait_ge(consts_step, 7)
            step(nc.gpsimd.affine_select(out=tri[:, :], in_=ones[:, :], compare_op=ALU.is_gt,
                                         fill=0.0, base=0, pattern=[[1, P]], channel_multiplier=-1))
            step(nc.gpsimd.memset(posj[:, :, :], -1.0))
            step(nc.gpsimd.memset(gatej[:, :, :], 0.0))
            step(nc.gpsimd.memset(gslot[:, :], 0.0))
            step(nc.gpsimd.memset(onehotT[:, :].bitcast(F32), 0.0))

            step(nc.gpsimd.memset(power[:, :], -0.5))
            pool.wait_ge(consts_step, 13)

            def powers(a, z):
                for r in range(a, z, BLK):
                    pool.wait_ge(mean2_done, r + BLK)
                    nc.gpsimd.tensor_tensor(root[:, r:r + BLK], mean2[:, r:r + BLK], power[:, :],
                                            ALU.pow).then_inc(root_done, BLK)

            powers(0, BLK)
            for p, (c, tap) in enumerate(PRODUCTS):
                if tap:
                    pool.wait_ge(tap_product, p + 1)
                    if tap > 1:
                        pool.wait_ge(conv_pool, adds(p - 1))
                    acc = conv[:, c, :]
                    nc.gpsimd.tensor_tensor(acc, acc, tap_ring[p % len(tap_ring)], ALU.add).then_inc(conv_pool, 1)
                if p == LNA_AT:
                    powers(BLK, 2 * BLK)
            powers(2 * BLK, ROOTS - BLK)

            m = [0]

            def link(ins):
                m[0] += 1
                ins.then_inc(pool_step, 1)
                pool.wait_ge(pool_step, m[0])

            def fold(dst, src):
                w = NE // 2
                while w >= 1:
                    link(nc.gpsimd.tensor_tensor(dst if w == 1 else src[:, 0:w], src[:, 0:w], src[:, w:2 * w], ALU.add))
                    w //= 2

            pool.wait_ge(logits_done, 1)
            link(nc.gpsimd.memset(ysc_h[:, :].bitcast(F32), 0.0))
            nc.gpsimd.memset(ysc_l[:, :].bitcast(F32), 0.0).then_inc(ysc_lo, 1)

            pool.wait_ge(chosen, 1)
            pool.wait_ge(gates_split, 1)
            over = ov[:, 0, :]
            link(nc.gpsimd.tensor_scalar(over, ov[:, 4, :], float(P), None, ALU.is_gt))
            link(nc.gpsimd.tensor_copy(ov[:, 1, :], over))
            fold(ovs[:, 0:1], ov[:, 1, :])
            link(nc.gpsimd.tensor_copy(job_i[:, 0:1], ovs[:, 0:1]))
            before = ov[:, 5, :]
            link(nc.gpsimd.memset(before[:, 0:1], 0.0))
            for e in range(1, NE):
                link(nc.gpsimd.tensor_tensor(before[:, e:e + 1], before[:, e - 1:e], over[:, e - 1:e], ALU.add))
            for i in range(MAX_OVER):
                hot, ids = ov[:, 2, :], ov[:, 3, :]
                link(nc.gpsimd.tensor_scalar(hot, before, float(i), None, ALU.is_equal))
                link(nc.gpsimd.tensor_tensor(hot, hot, over, ALU.mult))
                link(nc.gpsimd.tensor_tensor(ids, hot, iota_id[:, :], ALU.mult))
                fold(ovs[:, 2:3], ids)
                link(nc.gpsimd.tensor_copy(job_i[:, 1 + i:2 + i], ovs[:, 2:3]))
                for b in range(BLK):
                    q = ov[:, 1, :]
                    link(nc.gpsimd.tensor_scalar(q, posj[:, b, 0:NE], float(1 - P), None, ALU.add))
                    link(nc.gpsimd.tensor_tensor(q, q, hot, ALU.mult))
                    fold(ovs[:, 3:4], q)
                    link(nc.gpsimd.tensor_scalar(posj[:, b, NE + i:NE + i + 1], ovs[:, 3:4], -1.0, None, ALU.add))
                    link(nc.gpsimd.tensor_tensor(q, gatej[:, b, 0:NE], hot, ALU.mult))
                    fold(gatej[:, b, NE + i:NE + i + 1], q)
            link(nc.gpsimd.tensor_copy(gate_hl[:, :, NE:, 0], gatej[:, :, NE:]))
            nc.gpsimd.tensor_tensor(gate_hl[:, :, NE:, 1], gatej[:, :, NE:], gate_hl[:, :, NE:, 0].bitcast(F32),
                                    ALU.subtract).then_inc(routed, 1)

            def first_columns(j):
                for m in range(PER):
                    i = S_MOE + m
                    pool.wait_ge(hi_done, j * PER + (i + 1))
                    nc.gpsimd.tensor_sub(lo[:, i % SPLIT, 0:POOL_COLS], raw[:, i % RAW, 0:POOL_COLS],
                                         hi[:, i % SPLIT, 0:POOL_COLS].bitcast(F32)).then_inc(slab_split[i % RAW], 1)

            with pool.Fori(1, NE) as j:
                first_columns(j)
            pool.wait_ge(routed, 1)
            n_over = pool.value_load(job_i[0:1, 0:1], min_val=0, max_val=MAX_OVER)
            with pool.If(n_over > 0):
                with pool.Fori(0, n_over) as i:
                    first_columns(i + NE)
            powers(ROOTS - BLK, ROOTS)

        CONSTS = 12
        LAST_PIECES = [0, 2, 1, 3]
        LAST_BANKS = [PB[5], PB[4], PB[0], PB[1]]

        @block.tensor
        def _(pe):
            def product(i, outs, stat, n, k_of, cols, first, last, job=None, ready=None, halves=False):
                h = hi[:, i % SPLIT, :].rearrange("p (k n) -> p k n", n=n)
                l = lo[:, i % SPLIT, :].rearrange("p (k n) -> p k n", n=n)
                times = 2 * (i // RAW + 1)
                pe.wait_ge(slab_split[i % RAW], times if job is None else job * (2 * PER // RAW) + times)
                steps = [(kk, k, b, q) for kk, k in enumerate(k_of) for b in range(len(outs))
                         for q in range(len(outs[b]))]
                if halves:
                    steps.sort(key=lambda s: s[3])
                mm = None
                for n_step, (kk, k, b, q) in enumerate(steps):
                    ps, s = outs[b][q], slice(q * cols, (q + 1) * cols)
                    if ready is not None and b == 0 and q == 0 and k % 2 == 0:
                        pe.wait_ge(hn_lo, ready + k + 2)
                    st, en = first and kk == 0, last and kk == len(k_of) - 1
                    nc.tensor.matmul(ps, stat(0, k, b), h[:, kk, s], start=st, stop=False)
                    nc.tensor.matmul(ps, stat(0, k, b), l[:, kk, s], start=False, stop=False)
                    mm = nc.tensor.matmul(ps, stat(1, k, b), h[:, kk, s], start=False, stop=en)
                    if halves and n_step == len(steps) // 2 - 1:
                        mm.then_inc(half_out, 1)
                mm.then_inc(slab_used, 1)

            def act_tile(part, k, b):
                t = (actT_h, actT_l)[part]
                return t[:, k * SEQ + b * P:k * SEQ + (b + 1) * P]

            def pick_tile(part, k, b):
                return (pickT_h, pickT_l)[part][:, k * P:(k + 1) * P]

            def stream_T(n, half):
                if n:
                    pe.wait_ge(x_updated, 4 * (n - 1) + 2 * half + 2)
                elif half == 0:
                    pe.wait_ge(x_loaded, 16 * BLK)
                for k in range(4 * half, 4 * half + 4):
                    for b in range(BLK):
                        o = (k % 2) * SEQ + b * P
                        t = nc.tensor.transpose(PB[T_BANK[k // 2]][:, o:o + P], xres[:, b, k * P:(k + 1) * P], ident[:, :])
                t.then_inc(x_T, 1)

            def in_half(i, h, banks, ready=None):
                product(i, [[PB[b][:, :]] for b in banks], act_tile, 512, range(4 * h, 4 * h + 4), 512, h == 0, h == 1,
                        ready=ready)

            def in_group(i, banks):
                for h in range(2):
                    in_half(i + h, h, banks)

            def keep_warm(n, bank):
                for _ in range(n):
                    nc.tensor.matmul(bank[:, 0:P], ident[:, :], ident[:, :], start=True, stop=True)

            pe.wait_ge(consts_step, 2)
            keep_warm(10, PB[1])
            for half in range(2):
                stream_T(0, half)
            pe.wait_ge(rows_loaded, 16 * N_ROW_DMAS)
            nc.tensor.transpose(PB[0][:, 0:P], prm_rows[:, 0, :], ident[:, :])
            nc.tensor.transpose(PB[0][:, P:P + N_ROWS2], prm_rows[0:N_ROWS2, 1, :],
                                ident[0:N_ROWS2, 0:N_ROWS2]).then_inc(setup_T, 1)

            def b_half(i, banks, ready=None):
                product(i, [[PB[b][:, 0:256]] for b in banks], act_tile, 256, range(KD), 256, True, True, ready=ready)

            def glu_half_T(h, bank):
                pe.wait_ge(glu_done, h + 1)
                for c in range(2):
                    for b in range(BLK):
                        o = c * SEQ + b * P
                        t = nc.tensor.transpose(PB[bank][:, o:o + P], glu[:, b, (2 * h + c) * P:(2 * h + c + 1) * P],
                                                ident[:, :])
                t.then_inc(glu_T, 1)

            keep_warm(19, PB[1])
            pe.wait_ge(prm_done, 1)
            b_half(S_IN, (0, 1), ready=0)
            b_half(S_IN + 1, (2, 3))
            b_half(S_IN + 2, (4, 5))
            glu_half_T(0, 0)
            b_half(S_IN + 3, (6, 7))
            in_half(S_IN + 4, 0, (2, 3))
            glu_half_T(1, 4)
            pe.wait_ge(gluT_done, 1)
            pe.wait_ge(ws_loaded, 16)
            for h in range(HEADS):
                t = nc.tensor.transpose(PB[0][:, h * P:(h + 1) * P], ws_rows[:, h, :], ident[:, :])
            t.then_inc(setup_T, 1)
            in_half(S_IN + 5, 1, (2, 3))
            in_group(S_IN + 6, (6, 7))
            pe.wait_ge(prm_done, 2)
            pe.wait_ge(gluT_done, 2)
            for b in range(BLK):
                pe.wait_ge(vn_done, b + 1)
                for h in range(HEADS):
                    t = nc.tensor.matmul(PB[(1, 5)[b]][:, h * P:(h + 1) * P], wsT[:, h, :], va[:, b, h * P:(h + 1) * P],
                                         start=True, stop=True)
                t.then_inc(gated, 1)
            keep_warm(10, PB[3])
            pe.wait_ge(aout_done, BLK)
            for c in range(HEADS):
                for b in range(BLK):
                    o = (c % 2) * SEQ + b * P
                    t = nc.tensor.transpose(PB[(0, 2)[c // 2]][:, o:o + P], ua[:, b, c * P:(c + 1) * P], ident[:, :])
                if c % 2:
                    t.then_inc(aout_T, 1)

            out_banks = [[PB[4 + 2 * b][:, :], PB[5 + 2 * b][:, :]] for b in range(BLK)]
            for i in range(2):
                pe.wait_ge(hn_lo, KD + 2 * i + 2)
                product(S_OUT + i, out_banks, act_tile, D, range(2 * i, 2 * i + 2), 512, i == 0, False)
            for tap in range(2, TAPS, 3):
                pe.wait_ge(conv_dve, TAPS + 1 + tap)
                keep_warm(3, PB[3])
            pe.wait_ge(conv_dve, DVE_STEPS)
            pe.wait_ge(conv_pool, adds(len(PRODUCTS) - 1))
            for b in range(BLK):
                for c in range(HEADS):
                    t = nc.tensor.transpose(PB[b][:, c * P:(c + 1) * P], conv[:, c, b * P:(b + 1) * P], ident[:, :])
                t.then_inc(c_T, 1)
            keep_warm(12, PB[3])
            pe.wait_ge(cn_done, BLK)
            for b in range(BLK):
                for c in range(HEADS):
                    o = (c % 2) * SEQ + b * P
                    t = nc.tensor.transpose(PB[2 + c // 2][:, o:o + P], cn[:, b, c * P:(c + 1) * P], ident[:, :])
            t.then_inc(cn_T, 1)
            keep_warm(6, PB[0])
            for i in range(2, 4):
                pe.wait_ge(hn_lo, KD + 2 * i + 2)
                product(S_OUT + i, out_banks, act_tile, D, range(2 * i, 2 * i + 2), 512, False, i == 3, halves=i == 3)

            def hid_transposes(c, b, bank, w, count):
                pe.wait_ge(hid_done, count)
                for kk in range(CHUNKS[c] // P):
                    t = nc.tensor.transpose(bank[:, kk * P:(kk + 1) * P], hid[:, b, (c % 2) * 512 + kk * P:
                                                                            (c % 2) * 512 + (kk + 1) * P], ident[:, :])
                t.then_inc(hid_T, 1)

            stream_T(1, 0)
            stream_T(1, 1)
            for m, (kind, c, part) in enumerate(DENSE):
                i = S_FFN + m
                if kind == "w2":
                    if m == FIRST_Y[c]:
                        pe.wait_ge(hidT_lo, BLK * (c + 1))

                    def stat(p, k, b, c=c):
                        t = hidT((mlp_h, mlp_l)[p], c, SEQ)
                        return t[:, (b * 4 + k) * P:(b * 4 + k + 1) * P]
                    product(i, out_banks, stat, D, range(2 * part, 2 * part + 2), 512,
                            m == FIRST_Y[0], m == PER - 1, halves=m == PER - 1)
                else:
                    if c > 0 and part in (0, None) and kind == "w1":
                        pe.wait_ge(hidT_lo, BLK * c)
                    n = CHUNKS[c]
                    w = 0 if kind == "w1" else 2
                    ks = range(KD) if part is None else range(4 * part, 4 * part + 4)
                    product(i, [[PB[w + b][:, 0:n]] for b in range(BLK)], act_tile, n, ks, n,
                            part in (0, None), part in (1, None), ready=KD + 8 if c == 0 else None)
                if (c == 0 and m == LAST_H[0]) or (kind == "w2" and m == FIRST_Y[c] and c + 1 < NCH):
                    nxt = 0 if m == LAST_H[0] else c + 1
                    for b in range(BLK):
                        hid_transposes(nxt, b, PB[b], SEQ, BLK * nxt + b + 1)

            def tile_T(src, banks, signal):
                for b in range(BLK):
                    for c in range(4):
                        o = (c % 2) * SEQ + b * P
                        t = nc.tensor.transpose(PB[banks[c // 2]][:, o:o + P], src[:, b, c * P:(c + 1) * P], ident[:, :])
                t.then_inc(signal, 1)

            stream_T(2, 0)
            stream_T(2, 1)
            for i in range(4):
                in_half(S_CIN + i, i // 2, ((0, 1), (2, 3))[i % 2], ready=2 * KD + 8)
            for i in range(4, 8):
                in_half(S_CIN + i, i // 2 - 2, ((4, 5), (6, 7))[i % 2])
                if i == 5:
                    pe.wait_ge(t_done, BLK)
                    tile_T(tt, (0, 1), t_T)
            in_group(S_CIN + 8, (2, 3))
            pe.wait_ge(t_done, 2 * BLK)
            tile_T(tt, (4, 5), t_T)
            product(S_CIN + 10, [[PB[6][:, :]], [PB[7][:, :]]], act_tile, 512, range(4), 512, True, False)
            pe.wait_ge(tT_done, 1)
            pe.wait_ge(gb_done, BLK)
            tile_T(gbs, (0, 1), gb_T)
            product(S_CIN + 11, [[PB[6][:, :]], [PB[7][:, :]]], act_tile, 512, range(4, 8), 512, False, True)
            pe.wait_ge(gb_done, 2 * BLK)
            tile_T(gbs, (2, 3), gb_T)
            pe.wait_ge(tT_done, 2)
            for i in range(4):
                if i % 2 == 0:
                    pe.wait_ge(hn_lo, 3 * KD + 8 + 4 * (i // 2 + 1))
                product(S_COUT + i, out_banks, act_tile, D, range(2 * i, 2 * i + 2), 512, i == 0, i == 3, halves=i == 3)

            pe.wait_ge(rw_lo, 1)
            for half in range(2):
                stream_T(3, half)
            for half in range(2):
                pe.wait_ge(hn_lo, 3 * KD + 16 + 4 * half + 4)
                for k in range(4 * half, 4 * half + 4):
                    for part in (actT_h, actT_l):
                        t = nc.tensor.matmul(PB[0][0:2 * NE, 0:SEQ], rw_hl[:, k, :], part[:, k * SEQ:(k + 1) * SEQ],
                                             start=(k == 0 and part is actT_h), stop=(k == KD - 1 and part is actT_l))
            t.then_inc(logits_done, 1)
            pe.wait_ge(pair_done, 1)
            pe.wait_ge(logits_sb, 1)
            for b in range(BLK):
                t = nc.tensor.matmul(PB[1][:, b * NE:(b + 1) * NE], lgT[:, b * P:(b + 1) * P], pair_sum[:, :],
                                     start=True, stop=True)
            t.then_inc(logits_done, 1)
            keep_warm(9, PB[3])
            pe.wait_ge(rt_step, RT_SEL)
            nc.tensor.matmul(PB[2][:, 0:NE], tri[:, :], sel_bf[:, 0, :], start=True, stop=True)
            nc.tensor.matmul(PB[2][:, NE:2 * NE], ones[:, :], sel_bf[:, 0, :], start=True, stop=False)
            nc.tensor.matmul(PB[2][:, NE:2 * NE], tri[:, :], sel_bf[:, 1, :], start=False, stop=True)
            nc.tensor.matmul(PB[2][:, 2 * NE:3 * NE], ones[:, :], sel_bf[:, 0, :], start=True, stop=False)
            nc.tensor.matmul(PB[2][:, 2 * NE:3 * NE], ones[:, :], sel_bf[:, 1, :], start=False,
                             stop=True).then_inc(counts_done, 1)

            MISC = PB[5]

            def gather(half, bank):
                s = slice(half * 512, (half + 1) * 512)
                for c in range(BLK):
                    nc.tensor.matmul(bank[:, :], onehot[:, c, :], tokn_h[:, c, s], start=(c == 0), stop=False)
                    t = nc.tensor.matmul(bank[:, :], onehot[:, c, :], tokn_l[:, c, s], start=False, stop=(c == BLK - 1))
                t.then_inc(picked, 1)

            def gather_T(half):
                for k in range(4 * half, 4 * half + 4):
                    t = nc.tensor.transpose(PB[half][:, (k % 4) * P:(k % 4 + 1) * P], pick[:, k * P:(k + 1) * P],
                                            ident[:, :])
                t.then_inc(pick_T, 1)

            def scatter(piece, bank):
                b, s = piece % 2, slice((piece // 2) * 512, (piece // 2 + 1) * 512)
                st = onehotT[:, b * P:(b + 1) * P]
                nc.tensor.matmul(bank[:, :], st, ysc_h[:, s], start=True, stop=False)
                nc.tensor.matmul(bank[:, :], st, ysc_l[:, s], start=False, stop=True).then_inc(scat, 1)

            pe.wait_ge(place_done, 1)
            for half in range(2):
                pe.wait_ge(tok_lo, half + 1)
                gather(half, (MISC, PB[4])[half])
            for half in range(2):
                pe.wait_ge(picked_sb, half + 1)
                gather_T(half)
            keep_warm(4, PB[3])

            def run_job(j):
                for m, (kind, c, part) in enumerate(EXPERT):
                    i = S_MOE + m
                    if m < 2:
                        pe.wait_ge(pickT_lo, j * 2 + (m + 1))
                    if kind == "w2":
                        if m == E_FIRST_Y[c]:
                            pe.wait_ge(hidT_lo, j * NCH + (BLK * NCH + c + 1))

                        def stat(p, k, b, c=c):
                            return hidT((mlp_h, mlp_l)[p], c, P)[:, k * P:(k + 1) * P]
                        product(i, [[PB[6][:, :], PB[7][:, :]]], stat, D, range(2 * part, 2 * part + 2), 512,
                                m == E_FIRST_Y[0], m == PER - 1, job=j, halves=m == PER - 1)
                    else:
                        n = CHUNKS[c]
                        bank = PB[2 * (c % 2) + (0 if kind == "w1" else 1)]
                        ks = range(KD) if part is None else range(4 * part, 4 * part + 4)
                        product(i, [[bank[:, 0:n]]], pick_tile, n, ks, n, part in (0, None), part in (1, None),
                                job=j)
                    for c in range(NCH):
                        if m == T_AT[c]:
                            pe.wait_ge(hid_done, j * NCH + (BLK * NCH + c + 1))
                            if c:
                                pe.wait_ge(hidT_lo, j * NCH + (BLK * NCH + c))
                            for kk in range(CHUNKS[c] // P):
                                t = nc.tensor.transpose(PB[4][:, kk * P:(kk + 1) * P],
                                                        hid[:, 0, (c % 2) * 512 + kk * P:(c % 2) * 512 + (kk + 1) * P],
                                                        ident[:, :])
                            t.then_inc(hid_T, 1)
                    if m in SC_AT:
                        piece = SC_AT.index(m)
                        if piece == 0:
                            pe.wait_ge(ysc_lo, j + 1)
                        else:
                            pe.wait_ge(x_updated, j * 4 + (X_C + piece))
                        scatter(piece, MISC)
                    if m == PT_AT:
                        pe.wait_ge(x_updated, j * 4 + (X_C + 4))
                        pe.wait_ge(gates_split, 1)
                        for b in range(BLK):
                            nc.tensor.transpose(MISC[:, b * P:(b + 1) * P], onehot[:, b, :].bitcast(F32), ident[:, :])
                        for b in range(BLK):
                            t = nc.tensor.matmul(MISC[:, SEQ:SEQ + 2], onehot[:, b, :],
                                                 gate_hl[:, b, bass.ds(j, 1), :].rearrange("p a t -> p (a t)"),
                                                 start=(b == 0), stop=(b == BLK - 1))
                        t.then_inc(place_T, 1)
                    if m in G_AT:
                        half = G_AT.index(m)
                        if half == 0:
                            pe.wait_ge(placeT_done, j + 1)
                            pe.wait_ge(gslot_done, j + 1)
                            pe.wait_ge(place_done, j + 2)
                        else:
                            pe.wait_ge(picked_sb, j * 2 + 3)
                        gather(half, MISC)
                    if m == GT_AT:
                        pe.wait_ge(picked_sb, j * 2 + 4)
                        gather_T(0)
                        gather_T(1)

            with pe.Fori(0, NE) as j:
                run_job(j)
            pe.wait_ge(routed, 1)
            n_over = pe.value_load(job_i[0:1, 0:1], min_val=0, max_val=MAX_OVER)
            with pe.If(n_over > 0):
                with pe.Fori(0, n_over) as i:
                    run_job(i + NE)
            jobs = n_over + NE
            pe.wait_ge(ysc_lo, jobs + 1)
            pe.wait_ge(pickT_lo, jobs * 2 + 2)
            for n, piece in enumerate(LAST_PIECES):
                scatter(piece, LAST_BANKS[n])

        @block.scalar
        def _(act):
            done = [0]

            def split(upto):
                while done[0] <= upto:
                    i = done[0]
                    act.wait_ge(raw_loaded[i % RAW], 16 * (i // RAW + 1))
                    if i >= SPLIT:
                        act.wait_ge(slab_used, i - SPLIT + 1)
                    nc.scalar.copy(hi[:, i % SPLIT, :], raw[:, i % RAW, :]).then_inc(hi_done, 1)
                    done[0] += 1

            def square(n, b, half, done):
                if done:
                    act.wait_ge(sq_done, done)
                junk = scratch[:, 3072:3584] if n == 0 else tokB[:, 0:512] if n == 4 else tokB[:, D:D + 512]
                nc.scalar.activation(junk, xres[:, b, half * 512:(half + 1) * 512], ACT.Square,
                                     accum_out=ss[:, n, b, half:half + 1]).then_inc(sq_done, 1)

            def squares(n, half):
                for b in range(BLK):
                    if n == 0:
                        act.wait_ge(x_loaded, 16 * BLK)
                    else:
                        act.wait_ge(x_updated, 4 * (n - 1) + 2 * half + b + 1)
                    square(n, b, half, 4 * n + 2 * half + b)

            def stream_hi(n):
                for half in range(2):
                    act.wait_ge(x_T, 2 * n + half + 1)
                    for k in range(4 * half, 4 * half + 4):
                        o = (k % 2) * SEQ
                        nc.scalar.activation(actT_h[:, k * SEQ:(k + 1) * SEQ], PB[T_BANK[k // 2]][:, o:o + SEQ],
                                             ACT.Copy, scale=prm[:, GAIN[n] + k:GAIN[n] + k + 1]).then_inc(hn_hi, 1)

            def norm(n):
                squares(n, 0)
                stream_hi(n)
                squares(n, 1)

            squares(0, 0)
            split(S_IN)
            act.wait_ge(setup_T, 1)
            nc.scalar.copy(prm[:, :], PB[0][:, 0:P + N_ROWS2]).then_inc(prm_done, 1)
            act.wait_ge(prm_done, 1)
            stream_hi(0)
            split(S_IN + 1)
            squares(0, 1)

            def b_gate(h):
                act.wait_ge(slab_used, S_IN + 2 * h + 2)
                for b in range(BLK):
                    act.wait_ge(root_done, R_NORM[0] + b + 1)
                    nc.scalar.activation(glu[:, b, h * 256:(h + 1) * 256], PB[(2, 6)[h] + b][:, 0:256], ACT.Sigmoid,
                                         scale=rms(0, b)).then_inc(sig_done, 1)

            sent = [0]

            def products(upto):
                while sent[0] < upto:
                    p = sent[0]
                    c, tap = PRODUCTS[p]
                    w, src = tap_of(c, tap)
                    if tap == 0:
                        act.wait_ge(gluT_done, c // 2 + 1)
                        nc.scalar.activation(conv[:, c, :], src, ACT.Identity, bias=prm[:, C_CB + c:C_CB + c + 1],
                                             scale=w).then_inc(tap_product, 1)
                    else:
                        if p >= len(tap_ring):
                            act.wait_ge(conv_pool, adds(p - len(tap_ring)))
                        nc.scalar.activation(tap_ring[p % len(tap_ring)], src, ACT.Copy, scale=w).then_inc(tap_product, 1)
                    sent[0] += 1

            def gluT_copy(h):
                act.wait_ge(glu_T, h + 1)
                nc.scalar.copy(gluT[:, 2 * h:2 * h + 2, PAD:PAD + SEQ],
                               PB[(0, 4)[h]][:, :].rearrange("p (c t) -> p c t", c=2)).then_inc(gluT_done, 1)

            split(S_IN + 3)
            b_gate(0)
            split(S_IN + 4)
            act.wait_ge(consts_step, 3)
            gluT_copy(0)
            products(7)
            split(S_IN + 5)
            b_gate(1)
            products(11)
            act.wait_ge(router_loaded, 16)
            nc.scalar.copy(rw_hl[:, :, 0:NE], rw[:, :, :]).then_inc(rw_hi, 1)
            split(S_IN + 6)
            products(14)
            gluT_copy(1)
            act.wait_ge(setup_T, 2)
            nc.scalar.copy(wsT, PB[0][:, :].rearrange("p (h t) -> p h t", h=HEADS)).then_inc(prm_done, 1)
            products(17)
            split(S_IN + 7)
            products(20)
            act.wait_ge(slab_used, S_IN + 6)
            for b in range(BLK):
                nc.scalar.activation(va[:, b, :], PB[2 + b][:, :], ACT.Gelu_apprx_tanh,
                                     scale=rms(0, b)).then_inc(v_done, 1)
            split(S_OUT)
            products(26)
            split(S_OUT + 1)
            products(32)
            act.wait_ge(slab_used, S_IN + 8)
            for b in range(BLK):
                nc.scalar.activation(ua[:, b, :], PB[6 + b][:, :], ACT.Gelu_apprx_tanh,
                                     scale=rms(0, b)).then_inc(u_done, 1)
            products(39)
            for c in range(0, HEADS, 2):
                act.wait_ge(aout_T, c // 2 + 1)
                nc.scalar.copy(actT_h[:, c * SEQ:(c + 2) * SEQ], PB[(0, 2)[c // 2]][:, :]).then_inc(hn_hi, 2)
            split(S_OUT + 2)
            products(len(PRODUCTS))
            split(S_FFN)
            act.wait_ge(cn_T, 1)
            for c in range(HEADS):
                o = (c % 2) * SEQ
                nc.scalar.activation(cs[:, c, :], PB[2 + c // 2][:, o:o + SEQ], ACT.Silu,
                                     bias=prm[:, C_LB + c:C_LB + c + 1],
                                     scale=prm[:, C_LG + c:C_LG + c + 1]).then_inc(cs_done, 1)
                if c % 2:
                    for e in (c - 1, c):
                        act.wait_ge(cs_done, e + 1)
                        nc.scalar.copy(actT_h[:, (4 + e) * SEQ:(5 + e) * SEQ], cs[:, e, :]).then_inc(hn_hi, 1)
            split(S_FFN + 1)

            norm(1)
            for c in range(NCH):
                n, q = CHUNKS[c], S_FFN + LAST_H[c]
                split(min(q + 2, S_CIN - 1))
                act.wait_ge(slab_used, q + 1)
                for b in range(BLK):
                    if c == 0:
                        act.wait_ge(root_done, R_NORM[1] + b + 1)
                    if c > 1:
                        act.wait_ge(hid_T, BLK * (c - 2) + b + 1)
                    nc.scalar.activation(hid[:, b, (c % 2) * 512:(c % 2) * 512 + n], PB[b][:, 0:n],
                                         ACT.Silu, scale=rms(1, b)).then_inc(silu_done, 1)
                if c:
                    split(q + 3)
                for b in range(BLK):
                    act.wait_ge(hid_T, BLK * c + b + 1)
                    o = b * 512
                    nc.scalar.copy(hidT(mlp_h, c, SEQ)[:, o:o + n], PB[b][:, 0:n]).then_inc(hidT_hi, 1)

            split(S_CIN + 1)
            norm(2)

            def c_gate(h):
                act.wait_ge(slab_used, S_CIN + 4 * h + 3)
                if h:
                    act.wait_ge(t_done, BLK)
                for b in range(BLK):
                    act.wait_ge(root_done, R_NORM[2] + b + 1)
                    nc.scalar.activation(gcv[:, b, :], PB[4 * h + b][:, :], ACT.Copy, scale=rms(2, b)).then_inc(gc_done, 1)

            def tT_copy(h):
                act.wait_ge(t_T, h + 1)
                for c in range(0, 4, 2):
                    t = nc.scalar.copy(tT[h][:, c:c + 2, 1:1 + SEQ],
                                       PB[4 * h + c // 2][:, :].rearrange("p (c t) -> p c t", c=2))
                t.then_inc(tT_done, 1)

            def b_copy(h):
                act.wait_ge(slab_used, S_CIN + 10 + 2 * h)
                if h:
                    act.wait_ge(gb_T, 1)
                for b in range(BLK):
                    nc.scalar.activation(gbs[:, b, :], PB[(2, 6)[h] + b][:, :], ACT.Copy,
                                         scale=rms(2, b)).then_inc(gb_done, 1)

            def y_hi(h):
                for k in range(4 * h, 4 * h + 4):
                    act.wait_ge(y_done, k + 1)
                    nc.scalar.copy(actT_h[:, k * SEQ:(k + 1) * SEQ], yT[:, k, :]).then_inc(hn_hi, 1)

            split(S_CIN + 4)
            c_gate(0)
            split(S_CIN + 7)
            tT_copy(0)
            split(S_CIN + 8)
            c_gate(1)
            split(S_CIN + 11)
            b_copy(0)
            tT_copy(1)
            split(S_COUT + 1)
            y_hi(0)
            b_copy(1)
            y_hi(1)
            split(S_MOE - 1)

            norm(3)
            act.wait_ge(sq_done, 8 * BLK)
            act.dma_start(tokB[:, D:2 * D], final_g.partition_broadcast(P)).then_inc(bcast_loaded, 16)
            act.wait_ge(root_done, R_NORM[3] + BLK)
            for half in range(2):
                hs = slice(half * 512, (half + 1) * 512)
                for b in range(BLK):
                    nc.scalar.activation(tokn_h[:, b, hs], xres[:, b, hs], ACT.Copy, scale=rms(3, b)).then_inc(tok_hi, 1)
            split(S_MOE + AHEAD - 2)

            def picked_copy(count, half, bank):
                act.wait_ge(picked, count)
                nc.scalar.copy(pick[:, half * 512:(half + 1) * 512], bank[:, :]).then_inc(picked_sb, 1)

            def pickT_copy(count):
                for k in range(KD):
                    if k % 4 == 0:
                        act.wait_ge(pick_T, count + (k // 4 + 1))
                    nc.scalar.activation(pickT_h[:, k * P:(k + 1) * P], PB[k // 4][:, (k % 4) * P:(k % 4 + 1) * P],
                                         ACT.Copy, scale=prm[:, GAIN[3] + k:GAIN[3] + k + 1]).then_inc(pickT_hi, 1)

            def gated_hi(jobs):
                for half in range(2):
                    if half == 0:
                        act.wait_ge(half_out, jobs + 3)
                    else:
                        act.wait_ge(slab_used, jobs * PER + S_MOE)
                    nc.scalar.activation(ysc_h[:, half * 512:(half + 1) * 512], PB[6 + half][:, :], ACT.Copy,
                                         scale=gslot[:, 0:1]).then_inc(ysc_hi, 1)

            for half in range(2):
                picked_copy(half + 1, half, (PB[5], PB[4])[half])
            pickT_copy(0)
            split(S_MOE + AHEAD - 1)
            act.wait_ge(consts_step, CONSTS)

            def run_job(j, first=False):
                for m in range(PER):
                    i = S_MOE + m
                    if not first or m >= AHEAD:
                        act.wait_ge(raw_loaded[i % RAW], j * (16 * PER // RAW) + 16 * (i // RAW + 1))
                        act.wait_ge(slab_used, j * PER + (i - SPLIT + 1))
                        nc.scalar.copy(hi[:, i % SPLIT, :], raw[:, i % RAW, :]).then_inc(hi_done, 1)
                    if m == 1 and not first:
                        gated_hi(j)
                    if m == AHEAD and first:
                        act.wait_ge(rt_step, RT_DIFF)
                        nc.scalar.activation(rs[:, 3, :], rs[:, 2, :], ACT.Exp).then_inc(exp_done, 1)
                    for c in range(NCH):
                        n = CHUNKS[c]
                        if m == min(E_LAST_H[c] + 2, PER - 1):
                            act.wait_ge(slab_used, j * PER + (S_MOE + E_LAST_H[c] + 1))
                            nc.scalar.activation(hid[:, 0, (c % 2) * 512:(c % 2) * 512 + n],
                                                 PB[2 * (c % 2)][:, 0:n], ACT.Silu).then_inc(silu_done, 1)
                        if m == min(T_AT[c] + 2, PER - 1):
                            act.wait_ge(hid_T, j * NCH + (BLK * NCH + c + 1))
                            nc.scalar.copy(hidT(mlp_h, c, P)[:, 0:n], PB[4][:, 0:n]).then_inc(hidT_hi, 1)
                    if m == PT_AT + 2:
                        act.wait_ge(place_T, j + 1)
                        nc.scalar.copy(onehotT[:, :], PB[5][:, 0:SEQ]).then_inc(placeT_done, 1)
                    for half in range(2):
                        if m == G_AT[half] + 2:
                            picked_copy(j * 2 + (3 + half), half, PB[5])
                    if m == GT_AT + 2:
                        pickT_copy(j * 2 + 2)

            run_job(0, first=True)
            with act.Fori(1, NE) as j:
                run_job(j)
            act.wait_ge(routed, 1)
            n_over = act.value_load(job_i[0:1, 0:1], min_val=0, max_val=MAX_OVER)
            with act.If(n_over > 0):
                with act.Fori(0, n_over) as i:
                    run_job(i + NE)
            gated_hi(n_over + NE)

            for n, piece in enumerate(LAST_PIECES):
                act.wait_ge(x_updated, (n_over + NE) * 4 + (X_C + n + 1))
                square(4, piece % 2, piece // 2, 16 + n)
            act.wait_ge(gained, 1)
            act.wait_ge(root_done, ROOTS)
            nc.scalar.activation(tokA[:, 0, :], tokA[:, 0, :], ACT.Copy, scale=rms(4, 0)).then_inc(out_ready, 1)

        @block.vector
        def _(dve):
            chain, done = [0], [0]

            def link(ins):
                chain[0] += 1
                ins.then_inc(dve_step, 1)
                dve.wait_ge(dve_step, chain[0])

            def split(upto):
                while done[0] <= upto:
                    i = done[0]
                    dve.wait_ge(hi_done, i + 1)
                    nc.vector.tensor_sub(lo[:, i % SPLIT, :], raw[:, i % RAW, :],
                                         hi[:, i % SPLIT, :].bitcast(F32)).then_inc(slab_split[i % RAW], 2)
                    done[0] += 1

            def mean_square(src, r, scale, eps):
                nc.vector.tensor_scalar(mean2[:, r:r + 1], src, scale, eps, ALU.mult, ALU.add).then_inc(mean2_done, 1)

            def mean_squares(n):
                dve.wait_ge(sq_done, 4 * (n + 1))
                link(nc.vector.tensor_tensor(ss[:, n, :, 0], ss[:, n, :, 0], ss[:, n, :, 1], ALU.add))
                r = R_NORM[n]
                nc.vector.tensor_scalar(mean2[:, r:r + BLK], ss[:, n, :, 0], 1.0 / D, RMS_EPS, ALU.mult,
                                        ALU.add).then_inc(mean2_done, BLK)

            def stream_lo(n):
                base = n * KD + (8 if n > 0 else 0) + (8 if n > 2 else 0)
                for k in range(KD):
                    o = (k % 2) * SEQ
                    dve.wait_ge(hn_hi, base + 2 * (k // 2) + 2)
                    nc.vector.scalar_tensor_tensor(out=actT_l[:, k * SEQ:(k + 1) * SEQ],
                                                   in0=PB[T_BANK[k // 2]][:, o:o + SEQ],
                                                   scalar=prm[:, GAIN[n] + k:GAIN[n] + k + 1],
                                                   in1=actT_h[:, k * SEQ:(k + 1) * SEQ].bitcast(F32),
                                                   op0=ALU.mult, op1=ALU.subtract).then_inc(hn_lo, 1)

            def residual(n, done_slabs):
                for h in range(2):
                    if h == 0:
                        dve.wait_ge(half_out, n)
                    else:
                        dve.wait_ge(slab_used, done_slabs)
                    for b in range(BLK):
                        xs = xres[:, b, h * 512:(h + 1) * 512]
                        nc.vector.tensor_tensor(xs, xs, PB[4 + 2 * b + h][:, :], ALU.add).then_inc(x_updated, 1)

            def layer_stats(src, s, r):
                link(nc.vector.bn_stats(bst[:, s, :], src))
                link(nc.vector.bn_aggr(mv[:, s, :], bst[:, s, :]))
                mean_square(mv[:, s, 1:2], r, 1.0, LN_EPS)

            split(S_IN)
            dve.wait_ge(prm_done, 1)
            stream_lo(0)
            split(S_IN + 1)
            mean_squares(0)

            def glu_half(h):
                for b in range(BLK):
                    dve.wait_ge(sig_done, BLK * h + b + 1)
                    g = glu[:, b, h * 256:(h + 1) * 256]
                    t = nc.vector.scalar_tensor_tensor(out=g, in0=PB[(0, 4)[h] + b][:, 0:256], scalar=rms(0, b), in1=g,
                                                       op0=ALU.mult, op1=ALU.mult)
                t.then_inc(glu_done, 1)

            def taps(e, a, z):
                c = DVE_GROUPS[e]
                base = e * (TAPS + 1)
                first_sum = conv[:, c, :]
                for tap in range(a, z):
                    w, src = tap_of(c, tap)
                    if tap == 0:
                        t = nc.vector.tensor_scalar(first_sum, src, w, prm[:, C_CB + c:C_CB + c + 1], ALU.mult, ALU.add)
                    elif tap == 1:
                        if e:
                            dve.wait_ge(conv_dve, base)
                        t = nc.vector.tensor_scalar(dve_sum, src, w, None, ALU.mult)
                    else:
                        dve.wait_ge(conv_dve, base + tap - 1)
                        acc = dve_sum if tap % 2 else first_sum
                        t = nc.vector.scalar_tensor_tensor(out=acc, in0=src, scalar=w, in1=acc, op0=ALU.mult, op1=ALU.add)
                    t.then_inc(conv_dve, 1)
                if z == TAPS:
                    dve.wait_ge(conv_dve, base + TAPS)
                    nc.vector.tensor_tensor(first_sum, first_sum, dve_sum, ALU.add).then_inc(conv_dve, 1)

            split(S_IN + 3)
            glu_half(0)
            split(S_IN + 4)
            dve.wait_ge(gluT_done, 1)
            taps(0, 0, 6)
            split(S_IN + 5)
            glu_half(1)
            dve.wait_ge(rw_hi, 1)
            nc.vector.tensor_sub(rw_hl[:, :, NE:2 * NE], rw[:, :, :], rw_hl[:, :, 0:NE].bitcast(F32)).then_inc(rw_lo, 1)
            taps(0, 6, 11)
            split(S_IN + 6)
            taps(0, 11, 17)
            split(S_IN + 7)
            dve.wait_ge(bcast_loaded, 32)
            for b in range(BLK):
                dve.wait_ge(v_done, b + 1)
                layer_stats(va[:, b, :], b, R_LNA + b)
            split(S_OUT)
            for b in range(BLK):
                dve.wait_ge(root_done, R_LNA + b + 1)
                link(nc.vector.tensor_scalar(va[:, b, :], va[:, b, :], mv[:, b, 0:1], root[:, R_LNA + b:R_LNA + b + 1],
                                             ALU.subtract, ALU.mult))
                link(nc.vector.tensor_tensor(va[:, b, :], va[:, b, :], lna[:, 0, :], ALU.mult))
                nc.vector.tensor_tensor(va[:, b, :], va[:, b, :], lna[:, 1, :], ALU.add).then_inc(vn_done, 1)
            taps(0, 17, 20)
            for b in range(BLK):
                dve.wait_ge(u_done, b + 1)
                dve.wait_ge(gated, b + 1)
                for h in range(HEADS):
                    s = slice(h * P, (h + 1) * P)
                    t = nc.vector.scalar_tensor_tensor(out=ua[:, b, s], in0=PB[(1, 5)[b]][:, s],
                                                       scalar=prm[:, C_BS + h:C_BS + h + 1], in1=ua[:, b, s],
                                                       op0=ALU.add, op1=ALU.mult)
                t.then_inc(aout_done, 1)
            taps(0, 20, 22)
            for c in range(0, HEADS, 2):
                dve.wait_ge(hn_hi, KD + c + 2)
                nc.vector.tensor_tensor(actT_l[:, c * SEQ:(c + 2) * SEQ], PB[(0, 2)[c // 2]][:, :],
                                        actT_h[:, c * SEQ:(c + 2) * SEQ].bitcast(F32), ALU.subtract).then_inc(hn_lo, 2)
            split(S_OUT + 1)
            taps(0, 22, TAPS)
            dve.wait_ge(gluT_done, 2)
            taps(1, 0, TAPS)
            for n in range(OWN):
                w, src = tap_of(3, TAPS - OWN + n)
                dve.wait_ge(conv_dve, 2 * (TAPS + 1) + n)
                if n == 0:
                    t = nc.vector.tensor_scalar(dve_sum, src, w, None, ALU.mult)
                else:
                    t = nc.vector.scalar_tensor_tensor(out=dve_sum, in0=src, scalar=w, in1=dve_sum, op0=ALU.mult,
                                                       op1=ALU.add)
                t.then_inc(conv_dve, 1)
            dve.wait_ge(conv_dve, DVE_STEPS - 1)
            dve.wait_ge(conv_pool, adds(len(PRODUCTS) - 1))
            nc.vector.tensor_tensor(conv[:, 3, :], conv[:, 3, :], dve_sum, ALU.add).then_inc(conv_dve, 1)
            for b in range(BLK):
                dve.wait_ge(c_T, b + 1)
                layer_stats(PB[b][:, :], 2 + b, R_LNB + b)
            for b in range(BLK):
                dve.wait_ge(root_done, R_LNB + b + 1)
                nc.vector.tensor_scalar(cn[:, b, :], PB[b][:, :], mv[:, 2 + b, 0:1], root[:, R_LNB + b:R_LNB + b + 1],
                                        ALU.subtract, ALU.mult).then_inc(cn_done, 1)
            split(S_OUT + 2)
            for c in range(HEADS):
                if c == 2:
                    split(S_OUT + 3)
                dve.wait_ge(hn_hi, KD + 4 + c + 1)
                nc.vector.tensor_tensor(actT_l[:, (4 + c) * SEQ:(5 + c) * SEQ], cs[:, c, :],
                                        actT_h[:, (4 + c) * SEQ:(5 + c) * SEQ].bitcast(F32),
                                        ALU.subtract).then_inc(hn_lo, 1)
            split(S_FFN + 1)
            residual(1, S_FFN)

            stream_lo(1)
            mean_squares(1)
            for c in range(NCH):
                n, q = CHUNKS[c], S_FFN + LAST_H[c]
                split(min(q + 2, S_CIN - 1))
                for b in range(BLK):
                    dve.wait_ge(silu_done, BLK * c + b + 1)
                    hs = hid[:, b, (c % 2) * 512:(c % 2) * 512 + n]
                    nc.vector.scalar_tensor_tensor(out=hs, in0=PB[2 + b][:, 0:n], scalar=rms(1, b), in1=hs,
                                                   op0=ALU.mult, op1=ALU.mult).then_inc(hid_done, 1)
                if c:
                    split(q + 3)
                for b in range(BLK):
                    dve.wait_ge(hidT_hi, BLK * c + b + 1)
                    o = b * 512
                    nc.vector.tensor_tensor(hidT(mlp_l, c, SEQ)[:, o:o + n], PB[b][:, 0:n],
                                            hidT(mlp_h, c, SEQ)[:, o:o + n].bitcast(F32),
                                            ALU.subtract).then_inc(hidT_lo, 1)
            split(S_CIN + 1)
            residual(2, S_CIN)

            stream_lo(2)
            mean_squares(2)
            for h in range(2):
                nc.vector.memset(tT[h][:, :, 0:1], 0.0).then_inc(dve_step, 1)
                nc.vector.memset(tT[h][:, :, TP - 1:TP], 0.0).then_inc(dve_step, 1)
            chain[0] += 4

            def gated_v(h):
                dve.wait_ge(slab_used, S_CIN + 4 * h + 4)
                if h:
                    dve.wait_ge(t_T, 1)
                for b in range(BLK):
                    dve.wait_ge(gc_done, BLK * h + b + 1)
                    nc.vector.scalar_tensor_tensor(out=tt[:, b, :], in0=PB[(2, 6)[h] + b][:, :], scalar=rms(2, b),
                                                   in1=gcv[:, b, :], op0=ALU.mult, op1=ALU.mult).then_inc(t_done, 1)

            def conv3(h, tap):
                if tap == 0:
                    dve.wait_ge(tT_done, h + 1)
                    dve.wait_ge(dve_step, chain[0])
                for c in range(4):
                    k = 4 * h + c
                    w = prm[:, C_OD + tap * KD + k:C_OD + tap * KD + k + 1]
                    src = tT[h][:, c, tap:tap + SEQ]
                    if tap == 0:
                        t = nc.vector.tensor_scalar(yT[:, k, :], src, w, None, ALU.mult)
                    else:
                        dve.wait_ge(dve_step, chain[0] - 3)
                        t = nc.vector.scalar_tensor_tensor(out=yT[:, k, :], in0=src, scalar=w, in1=yT[:, k, :],
                                                           op0=ALU.mult, op1=ALU.add)
                    t.then_inc(dve_step, 1)
                    chain[0] += 1

            def gate_b(h, taken):
                dve.wait_ge(gb_T, h + 1)
                dve.wait_ge(dve_step, taken)
                for k in range(4 * h, 4 * h + 4):
                    o = (k % 2) * SEQ
                    nc.vector.tensor_tensor(yT[:, k, :], yT[:, k, :], PB[2 * h + k % 4 // 2][:, o:o + SEQ],
                                            ALU.mult).then_inc(y_done, 1)

            def y_lo(h):
                for k in range(4 * h, 4 * h + 4):
                    dve.wait_ge(hn_hi, 3 * KD + 8 + k + 1)
                    nc.vector.tensor_tensor(actT_l[:, k * SEQ:(k + 1) * SEQ], yT[:, k, :],
                                            actT_h[:, k * SEQ:(k + 1) * SEQ].bitcast(F32),
                                            ALU.subtract).then_inc(hn_lo, 1)

            split(S_CIN + 5)
            gated_v(0)
            split(S_CIN + 7)
            conv3(0, 0)
            split(S_CIN + 8)
            conv3(0, 1)
            split(S_CIN + 9)
            gated_v(1)
            conv3(0, 2)
            first_half = chain[0]
            split(S_CIN + 11)
            conv3(1, 0)
            split(S_COUT)
            gate_b(0, first_half)
            conv3(1, 1)
            y_lo(0)
            split(S_COUT + 1)
            conv3(1, 2)
            gate_b(1, chain[0])
            y_lo(1)
            split(S_MOE - 1)
            residual(3, S_MOE)

            stream_lo(3)
            mean_squares(3)

            def tokens_lo(half):
                hs = slice(half * 512, (half + 1) * 512)
                for b in range(BLK):
                    dve.wait_ge(tok_hi, BLK * half + b + 1)
                    t = nc.vector.scalar_tensor_tensor(out=tokn_l[:, b, hs], in0=xres[:, b, hs], scalar=rms(3, b),
                                                       in1=tokn_h[:, b, hs].bitcast(F32), op0=ALU.mult, op1=ALU.subtract)
                t.then_inc(tok_lo, 1)

            nc.vector.tensor_tensor(pair_sum[:, :], ident[0:2 * NE, 0:NE], ident[0:2 * NE, NE:2 * NE],
                                    ALU.add).then_inc(pair_done, 1)
            dve.wait_ge(logits_done, 1)
            nc.vector.tensor_copy(lgT, PB[0][0:2 * NE, 0:SEQ]).then_inc(logits_sb, 1)
            dve.wait_ge(root_done, R_NORM[3] + BLK)
            dve.wait_ge(logits_done, 2)
            for b in range(BLK):
                t = nc.vector.tensor_scalar(rt[:, 0, b, :], PB[1][:, b * NE:(b + 1) * NE], rms(3, b), None, ALU.mult)
            link(t)

            def wide(v):
                return v.unsqueeze(2).to_broadcast([P, BLK, NE])

            def first_max(src, val, eq, key, kmax, hot):
                link(nc.vector.tensor_reduce(val, src, AX.X, ALU.max))
                link(nc.vector.tensor_tensor(eq, src, wide(val), ALU.is_equal))
                link(nc.vector.tensor_tensor(key, eq, iota_e[:, :, :], ALU.mult))
                link(nc.vector.tensor_reduce(kmax, key, AX.X, ALU.max))
                link(nc.vector.tensor_tensor(hot, key, wide(kmax), ALU.is_equal))

            dve.wait_ge(consts_step, CONSTS)
            hot1, hot2 = rt[:, 3, :, :], rt[:, 7, :, :]
            first_max(rt[:, 0, :, :], rs[:, 0, :], rt[:, 1, :, :], rt[:, 2, :, :], rs[:, 4, :], hot1)
            link(nc.vector.scalar_tensor_tensor(out=rt[:, 4, :, :], in0=hot1, scalar=-3.0e38, in1=rt[:, 0, :, :],
                                                op0=ALU.mult, op1=ALU.add))
            first_max(rt[:, 4, :, :], rs[:, 1, :], rt[:, 5, :, :], rt[:, 6, :, :], rs[:, 5, :], hot2)
            nc.vector.tensor_tensor(rs[:, 2, :], rs[:, 1, :], rs[:, 0, :], ALU.subtract).then_inc(rt_step, 1)
            nc.vector.tensor_tensor(sel_bf[:, :, :], hot1, hot2, ALU.add).then_inc(rt_step, 1)
            link(nc.vector.tensor_tensor(rt[:, 8, :, :], hot1, hot2, ALU.add))
            tokens_lo(0)
            dve.wait_ge(counts_done, 1)
            pos = PB[2][:, 0:2 * NE].rearrange("p (b e) -> p b e", b=BLK)
            link(nc.vector.scalar_tensor_tensor(out=rt[:, 11, :, :], in0=pos, scalar=1.0, in1=rt[:, 8, :, :],
                                                op0=ALU.add, op1=ALU.mult))
            link(nc.vector.tensor_scalar(posj[:, :, 0:NE], rt[:, 11, :, :], -1.0, None, ALU.add))

            def one_hot(job):
                for b in range(BLK):
                    t = nc.vector.tensor_scalar(onehot[:, b, :], iota_s[:, :], posj[:, b, bass.ds(job, 1)], None,
                                                ALU.is_equal)
                t.then_inc(place_done, 1)

            one_hot(0)
            nc.vector.tensor_copy(ov[:, 4, :], PB[2][:, 2 * NE:3 * NE]).then_inc(chosen, 1)
            tokens_lo(1)
            split(S_MOE)

            def pickT_split(hi_count):
                for k in range(KD):
                    dve.wait_ge(pickT_hi, hi_count + 4 * (k // 4 + 1))
                    s = slice(k * P, (k + 1) * P)
                    t = nc.vector.scalar_tensor_tensor(out=pickT_l[:, s], in0=PB[k // 4][:, (k % 4) * P:(k % 4 + 1) * P],
                                                       scalar=prm[:, GAIN[3] + k:GAIN[3] + k + 1],
                                                       in1=pickT_h[:, s].bitcast(F32), op0=ALU.mult, op1=ALU.subtract)
                    if k % 4 == 3:
                        t.then_inc(pickT_lo, 1)

            def gated_lo(hi_count):
                for half in range(2):
                    dve.wait_ge(ysc_hi, hi_count + (half + 1))
                    s = slice(half * 512, (half + 1) * 512)
                    t = nc.vector.scalar_tensor_tensor(out=ysc_l[:, s], in0=PB[6 + half][:, :], scalar=gslot[:, 0:1],
                                                       in1=ysc_h[:, s].bitcast(F32), op0=ALU.mult, op1=ALU.subtract)
                t.then_inc(ysc_lo, 1)

            def scatter_add(job4, piece):
                dve.wait_ge(scat, job4 + (piece + 1))
                dve.wait_ge(x_updated, job4 + (X_C - 3 + piece))
                xs = xres[:, piece % 2, (piece // 2) * 512:(piece // 2 + 1) * 512]
                nc.vector.tensor_tensor(xs, xs, PB[5][:, :], ALU.add).then_inc(x_updated, 1)

            pickT_split(0)
            split(S_MOE + AHEAD - 1)

            def gates():
                dve.wait_ge(exp_done, 1)
                link(nc.vector.tensor_scalar(rs[:, 6, :], rs[:, 3, :], 1.0, None, ALU.add))
                link(nc.vector.reciprocal(rs[:, 6, :], rs[:, 6, :]))
                link(nc.vector.tensor_tensor(rs[:, 7, :], rs[:, 3, :], rs[:, 6, :], ALU.mult))
                link(nc.vector.tensor_tensor(rt[:, 9, :, :], hot1, wide(rs[:, 6, :]), ALU.mult))
                link(nc.vector.tensor_tensor(rt[:, 10, :, :], hot2, wide(rs[:, 7, :]), ALU.mult))
                link(nc.vector.tensor_tensor(gatej[:, :, 0:NE], rt[:, 9, :, :], rt[:, 10, :, :], ALU.add))
                link(nc.vector.tensor_copy(gate_hl[:, :, 0:NE, 0], gatej[:, :, 0:NE]))
                nc.vector.tensor_tensor(gate_hl[:, :, 0:NE, 1], gatej[:, :, 0:NE], gate_hl[:, :, 0:NE, 0].bitcast(F32),
                                        ALU.subtract).then_inc(gates_split, 1)


            def run_job(j, first=False):
                for m in range(PER):
                    i = S_MOE + m
                    if first:
                        split(i)
                    else:
                        dve.wait_ge(hi_done, j * PER + (i + 1))
                        nc.vector.tensor_sub(lo[:, i % SPLIT, POOL_COLS:], raw[:, i % RAW, POOL_COLS:],
                                             hi[:, i % SPLIT, POOL_COLS:].bitcast(F32)).then_inc(slab_split[i % RAW], 1)
                    if m == 1 and not first:
                        gated_lo(j * 2 - 2)
                    if m == AHEAD + 1 and first:
                        gates()
                    for c in range(NCH):
                        n = CHUNKS[c]
                        if m == min(E_LAST_H[c] + 2, PER - 1):
                            dve.wait_ge(silu_done, j * NCH + (BLK * NCH + c + 1))
                            hs = hid[:, 0, (c % 2) * 512:(c % 2) * 512 + n]
                            nc.vector.tensor_tensor(hs, hs, PB[2 * (c % 2) + 1][:, 0:n], ALU.mult).then_inc(hid_done, 1)
                        if m == min(T_AT[c] + 2, PER - 1):
                            dve.wait_ge(hidT_hi, j * NCH + (BLK * NCH + c + 1))
                            nc.vector.tensor_tensor(hidT(mlp_l, c, P)[:, 0:n], PB[4][:, 0:n],
                                                    hidT(mlp_h, c, P)[:, 0:n].bitcast(F32),
                                                    ALU.subtract).then_inc(hidT_lo, 1)
                    for piece in range(4):
                        if m == SC_AT[piece] + 2:
                            scatter_add(j * 4, piece)
                    if m == PT_AT + 2:
                        dve.wait_ge(placeT_done, j + 1)
                        nc.vector.tensor_reduce(gslot[:, 0:1], PB[5][:, SEQ:SEQ + 2], AX.X,
                                                ALU.add).then_inc(gslot_done, 1)
                        if not first:
                            dve.wait_ge(routed, 1)
                        one_hot(j + 1)
                    if m == GT_AT + 2:
                        pickT_split(j * KD + KD)

            run_job(0, first=True)
            with dve.Fori(1, NE) as j:
                run_job(j)
            n_over = dve.value_load(job_i[0:1, 0:1], min_val=0, max_val=MAX_OVER)
            with dve.If(n_over > 0):
                with dve.Fori(0, n_over) as i:
                    run_job(i + NE)
            jobs = n_over + NE
            gated_lo(jobs * 2 - 2)
            for n, piece in enumerate(LAST_PIECES):
                dve.wait_ge(scat, jobs * 4 + (n + 1))
                dve.wait_ge(x_updated, jobs * 4 + X_C)
                xs = xres[:, piece % 2, (piece // 2) * 512:(piece // 2 + 1) * 512]
                nc.vector.tensor_tensor(xs, xs, LAST_BANKS[n][:, :], ALU.add).then_inc(x_updated, 1)

            dve.wait_ge(bcast_loaded, 48)
            dve.wait_ge(x_updated, jobs * 4 + (X_C + 4))
            for b in range(BLK):
                nc.vector.tensor_tensor(tokA[:, b, :], xres[:, b, :], tokB[:, D:2 * D], ALU.mult).then_inc(gained, 1)
                if b == 0:
                    mean_squares(4)
            dve.wait_ge(gained, BLK)
            dve.wait_ge(root_done, ROOTS)
            nc.vector.tensor_scalar(tokA[:, 1, :], tokA[:, 1, :], rms(4, 1), None, ALU.mult).then_inc(out_ready1, 1)


_INS = ["x", "norm_mix_g", "norm_ffn_g", "ev_w_in", "ev_ws", "ev_bs", "ev_ln_a_g", "ev_ln_a_b", "ev_conv_w",
        "ev_conv_b", "ev_ln_b_g", "ev_ln_b_b", "ev_w_out", "od_w_in", "od_conv_w", "od_w_out", "ffn_w1", "ffn_w3",
        "ffn_w2", "moe_router", "moe_w1", "moe_w3", "moe_w2", "final_g"]


def kernel(**inputs):
    import numpy as np
    import concourse.bacc as bacc
    from concourse.bass_utils import run_bass_kernel_spmd

    nc = bacc.Bacc("TRN2", target_bir_lowering=False, num_devices=1)
    arrays, args = {}, []
    for name in _INS:
        a = np.ascontiguousarray(inputs[name])
        arrays[f"in_{name}"] = a
        args.append(nc.dram_tensor(f"in_{name}", a.shape, mybir.dt.from_np(a.dtype), kind="ExternalInput").ap())
    out = nc.dram_tensor("out_0", (1, SEQ, D), F32, kind="ExternalOutput").ap()
    trunk(nc, *args, out)
    r = run_bass_kernel_spmd(nc, [arrays], core_ids=[0])
    return r.results[0]["out_0"]
```
